# Optimizing a Trainium2 kernel written in Bass

```python
import jax, jax.numpy as jnp
from jax import lax
import numpy as np

D_MODEL = 1024
BATCH = 1
SEQ = 1024
DEPTH = 2
DEC_BATCH = 8
DEC_SEQ = 16
PAST_LEN = 512

CHUNK = 64
N_MIXERS = 2
N_A = (DEPTH + 1) // 2
N_B = DEPTH // 2
A_HEADS = 16
A_KV_HEADS = 4
A_HEAD_DIM = D_MODEL // A_HEADS
A_GROUP = A_HEADS // A_KV_HEADS
IDX_HEADS = 8
IDX_DIM = 64
TOPK_MAX = 256
Q_BLOCK = 128
A_SPLITS = [A_HEADS * A_HEAD_DIM, A_KV_HEADS * A_HEAD_DIM, A_KV_HEADS * A_HEAD_DIM,
            IDX_HEADS * IDX_DIM, IDX_DIM, IDX_HEADS]
A_IN = sum(A_SPLITS)
GLA_HEADS = 4
GLA_DK = D_MODEL // 2 // GLA_HEADS
GLA_DV = D_MODEL // GLA_HEADS
GLA_RANK = 16
GLA_TAU = 16.0
GLA_CHUNK = 64
B_SPLITS = [GLA_HEADS * GLA_DK, GLA_HEADS * GLA_DK, GLA_HEADS * GLA_DV, D_MODEL, GLA_RANK]
B_IN = sum(B_SPLITS)
D_FF = 4 * D_MODEL
EPS = 1e-6

kernel_name = 'dsa_gla_streaming_encoder_step'

def rmsnorm(x, g):
    xf = x.astype(jnp.float32)
    y = xf * lax.rsqrt(jnp.mean(xf * xf, axis=-1, keepdims=True) + EPS)
    return (y * g.astype(jnp.float32)).astype(x.dtype)

def split_cols(h, sizes):
    offs = np.cumsum(sizes)[:-1].tolist()
    return jnp.split(h, offs, axis=-1)

def sq_relu_mlp(x, w_up, w_down):
    return jnp.square(jax.nn.relu(x @ w_up)) @ w_down

def dsa_project(x, w_in):
    B, T, _ = x.shape
    q, k, v, qi, ki, wt = split_cols(x @ w_in, A_SPLITS)
    return (q.reshape(B, T, A_KV_HEADS, A_GROUP, A_HEAD_DIM),
            k.reshape(B, T, A_KV_HEADS, A_HEAD_DIM),
            v.reshape(B, T, A_KV_HEADS, A_HEAD_DIM),
            qi.reshape(B, T, IDX_HEADS, IDX_DIM), ki, wt)

def dsa_attend(q, qi, wt, q_pos, k, v, ki, topk):
    L = k.shape[1]
    s = jnp.einsum('bqhd,bld->bqhl', qi, ki).astype(jnp.float32) * (IDX_DIM ** -0.5)
    w = wt.astype(jnp.float32) * (IDX_HEADS ** -0.5)
    score = jnp.einsum('bqhl,bqh->bql', jax.nn.relu(s), w)
    limit = (q_pos // CHUNK + 1) * CHUNK
    adm = jnp.arange(L)[None, :] < limit[:, None]
    score = jnp.where(adm[None], score, -jnp.inf)
    _, idx = lax.top_k(score, topk)
    valid = idx < limit[None, :, None]
    k_sel = jax.vmap(lambda kk, ii: kk[ii])(k, idx)
    v_sel = jax.vmap(lambda vv, ii: vv[ii])(v, idx)
    logits = jnp.einsum('bqhgd,bqjhd->bqhgj', q, k_sel).astype(jnp.float32) * (A_HEAD_DIM ** -0.5)
    logits = jnp.where(valid[:, :, None, None, :], logits, -jnp.inf)
    p = jax.nn.softmax(logits, axis=-1).astype(v.dtype)
    o = jnp.einsum('bqhgj,bqjhd->bqhgd', p, v_sel)
    return o.reshape(o.shape[0], o.shape[1], A_HEADS * A_HEAD_DIM)

def dsa_prompt(x, w_in, w_o):
    B, S, _ = x.shape
    q, k, v, qi, ki, wt = dsa_project(x, w_in)
    topk = min(TOPK_MAX, S // 4)
    nb = S // Q_BLOCK

    def blocks(a):
        return jnp.moveaxis(a.reshape((B, nb, Q_BLOCK) + a.shape[2:]), 1, 0)

    pos = jnp.arange(S, dtype=jnp.int32).reshape(nb, Q_BLOCK)
    o = lax.map(lambda a: dsa_attend(a[0], a[1], a[2], a[3], k, v, ki, topk),
                (blocks(q), blocks(qi), blocks(wt), pos))
    o = jnp.moveaxis(o, 0, 1).reshape(B, S, A_HEADS * A_HEAD_DIM)
    return o @ w_o, k, v, ki

def dsa_sample(x, c_k, c_v, c_ki, w_in, w_o):
    B, T, _ = x.shape
    q, k, v, qi, ki, wt = dsa_project(x, w_in)
    past = c_k.shape[1]
    k_all = jnp.concatenate([c_k.astype(k.dtype), k], axis=1)
    v_all = jnp.concatenate([c_v.astype(v.dtype), v], axis=1)
    ki_all = jnp.concatenate([c_ki.astype(ki.dtype), ki], axis=1)
    topk = min(TOPK_MAX, (past + T) // 4)
    pos = past + jnp.arange(T, dtype=jnp.int32)
    o = dsa_attend(q, qi, wt, pos, k_all, v_all, ki_all, topk)
    return o @ w_o, k, v, ki

def gla_project(x, w_in, w_a2, b_a):
    B, T, _ = x.shape
    q, k, v, g, a = split_cols(x @ w_in, B_SPLITS)
    la = jax.nn.log_sigmoid((a @ w_a2 + b_a).astype(jnp.float32)) / GLA_TAU
    shp = (B, T, GLA_HEADS, GLA_DK)
    return (q.reshape(shp).astype(jnp.float32) * (GLA_DK ** -0.5),
            k.reshape(shp).astype(jnp.float32),
            v.reshape(B, T, GLA_HEADS, GLA_DV).astype(jnp.float32),
            la.reshape(shp), g)

def gla_chunk(S0, q, k, v, la):
    C = q.shape[1]
    b = jnp.cumsum(la, axis=1)
    causal = jnp.tril(jnp.ones((C, C), dtype=bool))
    diff = b[:, :, None] - b[:, None, :]
    decay = jnp.exp(jnp.where(causal[None, :, :, None, None], diff, -jnp.inf))
    A = jnp.einsum('bthk,bshk,btshk->bhts', q, k, decay)
    o = (jnp.einsum('bthk,bhkv->bthv', q * jnp.exp(b), S0)
         + jnp.einsum('bhts,bshv->bthv', A, v))
    bC = b[:, -1]
    S1 = (jnp.exp(bC)[..., None] * S0
          + jnp.einsum('bshk,bshv->bhkv', k * jnp.exp(bC[:, None] - b), v))
    return S1, o

def gla_output(o, g, norm_g, w_o):
    B, T = o.shape[0], o.shape[1]
    o = rmsnorm(o, norm_g).reshape(B, T, GLA_HEADS * GLA_DV)
    o = o * jax.nn.silu(g.astype(jnp.float32))
    return o.astype(g.dtype) @ w_o

def gla_prompt(x, w_in, w_a2, b_a, norm_g, w_o):
    B, S, _ = x.shape
    q, k, v, la, g = gla_project(x, w_in, w_a2, b_a)
    n = S // GLA_CHUNK

    def chunks(a):
        return jnp.moveaxis(a.reshape((B, n, GLA_CHUNK) + a.shape[2:]), 1, 0)

    S0 = jnp.zeros((B, GLA_HEADS, GLA_DK, GLA_DV), jnp.float32)
    S_fin, o = lax.scan(lambda s, xs: gla_chunk(s, xs[0], xs[1], xs[2], xs[3]), S0,
                        (chunks(q), chunks(k), chunks(v), chunks(la)))
    o = jnp.moveaxis(o, 0, 1).reshape(B, S, GLA_HEADS, GLA_DV)
    return gla_output(o, g, norm_g, w_o), S_fin.astype(x.dtype)

def gla_sample(x, state, w_in, w_a2, b_a, norm_g, w_o):
    q, k, v, la, g = gla_project(x, w_in, w_a2, b_a)
    S1, o = gla_chunk(state.astype(jnp.float32), q, k, v, la)
    return gla_output(o, g, norm_g, w_o), S1.astype(x.dtype)

def setup_inputs(seed: int = 0) -> dict:
    key = jax.random.key(seed)
    ks = jax.random.split(key, 20)
    f32 = jnp.float32
    nrm = lambda k, shp, s: jax.random.normal(k, shp, f32) * s
    return {
        'x_prompt': nrm(ks[0], (BATCH, SEQ, D_MODEL), 1.0),
        'x_sample': nrm(ks[1], (DEC_BATCH, DEC_SEQ, D_MODEL), 1.0),
        'cache_k': nrm(ks[2], (N_A, DEC_BATCH, PAST_LEN, A_KV_HEADS, A_HEAD_DIM), 1.0),
        'cache_v': nrm(ks[3], (N_A, DEC_BATCH, PAST_LEN, A_KV_HEADS, A_HEAD_DIM), 1.0),
        'cache_kidx': nrm(ks[4], (N_A, DEC_BATCH, PAST_LEN, IDX_DIM), 1.0),
        'state_gla': nrm(ks[5], (N_B, DEC_BATCH, GLA_HEADS, GLA_DK, GLA_DV), 1.0),
        'norm_mix': 1.0 + nrm(ks[6], (DEPTH, D_MODEL), 0.01),
        'norm_ffn': 1.0 + nrm(ks[7], (DEPTH, D_MODEL), 0.01),
        'norm_final': 1.0 + nrm(ks[8], (D_MODEL,), 0.01),
        'a_w_in': nrm(ks[9], (N_A, D_MODEL, A_IN), D_MODEL ** -0.5),
        'a_w_o': nrm(ks[10], (N_A, A_HEADS * A_HEAD_DIM, D_MODEL), (A_HEADS * A_HEAD_DIM) ** -0.5),
        'b_w_in': nrm(ks[11], (N_B, D_MODEL, B_IN), D_MODEL ** -0.5),
        'b_w_a2': nrm(ks[12], (N_B, GLA_RANK, GLA_HEADS * GLA_DK), GLA_RANK ** -0.5),
        'b_b_a': nrm(ks[13], (N_B, GLA_HEADS * GLA_DK), 0.1),
        'b_norm': 1.0 + nrm(ks[14], (N_B, GLA_DV), 0.01),
        'b_w_o': nrm(ks[15], (N_B, GLA_HEADS * GLA_DV, D_MODEL), (GLA_HEADS * GLA_DV) ** -0.5),
        'ffn_w_up': nrm(ks[16], (DEPTH, D_MODEL, D_FF), D_MODEL ** -0.5),
        'ffn_w_down': nrm(ks[17], (DEPTH, D_FF, D_MODEL), D_FF ** -0.5),
    }

def reference(x_prompt, x_sample, cache_k, cache_v, cache_kidx, state_gla,
              norm_mix, norm_ffn, norm_final, a_w_in, a_w_o,
              b_w_in, b_w_a2, b_b_a, b_norm, b_w_o, ffn_w_up, ffn_w_down):
    hp, hs = x_prompt, x_sample
    kp_l, vp_l, ip_l, sp_l = [], [], [], []
    ks_l, vs_l, is_l, ss_l = [], [], [], []
    for i in range(DEPTH):
        j = i // N_MIXERS
        up = rmsnorm(hp, norm_mix[i])
        us = rmsnorm(hs, norm_mix[i])
        if i % N_MIXERS == 0:
            mp, k1, v1, i1 = dsa_prompt(up, a_w_in[j], a_w_o[j])
            ms, k2, v2, i2 = dsa_sample(us, cache_k[j], cache_v[j], cache_kidx[j], a_w_in[j], a_w_o[j])
            kp_l.append(k1); vp_l.append(v1); ip_l.append(i1)
            ks_l.append(k2); vs_l.append(v2); is_l.append(i2)
        else:
            mp, s1 = gla_prompt(up, b_w_in[j], b_w_a2[j], b_b_a[j], b_norm[j], b_w_o[j])
            ms, s2 = gla_sample(us, state_gla[j], b_w_in[j], b_w_a2[j], b_b_a[j], b_norm[j], b_w_o[j])
            sp_l.append(s1); ss_l.append(s2)
        hp = hp + mp
        hs = hs + ms
        hp = hp + sq_relu_mlp(rmsnorm(hp, norm_ffn[i]), ffn_w_up[i], ffn_w_down[i])
        hs = hs + sq_relu_mlp(rmsnorm(hs, norm_ffn[i]), ffn_w_up[i], ffn_w_down[i])
    y_prompt = rmsnorm(hp, norm_final)
    y_sample = rmsnorm(hs, norm_final)
    k_prompt = jnp.stack(kp_l)
    v_prompt = jnp.stack(vp_l)
    kidx_prompt = jnp.stack(ip_l)
    gla_prompt_state = jnp.stack(sp_l)
    k_sample = jnp.stack(ks_l)
    v_sample = jnp.stack(vs_l)
    kidx_sample = jnp.stack(is_l)
    gla_sample_state = jnp.stack(ss_l)
    return (y_prompt, y_sample, k_prompt, v_prompt, kidx_prompt, gla_prompt_state,
            k_sample, v_sample, kidx_sample, gla_sample_state)


_drawn_inputs = setup_inputs


def setup_inputs(seed=0):
    import zlib

    import numpy as np

    out = dict(_drawn_inputs(seed))
    spreads = {}
    factors = {}
    for name, (base, spread) in spreads.items():
        noise = np.random.default_rng([zlib.crc32(name.encode()), seed]).standard_normal(out[name].shape)
        drawn = base * np.exp(spread * noise) if base else spread * noise
        out[name] = __import__('jax').numpy.asarray(drawn.astype(out[name].dtype))
    for name, factor in factors.items():
        out[name] = (out[name] * factor).astype(out[name].dtype)
    return out
```

```python
from contextlib import ExitStack

import numpy as np

import concourse.bass as bass
from concourse import mybir

F32 = mybir.dt.float32
F32R = mybir.dt.float32r
U32 = mybir.dt.uint32
ACT = mybir.ActivationFunctionType
ALU = mybir.AluOpType
AX = mybir.AxisListType

P = 128
D = 1024
KB = D // P
SEQ, DEC_B, DEC_T, PAST = 1024, 8, 16, 512
NT_P = SEQ // P
NT = NT_P + 1
TOK = NT * P
GRP = 3
NG = NT // GRP
GW = GRP * P
HEADS, KVH, HD = 16, 4, 64
IH, ID = 8, 64
TOPK_P, TOPK_S = 256, (PAST + DEC_T) // 4
CHUNK = 64
A_IN = HEADS * HD + 2 * KVH * HD + IH * ID + ID + IH
GH, DK, DV, RANK = 4, 128, 256, 16
TAU = 16.0
B_IN = 2 * GH * DK + GH * DV + D + RANK
FF = 4 * D
CW = 256
EPS = 1e-6
FILL = -3.0e38
MARK = -3.2e38
CUT = -3.1e38
NEG = -1.0e30
LEVELS = (64, 32, 16, 8, 4, 2, 1)


def bc(ap, n):
    return ap.rearrange("(a n) -> a n", a=1).broadcast_to([P, n])


class Block:

    def __init__(self, nc, name):
        self.nc, self.name, self.ctx, self.sems = nc, name, ExitStack(), []

    def __enter__(self):
        self.ctx.__enter__()
        return self

    def __exit__(self, *a):
        if a[0] is None:
            self.nc.clear_and_free_semaphores(self.sems)
            self.nc.all_engine_barrier()
        return self.ctx.__exit__(*a)

    def sb(self, name, shape, dt=F32):
        return self.ctx.enter_context(self.nc.sbuf_tensor(f"{self.name}_{name}", shape, dt))

    def ps(self, name, shape, dt=F32):
        return self.ctx.enter_context(self.nc.psum_tensor(f"{self.name}_{name}", shape, dt))

    def sem(self, name):
        self.sems.append(self.nc.alloc_semaphore(f"{self.name}_{name}"))
        return self.sems[-1]


class TokenStage:

    def __init__(self, b, ident, src_dram=None, src_sb=None, gamma=None):
        self.b, self.ident, self.src_dram, self.src_sb, self.gamma = b, ident, src_dram, src_sb, gamma
        self.hi = b.sb("xT_hi", [P, KB, TOK], F32R)
        self.lo = b.sb("xT_lo", [P, KB, TOK], F32R)
        self.psT = b.ps("psT", [P, 2, 512])
        self.tile_in = [b.sem("tile_in0"), b.sem("tile_in1")]
        if src_dram is not None:
            self.x = b.sb("x_in", [P, 2, D])
        self.normed = gamma is not None
        if self.normed:
            self.junk = b.sb("sq_junk", [P, D])
            self.g = b.sb("gamma", [P, D])
            self.ss = b.sb("sumsq", [P, NT])
            self.ms = b.sb("meansq", [P, NT])
            self.rstd = b.sb("rstd", [P, NT])
            self.mhalf = b.sb("mhalf", [P, 1])
            self.u = b.sb("u", [P, 2, D])
            self.gamma_in, self.sumsq_ready = b.sem("gamma_in"), b.sem("sumsq_ready")
            self.mhalf_ready, self.ms_ready, self.rstd_ready = b.sem("mhalf_ready"), b.sem("ms_ready"), b.sem("rstd_ready")
            self.u_ready = b.sem("u_ready")
        self.t_done, self.hi_done, self.lo_done = b.sem("t_done"), b.sem("thi_done"), b.sem("tlo_done")

    def tile(self, t):
        return self.src_sb[:, t, :] if self.src_sb is not None else self.x[:, t % 2, :]

    def wait_tile(self, e, t):
        if self.src_sb is None:
            e.wait_ge(self.tile_in[t % 2], 16 * (t // 2 + 1))

    def load_gamma(self, e):
        if self.normed:
            e.dma_start(self.g[:, :], bc(self.gamma, D)).then_inc(self.gamma_in, 16)

    def load(self, e, t):
        if self.src_sb is not None:
            return
        if t >= 2:
            if self.normed:
                e.wait_ge(self.u_ready, t - 1)
            else:
                e.wait_ge(self.t_done, 2 * (t - 1))
        e.dma_start(self.x[:, t % 2, :], self.src_dram(t)).then_inc(self.tile_in[t % 2], 16)

    def act_sumsq(self, e, t):
        if self.normed:
            self.wait_tile(e, t)
            if t >= 1:
                e.wait_ge(self.sumsq_ready, t)
            e.activation(self.junk[:, :], self.tile(t), ACT.Square, accum_out=self.ss[:, t:t + 1])\
                .then_inc(self.sumsq_ready, 1)

    def act_hi(self, e, t):
        for half in range(2):
            e.wait_ge(self.t_done, 2 * t + half + 1)
            e.activation(self.hi[:, 4 * half:4 * half + 4, t * P:(t + 1) * P],
                         self.psT[:, half, :].rearrange("p (k c) -> p k c", k=4), ACT.Copy).then_inc(self.hi_done, 1)

    def pool_consts(self, e):
        if self.normed:
            e.memset(self.mhalf[:, :], -0.5).then_inc(self.mhalf_ready, 1)
            e.wait_ge(self.mhalf_ready, 1)

    def pool_rstd(self, e, t):
        if self.normed:
            e.wait_ge(self.sumsq_ready, t + 1)
            e.tensor_scalar(self.ms[:, t:t + 1], self.ss[:, t:t + 1], 1.0 / D, EPS, ALU.mult, ALU.add)\
                .then_inc(self.ms_ready, 1)
            e.wait_ge(self.ms_ready, t + 1)
            e.tensor_tensor(self.rstd[:, t:t + 1], self.ms[:, t:t + 1], self.mhalf[:, :], ALU.pow)\
                .then_inc(self.rstd_ready, 1)

    def dve_norm(self, e, t):
        if self.normed:
            if t == 0:
                e.wait_ge(self.gamma_in, 16)
            if t >= 2:
                e.wait_ge(self.t_done, 2 * (t - 1))
            self.wait_tile(e, t)
            e.wait_ge(self.rstd_ready, t + 1)
            e.scalar_tensor_tensor(self.u[:, t % 2, :], self.tile(t), self.rstd[:, t:t + 1], self.g[:, :],
                                   ALU.mult, ALU.mult).then_inc(self.u_ready, 1)

    def dve_lo(self, e, t):
        for half in range(2):
            e.wait_ge(self.hi_done, 2 * t + half + 1)
            e.tensor_tensor(self.lo[:, 4 * half:4 * half + 4, t * P:(t + 1) * P],
                            self.psT[:, half, :].rearrange("p (k c) -> p k c", k=4),
                            self.hi[:, 4 * half:4 * half + 4, t * P:(t + 1) * P].bitcast(F32), ALU.subtract)\
                .then_inc(self.lo_done, 1)

    def pe_transpose(self, e, t):
        if self.normed:
            e.wait_ge(self.u_ready, t + 1)
        else:
            self.wait_tile(e, t)
        src = self.u[:, t % 2, :] if self.normed else self.tile(t)
        for half in range(2):
            if t >= 1:
                e.wait_ge(self.lo_done, 2 * t + half - 1)
            for k in range(4):
                kk = 4 * half + k
                mm = e.transpose(self.psT[:, half, k * P:(k + 1) * P], src[:, kk * P:(kk + 1) * P], self.ident[:, :])
            mm.then_inc(self.t_done, 1)

    def wait_ready(self, e, tiles):
        e.wait_ge(self.lo_done, 2 * tiles)


def three(hi, lo):
    return ((0, 0), (0, 1), (1, 0))


def gemm_phase(nc, name, ident, chunks, src_dram=None, src_sb=None, gamma=None, residual=None, h=None):
    with Block(nc, name) as b:
        st = TokenStage(b, ident, src_dram, src_sb, gamma)
        raw = b.sb("w_raw", [P, 2, KB, CW])
        whi = b.sb("w_hi", [P, 2, KB, CW], F32R)
        wlo = b.sb("w_lo", [P, 2, KB, CW], F32R)
        NB = 4
        acc = b.ps("acc", [P, NB, 512])
        stage = b.sb("stage", [P, NB, GW])
        w_in = [b.sem("w_in0"), b.sem("w_in1")]
        whi_done, wlo_done = b.sem("whi_done"), b.sem("wlo_done")
        unit_done, unit_out = b.sem("unit_done"), b.sem("unit_out")
        sig_done = b.sem("sig_done")
        stored = [b.sem(f"stored{i}") for i in range(NB)]
        res_in = [b.sem(f"res_in{i}") for i in range(NB)]
        silu = any(c["op"] == "silu" for c in chunks)
        if silu:
            sig = b.sb("sigmoid", [P, 2, CW])
        if residual is not None:
            res = b.sb("residual", [P, NB, CW])
        units, n_sig = [], 0
        for ci, c in enumerate(chunks):
            M = c["w"].shape[1]
            us = []
            for g in range(NG):
                if c["form"] == "T":
                    for j in range(0, M, P):
                        us.append(dict(c=ci, g=g, j=j, m=min(P, M - j), n=GW))
                else:
                    for t in range(GRP * g, GRP * g + GRP):
                        us.append(dict(c=ci, g=g, t=t, m=P, n=M))
            for u in us:
                u["i"], u["op"], u["form"] = len(units), c["op"], c["form"]
                u["sig"] = n_sig
                n_sig += c["op"] == "silu"
                u["stores"] = c["out"](u) if c["out"] else []
                units.append(u)
        of = [[u for u in units if u["c"] == ci] for ci in range(len(chunks))]
        for s in range(NB):
            n = 0
            for u in units[s::NB]:
                u["stored_before"] = n
                n += 16 * len(u["stores"])
            total = n
            for u in units[s::NB]:
                u["stored_total"] = total

        with nc.Block() as block:
            @block.sync
            def _(sp):
                def load_w(ci):
                    c = chunks[ci]
                    if ci >= 2:
                        sp.wait_ge(wlo_done, ci - 1)
                    M = c["w"].shape[1]
                    sp.dma_start(raw[:, ci % 2, :, 0:M], c["w"].rearrange("(k p) n -> p k n", p=P))\
                        .then_inc(w_in[ci % 2], 16)

                def load_res(u):
                    if residual is None:
                        return
                    if u["i"] >= NB:
                        sp.wait_ge(unit_out, u["i"] - NB + 1)
                    c0 = u["c"] * CW
                    sp.dma_start(res[:, u["i"] % NB, :], residual(u["t"])[:, c0:c0 + CW])\
                        .then_inc(res_in[u["i"] % NB], 16)

                st.load(sp, 0)
                st.load_gamma(sp)
                st.load(sp, 1)
                load_w(0)
                for t in range(2, NT):
                    st.load(sp, t)
                    if t == 3 and len(chunks) > 1:
                        load_w(1)
                for u in units[:NB]:
                    load_res(u)
                for ci in range(len(chunks)):
                    if ci + 2 < len(chunks):
                        load_w(ci + 2)
                    for u in of[ci]:
                        if u["stores"]:
                            sp.wait_ge(unit_out, u["i"] + 1)
                        for dst, view in u["stores"]:
                            sp.dma_start(dst, view(stage[:, u["i"] % NB, :])).then_inc(stored[u["i"] % NB], 16)
                        if u["i"] + NB < len(units):
                            load_res(units[u["i"] + NB])
                for s in range(NB):
                    if len(units) > s and units[s]["stored_total"]:
                        sp.wait_ge(stored[s], units[s]["stored_total"])

            @block.scalar
            def _(act):
                def w_hi(ci):
                    M = chunks[ci]["w"].shape[1]
                    act.wait_ge(w_in[ci % 2], 16 * (ci // 2 + 1))
                    if ci >= 2:
                        act.wait_ge(unit_done, of[ci - 2][-1]["i"] + 1)
                    act.activation(whi[:, ci % 2, :, 0:M], raw[:, ci % 2, :, 0:M], ACT.Copy).then_inc(whi_done, 1)

                for t in range(NT):
                    st.act_sumsq(act, t)
                    if t >= 1:
                        st.act_hi(act, t - 1)
                    if t == 1:
                        w_hi(0)
                st.act_hi(act, NT - 1)
                if len(chunks) > 1:
                    w_hi(1)
                for ci in range(len(chunks)):
                    for u in of[ci]:
                        if u["op"] == "silu":
                            act.wait_ge(unit_done, u["i"] + 1)
                            if u["sig"] >= 2:
                                act.wait_ge(unit_out, u["i"] - 1)
                            act.activation(sig[:, u["sig"] % 2, 0:u["n"]], acc[:, u["i"] % NB, 0:u["n"]], ACT.Sigmoid)\
                                .then_inc(sig_done, 1)
                    if ci + 2 < len(chunks):
                        w_hi(ci + 2)

            @block.gpsimd
            def _(pool):
                def w_lo(ci):
                    M = chunks[ci]["w"].shape[1]
                    pool.wait_ge(whi_done, ci + 1)
                    pool.tensor_tensor(wlo[:, ci % 2, :, 0:M], raw[:, ci % 2, :, 0:M],
                                       whi[:, ci % 2, :, 0:M].bitcast(F32), ALU.subtract).then_inc(wlo_done, 1)

                st.pool_consts(pool)
                for t in range(NT):
                    st.pool_rstd(pool, t)
                    if t == 2:
                        w_lo(0)
                for ci in range(1, len(chunks)):
                    w_lo(ci)

            def unit_mms(pe, u):
                if u["i"] >= NB:
                    pe.wait_ge(unit_out, u["i"] - NB + 1)
                s = u["c"] % 2
                w, x = (whi, wlo), (st.hi, st.lo)
                last = KB * 3 - 1
                n = 0
                for k in range(KB):
                    for a, c in three(0, 0):
                        if u["form"] == "T":
                            mm = pe.matmul(acc[0:u["m"], u["i"] % NB, 0:GW], w[a][:, s, k, u["j"]:u["j"] + u["m"]],
                                           x[c][:, k, u["g"] * GW:(u["g"] + 1) * GW], start=(n == 0), stop=(n == last))
                        else:
                            mm = pe.matmul(acc[:, u["i"] % NB, 0:u["n"]], x[c][:, k, u["t"] * P:(u["t"] + 1) * P],
                                           w[a][:, s, k, 0:u["n"]], start=(n == 0), stop=(n == last))
                        n += 1
                mm.then_inc(unit_done, 1)

            @block.tensor
            def _(pe):
                pending = list(units)
                for t in range(NT):
                    st.pe_transpose(pe, t)
                    if t % GRP == GRP - 1 and t >= 2 * GRP - 1:
                        if t == 2 * GRP - 1:
                            pe.wait_ge(wlo_done, 1)
                        g = t // GRP - 1
                        st.wait_ready(pe, GRP * (g + 1))
                        while pending and pending[0]["c"] == 0 and pending[0]["g"] == g:
                            unit_mms(pe, pending.pop(0))
                st.wait_ready(pe, NT)
                ci = 0
                for u in pending:
                    if u["c"] != ci:
                        ci = u["c"]
                        pe.wait_ge(wlo_done, ci + 1)
                    unit_mms(pe, u)

            @block.vector
            def _(dve):
                def evacuate(u):
                    i, m, n = u["i"], u["m"], u["n"]
                    dve.wait_ge(unit_done, i + 1)
                    if i >= NB:
                        dve.wait_ge(unit_out, i - NB + 1)
                    if u["stored_before"]:
                        dve.wait_ge(stored[i % NB], u["stored_before"])
                    src, dst = acc[0:m, i % NB, 0:n], stage[0:m, i % NB, 0:n]
                    if u["op"] == "copy":
                        dve.tensor_copy(dst, src).then_inc(unit_out, 1)
                    elif u["op"] == "silu":
                        dve.wait_ge(sig_done, u["sig"] + 1)
                        dve.tensor_tensor(dst, src, sig[:, u["sig"] % 2, 0:n], ALU.mult).then_inc(unit_out, 1)
                    elif u["op"] == "resid":
                        cols = h[:, u["t"], u["c"] * CW:u["c"] * CW + n]
                        if residual is not None:
                            dve.wait_ge(res_in[i % NB], 16 * (i // NB + 1))
                            dve.tensor_tensor(cols, src, res[:, i % NB, 0:n], ALU.add).then_inc(unit_out, 1)
                        else:
                            dve.tensor_tensor(cols, src, cols, ALU.add).then_inc(unit_out, 1)
                    else:
                        dve.tensor_scalar(dst, src, u["op"], None, ALU.mult).then_inc(unit_out, 1)

                pending = list(units)
                for t in range(NT):
                    st.dve_norm(dve, t)
                    if t >= 1:
                        st.dve_lo(dve, t - 1)
                    if t % GRP == 0 and t >= 2 * GRP:
                        g = t // GRP - 2
                        while pending and pending[0]["c"] == 0 and pending[0]["g"] == g:
                            evacuate(pending.pop(0))
                st.dve_lo(dve, NT - 1)
                for u in pending:
                    evacuate(u)


def mlp_phase(nc, name, ident, h, gamma, w_up, w_down):
    NCH = FF // CW
    UU = NG * (CW // P)
    DU = NT * (D // 512)
    with Block(nc, name) as b:
        st = TokenStage(b, ident, None, h, gamma)
        FB = CW // P
        up_raw, dn_raw = b.sb("up_raw", [P, KB, CW]), b.sb("dn_raw", [P, FB, D])
        up_hi, up_lo = b.sb("up_hi", [P, KB, CW], F32R), b.sb("up_lo", [P, KB, CW], F32R)
        dn_hi, dn_lo = b.sb("dn_hi", [P, FB, D], F32R), b.sb("dn_lo", [P, FB, D], F32R)
        hid_hi, hid_lo = b.sb("hid_hi", [P, FB, TOK], F32R), b.sb("hid_lo", [P, FB, TOK], F32R)
        relu, sq = b.sb("relu", [P, 2, GW]), b.sb("sq", [P, 2, GW])
        up_acc, dn_acc = b.ps("up_acc", [P, 3, 512]), b.ps("dn_acc", [P, 3, 512])
        up_in, dn_in = b.sem("up_in"), b.sem("dn_in")
        up_hi_done, up_lo_done = b.sem("up_hi_done"), b.sem("up_lo_done")
        dn_hi_done, dn_lo_done = b.sem("dn_hi_done"), b.sem("dn_lo_done")
        up_done, dn_done, added = b.sem("up_done"), b.sem("dn_done"), b.sem("added")
        relu_done, sq_done = b.sem("relu_done"), b.sem("sq_done")
        hid_hi_done, hid_lo_done = b.sem("hid_hi_done"), b.sem("hid_lo_done")

        def up_src(i):
            return w_up[:, bass.ds(i * CW, CW)].rearrange("(k p) n -> p k n", p=P)

        def dn_src(i):
            return w_down[bass.ds(i * CW, CW), :].rearrange("(k p) n -> p k n", p=P)

        def chunks_loop(e, body):
            body(0, True, False)
            with e.Fori(1, NCH - 1) as i:
                body(i, False, False)
            body(NCH - 1, False, True)

        with nc.Block() as block:
            @block.sync
            def _(sp):
                st.load_gamma(sp)
                sp.dma_start(up_raw[:, :, :], up_src(0)).then_inc(up_in, 16)
                sp.dma_start(dn_raw[:, :, :], dn_src(0)).then_inc(dn_in, 16)

            @block.scalar
            def _(act):
                def split_up(i):
                    act.wait_ge(up_in, i * 16 + 16)
                    act.activation(up_hi[:, :, :], up_raw[:, :, :], ACT.Copy).then_inc(up_hi_done, 1)

                def body(i, first, last):
                    act.wait_ge(dn_in, i * 16 + 16)
                    if not first:
                        act.wait_ge(dn_done, i * DU)
                    act.activation(dn_hi[:, :, :], dn_raw[:, :, :], ACT.Copy).then_inc(dn_hi_done, 1)
                    if not last:
                        act.wait_ge(up_lo_done, i + 1)
                        act.dma_start(up_raw[:, :, :], up_src(i + 1)).then_inc(up_in, 16)
                    for u in range(UU):
                        g, j = u // FB, u % FB
                        act.wait_ge(up_done, i * UU + (u + 1))
                        if not (first and u < 2):
                            act.wait_ge(hid_lo_done, i * UU + (u - 1))
                        act.activation(relu[:, u % 2, :], up_acc[:, u % 3, 0:GW], ACT.Relu).then_inc(relu_done, 1)
                        act.wait_ge(relu_done, i * UU + (u + 1))
                        act.activation(hid_hi[:, j, g * GW:(g + 1) * GW], relu[:, u % 2, :], ACT.Square)\
                            .then_inc(hid_hi_done, 1)
                    if not last:
                        split_up(i + 1)
                        act.wait_ge(dn_lo_done, i + 1)
                        act.dma_start(dn_raw[:, :, :], dn_src(i + 1)).then_inc(dn_in, 16)

                for t in range(NT):
                    st.act_sumsq(act, t)
                    if t >= 1:
                        st.act_hi(act, t - 1)
                    if t == 1:
                        split_up(0)
                st.act_hi(act, NT - 1)
                chunks_loop(act, body)

            @block.gpsimd
            def _(pool):
                def split_up(i):
                    pool.wait_ge(up_hi_done, i + 1)
                    pool.tensor_tensor(up_lo[:, :, :], up_raw[:, :, :], up_hi[:, :, :].bitcast(F32), ALU.subtract)\
                        .then_inc(up_lo_done, 1)

                def body(i, first, last):
                    pool.wait_ge(dn_hi_done, i + 1)
                    pool.tensor_tensor(dn_lo[:, :, :], dn_raw[:, :, :], dn_hi[:, :, :].bitcast(F32), ALU.subtract)\
                        .then_inc(dn_lo_done, 1)
                    if not last:
                        split_up(i + 1)

                st.pool_consts(pool)
                for t in range(NT):
                    st.pool_rstd(pool, t)
                split_up(0)
                chunks_loop(pool, body)

            @block.tensor
            def _(pe):
                w_up_s, w_dn_s = (up_hi, up_lo), (dn_hi, dn_lo)
                x_s, hid_s = (st.hi, st.lo), (hid_hi, hid_lo)

                def up_unit(i, u, first):
                    g, j = u // FB, u % FB
                    if not (first and u < 3):
                        pe.wait_ge(relu_done, i * UU + (u - 2))
                    n = 0
                    for k in range(KB):
                        for a, c in three(0, 0):
                            mm = pe.matmul(up_acc[:, u % 3, 0:GW], w_up_s[a][:, k, j * P:(j + 1) * P],
                                           x_s[c][:, k, g * GW:(g + 1) * GW], start=(n == 0), stop=(n == 3 * KB - 1))
                            n += 1
                    mm.then_inc(up_done, 1)

                def body(i, first, last):
                    pe.wait_ge(up_lo_done, i + 1)
                    for u in range(UU):
                        if first and u % FB == 0:
                            st.wait_ready(pe, GRP * (u // FB + 1))
                        up_unit(i, u, first)
                    pe.wait_ge(dn_lo_done, i + 1)
                    for v in range(DU):
                        t, half = v // 2, v % 2
                        if v % (2 * GRP) == 0:
                            pe.wait_ge(hid_lo_done, i * UU + FB * (t // GRP + 1))
                        if not (first and v < 3):
                            pe.wait_ge(added, i * DU + (v - 2))
                        n = 0
                        for k in range(FB):
                            for a, c in three(0, 0):
                                mm = pe.matmul(dn_acc[:, v % 3, :], hid_s[c][:, k, t * P:(t + 1) * P],
                                               w_dn_s[a][:, k, half * 512:(half + 1) * 512],
                                               start=(n == 0), stop=(n == 3 * FB - 1))
                                n += 1
                        mm.then_inc(dn_done, 1)

                for t in range(NT):
                    st.pe_transpose(pe, t)
                chunks_loop(pe, body)

            @block.vector
            def _(dve):
                def body(i, first, last):
                    for u in range(UU):
                        g, j = u // FB, u % FB
                        dve.wait_ge(relu_done, i * UU + (u + 1))
                        dve.tensor_tensor(sq[:, u % 2, :], relu[:, u % 2, :], relu[:, u % 2, :], ALU.mult)\
                            .then_inc(sq_done, 1)
                        dve.wait_ge(sq_done, i * UU + (u + 1))
                        dve.wait_ge(hid_hi_done, i * UU + (u + 1))
                        dve.tensor_tensor(hid_lo[:, j, g * GW:(g + 1) * GW], sq[:, u % 2, :],
                                          hid_hi[:, j, g * GW:(g + 1) * GW].bitcast(F32), ALU.subtract)\
                            .then_inc(hid_lo_done, 1)
                    for v in range(DU):
                        t, half = v // 2, v % 2
                        cols = h[:, t, half * 512:(half + 1) * 512]
                        dve.wait_ge(dn_done, i * DU + (v + 1))
                        dve.tensor_tensor(cols, dn_acc[:, v % 3, :], cols, ALU.add).then_inc(added, 1)

                for t in range(NT):
                    st.dve_norm(dve, t)
                    if t >= 1:
                        st.dve_lo(dve, t - 1)
                st.dve_lo(dve, NT - 1)
                chunks_loop(dve, body)


def prompt_attention_phase(nc, name, ident, qT, qiT, wt, k_out, v_out, ki_out, o):
    with Block(nc, name) as b:
        kin, kiin = b.sb("k_in", [P, NT_P, KVH, 2, HD]), b.sb("ki_in", [P, NT_P, 2, ID])
        vin = b.sb("v_in", [P, NT_P, KVH * HD])
        kT = [b.sb("kT_even", [P, KVH, SEQ]), b.sb("kT_odd", [P, KVH, SEQ])]
        kiT = [b.sb("kiT_even", [P, SEQ]), b.sb("kiT_odd", [P, SEQ])]
        q, qi = b.sb("q", [P, 2, HEADS // 2, P]), b.sb("qi", [P, 2, IH // 2, P])
        w_raw, w = b.sb("w_raw", [P, NT_P, IH]), b.sb("w", [P, NT_P, IH])
        score = b.sb("score", [P, 4, SEQ])
        rl = b.sb("relu", [P, 2, SEQ])
        top8 = b.sb("top8", [P, 8])
        lg = b.sb("logits", [P, 3, SEQ])
        probs_T = b.sb("probs_T", [P, 2, SEQ])
        mx, nm = b.sb("max", [P, 4]), b.sb("neg_max", [P, 4])
        den, rden = b.sb("den", [P, 4]), b.sb("rden", [P, 4])
        ot = b.sb("o_tile", [P, 2, D])
        slot = b.ps("slot", [P, 2, SEQ])
        psT = b.ps("psT", [P, 2, 512])
        pv = b.ps("pv", [P, 2, 512])
        kv_in, v_in, w_in = b.sem("kv_in"), b.sem("v_in"), b.sem("w_in")
        zeros_done, w_done = b.sem("zeros_done"), b.sem("w_done")
        q_in, qi_in = [b.sem("q_in0"), b.sem("q_in1")], [b.sem("qi_in0"), b.sem("qi_in1")]
        keys_turned, keys_even, keys_odd = b.sem("keys_turned"), b.sem("keys_even"), b.sem("keys_odd")
        qi_done, relu_done, scored = b.sem("qi_done"), b.sem("relu_done"), b.sem("scored")
        filled, top8_done, replaced, bias_done = b.sem("filled"), b.sem("top8_done"), b.sem("replaced"), b.sem("bias_done")
        qk_done, masked, neg_done, exp_done = b.sem("qk_done"), b.sem("masked"), b.sem("neg_done"), b.sem("exp_done")
        turned, turned_out, pv_done = b.sem("turned"), b.sem("turned_out"), b.sem("pv_done")
        rden_done, o_done = b.sem("rden_done"), b.sem("o_done")
        o_stored = [b.sem("o_stored0"), b.sem("o_stored1")]

        T0 = 2
        ROUNDS = TOPK_P // 8
        steps = [("index", T0, ih) for ih in range(IH)]
        for t in range(NT_P):
            for hd in range(HEADS):
                steps.append(("head", t, hd))
                if hd % 2 == 0 and T0 < t + 3 < NT_P:
                    steps.append(("index", t + 3, hd // 2))
        n_head = n_index = 0
        uses = []
        plan = []
        for kind, t, x in steps:
            no = n_head if kind == "head" else n_index
            n_head, n_index = n_head + (kind == "head"), n_index + (kind == "index")
            plan.append((kind, t, x, no, len(uses)))
            uses.append((kind, no))
        N = NT_P * HEADS
        banks = []
        bank_of = {}
        for n in range(N):
            L = n // HEADS + 1
            bank_of[n] = []
            for b0 in range(0, L, 4):
                bank_of[n].append(len(banks))
                banks.append((n, b0, min(4, L - b0)))

        def wait_slot(pe, s):
            if s >= 2:
                kind, no = uses[s - 2]
                pe.wait_ge(relu_done if kind == "index" else masked, no + 1)

        with nc.Block() as block:
            @block.sync
            def _(sp):
                for r in range(2):
                    for t in range(NT_P):
                        sp.dma_start(kin[:, t, :, r, :], k_out[t * P:(t + 1) * P, :].rearrange("p (v d) -> p v d", d=HD))\
                            .then_inc(kv_in, 16)
                    sp.dma_start(kiin[:, :, r, :], ki_out.rearrange("(t p) c -> p t c", p=P)).then_inc(kv_in, 16)
                sp.dma_start(w_raw[:, :, :], wt[0:SEQ, :].rearrange("(t p) c -> p t c", p=P)).then_inc(w_in, 16)

                def load_qi(t):
                    if t >= T0 + 2:
                        sp.wait_ge(qi_done, IH * (t - T0 - 1))
                    sp.dma_start(qi[:, t % 2, :, :], qiT[:, t * P:(t + 1) * P].rearrange("(c p) n -> p c n", p=P))\
                        .then_inc(qi_in[t % 2], 16)

                def load_q(t):
                    if t >= 2:
                        sp.wait_ge(qk_done, HEADS * (t - 1))
                    sp.dma_start(q[:, t % 2, :, :], qT[:, t * P:(t + 1) * P].rearrange("(c p) n -> p c n", p=P))\
                        .then_inc(q_in[t % 2], 16)

                load_qi(T0)
                load_q(0)
                sp.dma_start(vin[:, :, :], v_out.rearrange("(t p) c -> p t c", p=P)).then_inc(v_in, 16)
                load_q(1)
                load_qi(T0 + 1)
                for t in range(NT_P):
                    if t >= 1 and t + 1 < NT_P:
                        load_q(t + 1)
                    if T0 + 1 < t + 4 < NT_P:
                        load_qi(t + 4)
                    sp.wait_ge(o_done, HEADS * (t + 1))
                    sp.dma_start(o[t * P:(t + 1) * P, :], ot[:, t % 2, :]).then_inc(o_stored[t % 2], 16)
                for i in range(2):
                    sp.wait_ge(o_stored[i], 16 * NT_P // 2)

            @block.gpsimd
            def _(pool):
                pool.memset(kT[0][HD:P, :, :], 0.0).then_inc(zeros_done, 1)
                pool.memset(kT[1][0:HD, :, :], 0.0).then_inc(zeros_done, 1)
                pool.memset(kiT[0][HD:P, :], 0.0).then_inc(zeros_done, 1)
                pool.memset(kiT[1][0:HD, :], 0.0).then_inc(zeros_done, 1)

            @block.tensor
            def _(pe):
                pe.wait_ge(kv_in, 32 * (NT_P + 1))
                for r in range(NT_P + 2):
                    if r >= 2:
                        pe.wait_ge(keys_even, r - 1)
                        pe.wait_ge(keys_odd, r - 1)
                    for c in range(4):
                        src = kin[:, r, c, :, :] if r < NT_P else kiin[:, 4 * (r - NT_P) + c, :, :]
                        mm = pe.transpose(psT[:, r % 2, c * P:(c + 1) * P], src.rearrange("p r d -> p (r d)"), ident[:, :])
                    mm.then_inc(keys_turned, 1)
                pe.wait_ge(keys_even, NT_P + 2)
                pe.wait_ge(keys_odd, NT_P + 2)
                pe.wait_ge(zeros_done, 4)
                pe.wait_ge(v_in, 16)

                def turn(n):
                    pe.wait_ge(exp_done, n + 1)
                    for i in bank_of[n]:
                        _, b0, nb = banks[i]
                        if i >= 2:
                            pe.wait_ge(turned_out, i - 1)
                        for j in range(nb):
                            mm = pe.transpose(psT[:, i % 2, j * P:(j + 1) * P],
                                              lg[:, n % 3, (b0 + j) * P:(b0 + j + 1) * P], ident[:, :])
                        mm.then_inc(turned, 1)

                def values(n):
                    t, hd = n // HEADS, n % HEADS
                    pair = hd // (2 * HEADS // KVH)
                    pe.wait_ge(turned_out, bank_of[n][-1] + 1)
                    if n >= 2:
                        pe.wait_ge(o_done, n - 1)
                    for j in range(t + 1):
                        mm = pe.matmul(pv[:, n % 2, 0:P], probs_T[:, n % 2, j * P:(j + 1) * P],
                                       vin[:, j, pair * P:(pair + 1) * P], start=(j == 0), stop=(j == t))
                    mm.then_inc(pv_done, 1)

                for kind, t, x, no, s in plan:
                    L = (t + 1) * P
                    wait_slot(pe, s)
                    if kind == "index":
                        if x == 0:
                            pe.wait_ge(qi_in[t % 2], 16 * ((t - T0) // 2 + 1))
                        lhs, rhs = qi[:, t % 2, x // 2, :], kiT[x % 2]
                    else:
                        if x == 0:
                            pe.wait_ge(q_in[t % 2], 16 * (t // 2 + 1))
                        lhs, rhs = q[:, t % 2, x // 2, :], kT[x % 2][:, x // (HEADS // KVH), :]
                    for c in range(0, L, 512):
                        n = min(512, L - c)
                        mm = pe.matmul(slot[:, s % 2, c:c + n], lhs, rhs[:, c:c + n], start=True, stop=True)
                    mm.then_inc(qi_done if kind == "index" else qk_done, 1)
                    if kind == "head":
                        if no >= 1:
                            turn(no - 1)
                        if no >= 2:
                            values(no - 2)
                turn(N - 1)
                values(N - 2)
                values(N - 1)

            @block.scalar
            def _(act):
                for r in range(NT_P + 2):
                    act.wait_ge(keys_turned, r + 1)
                    src = psT[0:HD, r % 2, :].rearrange("p (c n) -> p c n", c=4)
                    if r < NT_P:
                        act.activation(kT[0][0:HD, :, r * P:(r + 1) * P], src, ACT.Copy).then_inc(keys_even, 1)
                    else:
                        act.activation(kiT[0][0:HD, (r - NT_P) * 512:(r - NT_P + 1) * 512], psT[0:HD, r % 2, :], ACT.Copy)\
                            .then_inc(keys_even, 1)

                def turn_out(n):
                    for i in bank_of[n]:
                        _, b0, nb = banks[i]
                        act.wait_ge(turned, i + 1)
                        if n >= 2:
                            act.wait_ge(pv_done, n - 1)
                        act.activation(probs_T[:, n % 2, b0 * P:(b0 + nb) * P], psT[:, i % 2, 0:nb * P], ACT.Copy)\
                            .then_inc(turned_out, 1)

                for kind, t, x, no, s in plan:
                    L = (t + 1) * P
                    if kind == "index":
                        act.wait_ge(qi_done, no + 1)
                        if no >= 2:
                            act.wait_ge(scored, no - 1)
                        act.activation(rl[:, no % 2, 0:L], slot[:, s % 2, 0:L], ACT.Relu, scale=ID ** -0.5)\
                            .then_inc(relu_done, 1)
                    else:
                        act.wait_ge(neg_done, no + 1)
                        if no >= 4:
                            act.wait_ge(rden_done, no - 3)
                        act.activation(lg[:, no % 3, 0:L], lg[:, no % 3, 0:L], ACT.Exp, bias=nm[:, no % 4:no % 4 + 1],
                                       scale=HD ** -0.5, accum_out=den[:, no % 4:no % 4 + 1]).then_inc(exp_done, 1)
                        if no >= 1:
                            turn_out(no - 1)
                turn_out(N - 1)

            @block.vector
            def _(dve):
                dve.wait_ge(w_in, 16)
                dve.tensor_scalar(w[:, :, :], w_raw[:, :, :], IH ** -0.5, None, ALU.mult).then_inc(w_done, 1)
                for r in range(NT_P + 2):
                    dve.wait_ge(keys_turned, r + 1)
                    dve.wait_ge(keys_even, r + 1)
                    src = psT[HD:P, r % 2, :].rearrange("p (c n) -> p c n", c=4)
                    if r < NT_P:
                        dve.tensor_copy(kT[1][HD:P, :, r * P:(r + 1) * P], src).then_inc(keys_odd, 1)
                    else:
                        dve.tensor_copy(kiT[1][HD:P, (r - NT_P) * 512:(r - NT_P + 1) * 512], psT[HD:P, r % 2, :])\
                            .then_inc(keys_odd, 1)
                n_bias = 0
                for t in range(T0):
                    L = (t + 1) * P
                    dve.memset(score[:, t, 0:L], 0.0).then_inc(filled, 1)
                    n_bias += 1
                    dve.wait_ge(filled, n_bias)
                    dve.memset(score[0:CHUNK, t, L - CHUNK:L], NEG).then_inc(filled, 1)
                    n_bias += 1
                dve.wait_ge(w_done, 1)
                done = dict(filled=n_bias, rounds=0)

                def index(t, ih, no, L):
                    dve.wait_ge(relu_done, no + 1)
                    sc = score[:, t % 4, 0:L]
                    if ih == 0:
                        dve.tensor_scalar(sc, rl[:, no % 2, 0:L], w[:, t, 0:1], None, ALU.mult).then_inc(scored, 1)
                    else:
                        dve.wait_ge(scored, no)
                        dve.scalar_tensor_tensor(sc, rl[:, no % 2, 0:L], w[:, t, ih:ih + 1], sc, ALU.mult, ALU.add)\
                            .then_inc(scored, 1)
                    if ih == IH - 1:
                        dve.wait_ge(scored, no + 1)
                        dve.memset(score[0:CHUNK, t % 4, L - CHUNK:L], FILL).then_inc(filled, 1)
                        done["filled"] += 1

                def round_(t):
                    r = done["rounds"]
                    sc = score[:, t % 4, 0:(t + 1) * P]
                    dve.wait_ge(filled, done["filled"])
                    if r >= 1:
                        dve.wait_ge(replaced, r)
                    dve.max(top8[:, :], sc).then_inc(top8_done, 1)
                    dve.wait_ge(top8_done, r + 1)
                    dve.match_replace(sc, top8[:, :], sc, MARK).then_inc(replaced, 1)
                    done["rounds"] += 1

                def bias(t):
                    sc = score[:, t % 4, 0:(t + 1) * P]
                    dve.wait_ge(replaced, done["rounds"])
                    dve.tensor_scalar(sc, sc, CUT, NEG, ALU.is_gt, ALU.mult).then_inc(bias_done, 1)

                def finish(n):
                    t, hd = n // HEADS, n % HEADS
                    half = (hd // (HEADS // KVH)) % 2
                    dve.wait_ge(exp_done, n + 1)
                    dve.reciprocal(rden[:, n % 4:n % 4 + 1], den[:, n % 4:n % 4 + 1]).then_inc(rden_done, 1)
                    dve.wait_ge(rden_done, n + 1)
                    dve.wait_ge(pv_done, n + 1)
                    if t >= 2 and hd == 0:
                        dve.wait_ge(o_stored[t % 2], 16 * (t // 2))
                    dve.tensor_scalar(ot[:, t % 2, hd * HD:(hd + 1) * HD], pv[:, n % 2, half * HD:(half + 1) * HD],
                                      rden[:, n % 4:n % 4 + 1], None, ALU.mult).then_inc(o_done, 1)

                for kind, t, x, no, s in plan:
                    L = (t + 1) * P
                    if kind == "index":
                        index(t, x, no, L)
                        continue
                    dve.wait_ge(qk_done, no + 1)
                    if x == 0 and t < T0:
                        dve.wait_ge(filled, 2 * T0)
                    if x == 0 and t >= T0:
                        dve.wait_ge(bias_done, t - T0 + 1)
                    if no >= 3:
                        dve.wait_ge(turned, bank_of[no - 3][-1] + 1)
                    m = mx[:, no % 4:no % 4 + 1]
                    dve.tensor_tensor_reduce(lg[:, no % 3, 0:L], slot[:, s % 2, 0:L], score[:, t % 4, 0:L], 1.0, FILL,
                                             ALU.add, ALU.max, m).then_inc(masked, 1)
                    dve.wait_ge(masked, no + 1)
                    dve.tensor_scalar(nm[:, no % 4:no % 4 + 1], m, -HD ** -0.5, None, ALU.mult).then_inc(neg_done, 1)
                    if t + T0 < NT_P:
                        for _ in range(ROUNDS // HEADS):
                            round_(t + T0)
                        if x == HEADS - 1:
                            bias(t + T0)
                    if no >= 2:
                        finish(no - 2)
                finish(N - 2)
                finish(N - 1)


def sample_attention_phase(nc, name, ident, qT, qiT, wt, cache_k, cache_v, cache_ki, k_new, v_new, ki_new,
                           same_frame, o):
    L = PAST + DEC_T
    PB = PAST // P
    PAIRS = KVH // 2
    N = DEC_B * PAIRS
    with Block(nc, name) as b:
        frame_of, rows_of = b.sb("frame_of", [P, DEC_B, P]), b.sb("rows_of", [P, DEC_B, P])
        qi = b.sb("qi", [ID, DEC_B, IH, DEC_T])
        q = b.sb("q", [P, PAIRS, DEC_B, P])
        w_raw, w = b.sb("w_raw", [P, DEC_B]), b.sb("w", [P, DEC_B])
        cki = b.sb("cki", [P, DEC_B, PB, ID])
        nki, nk = b.sb("nki", [P, ID]), b.sb("nk", [P, KVH * HD])
        ck, cv = b.sb("ck", [P, DEC_B, PB, KVH * HD]), b.sb("cv", [P, DEC_B, PB, KVH * HD])
        nv = b.sb("nv", [DEC_T, DEC_B, KVH * HD])
        nkiT, nkT = b.sb("nkiT", [ID, P]), b.sb("nkT", [P, PAIRS, P])
        ckiT, ckT = b.sb("ckiT", [ID, 2, PAST]), b.sb("ckT", [P, 2, PAST])
        rl, sel = b.sb("relu", [P, 2, L]), b.sb("sel", [P, 2, P])
        PAD = (-TOPK_S) % 8
        score = b.sb("score", [P, L + PAD])
        top8 = b.sb("top8", [P, 8])
        probs = b.sb("probs", [P, 3, L])
        probs_T, probs_Tn = b.sb("probs_T", [P, 2, PAST]), b.sb("probs_Tn", [DEC_T, 2, P])
        mx, nm = b.sb("max", [P, 4]), b.sb("neg_max", [P, 4])
        den, rden = b.sb("den", [P, 4]), b.sb("rden", [P, 4])
        og = b.sb("o_group", [P, 4, P])
        slot = b.ps("slot", [P, 2, 1024])
        psT = b.ps("psT", [P, 2, 512])
        psN, pv = b.ps("psN", [P, 512]), b.ps("pv", [P, 512])
        idx_in, att_in = b.sem("idx_in"), b.sem("att_in")
        q_zero, w_done = b.sem("q_zero"), b.sem("w_done")
        turned, turned_out = b.sem("turned"), b.sem("turned_out")
        qi_done, relu_done, sel_done, summed = b.sem("qi_done"), b.sem("relu_done"), b.sem("sel_done"), b.sem("summed")
        score_out, pad_done = b.sem("score_out"), b.sem("pad_done")
        top8_done, replaced, bias_done = b.sem("top8_done"), b.sem("replaced"), b.sem("bias_done")
        kT_turned, kT_out = b.sem("kT_turned"), b.sem("kT_out")
        qk_done, neg_done, max_done, exp_done = b.sem("qk_done"), b.sem("neg_done"), b.sem("max_done"), b.sem("exp_done")
        p_turned, p_out, pn_out = b.sem("p_turned"), b.sem("p_out"), b.sem("pn_out")
        pv_done, rden_done, o_done = b.sem("pv_done"), b.sem("rden_done"), b.sem("o_done")
        stored = [b.sem(f"stored{i}") for i in range(4)]
        idx_loads, att_loads = [], []

        with nc.Block() as block:
            @block.sync
            def _(sp):
                def load(group, dst, src, **how):
                    sp.dma_start(dst, src, **how).then_inc(idx_in if group is idx_loads else att_in, 16)
                    group.append(dst)

                for s in range(DEC_B):
                    load(idx_loads, cki[:, s, :, :], cache_ki[s].rearrange("(k p) d -> p k d", p=P))
                load(idx_loads, nki[:, :], ki_new)
                for hh in range(IH):
                    load(idx_loads, qi[:, :, hh, :],
                         qiT[hh * ID:(hh + 1) * ID, SEQ:TOK].rearrange("d (b t) -> d b t", t=DEC_T))
                    load(idx_loads, w_raw[hh * DEC_T:(hh + 1) * DEC_T, :],
                         wt[SEQ:TOK, hh:hh + 1].rearrange("(b t) a -> t (b a)", t=DEC_T),
                         allow_slow_non_contiguous=True)
                load(idx_loads, frame_of[:, :, :], same_frame[0])
                load(idx_loads, rows_of[:, :, :], same_frame[1])
                sp.wait_ge(q_zero, 1)
                for v in range(KVH):
                    for g in range(HEADS // KVH):
                        r0 = (v * (HEADS // KVH) + g) * HD
                        c0 = (v % 2) * HD + g * DEC_T
                        load(att_loads, q[(v % 2) * HD:(v % 2 + 1) * HD, v // 2, :, c0:c0 + DEC_T],
                             qT[r0:r0 + HD, SEQ:TOK].rearrange("d (b t) -> d b t", t=DEC_T))
                load(att_loads, nk[:, :], k_new)
                load(att_loads, nv[:, :, :], v_new.rearrange("(b t) c -> t b c", t=DEC_T))
                for s in range(DEC_B):
                    load(att_loads, ck[:, s, :, :], cache_k[s].rearrange("(k p) c -> p k c", p=P))
                    load(att_loads, cv[:, s, :, :], cache_v[s].rearrange("(k p) c -> p k c", p=P))
                for n in range(N):
                    s, pair = n // PAIRS, n % PAIRS
                    sp.wait_ge(o_done, 2 * (n + 1))
                    for r in range(2):
                        v = 2 * pair + r
                        rows = o[SEQ + s * DEC_T:SEQ + (s + 1) * DEC_T, v * 4 * HD:(v + 1) * 4 * HD]
                        for g in range(HEADS // KVH):
                            sp.dma_start(rows[:, g * HD:(g + 1) * HD],
                                         og[r * HD + g * DEC_T:r * HD + (g + 1) * DEC_T, n % 4, r * HD:(r + 1) * HD])\
                                .then_inc(stored[n % 4], 16)
                for i in range(4):
                    sp.wait_ge(stored[i], 16 * 8 * N // 4)

            @block.gpsimd
            def _(pool):
                pool.memset(q[:, :, :, :], 0.0).then_inc(q_zero, 1)
                pool.memset(score[:, L:L + PAD], -FILL).then_inc(pad_done, 1)

            IDX, ATT = 16 * (3 + DEC_B + 2 * IH), 16 * (HEADS + 2 + 2 * DEC_B)

            @block.tensor
            def _(pe):
                pe.wait_ge(idx_in, IDX)
                pe.transpose(psN[0:ID, 0:P], nki[:, :], ident[:, :]).then_inc(turned, 1)

                def turn_ki(s):
                    if s >= 2:
                        pe.wait_ge(turned_out, s)
                    for k in range(PB):
                        mm = pe.transpose(psT[0:ID, s % 2, k * P:(k + 1) * P], cki[:, s, k, :], ident[:, :])
                    mm.then_inc(turned, 1)

                def add_scores(s):
                    pe.wait_ge(sel_done, s + 1)
                    pe.wait_ge(relu_done, s + 1)
                    pe.matmul(slot[:, 1, 0:PAST], sel[:, s % 2, :], rl[:, s % 2, 0:PAST],
                              start=(s == 0), stop=(s == DEC_B - 1))
                    pe.matmul(slot[:, 1, PAST:L], sel[:, s % 2, :], rl[:, s % 2, PAST:L],
                              start=(s == 0), stop=(s == DEC_B - 1)).then_inc(summed, 1)

                turn_ki(0)
                for s in range(DEC_B):
                    if s + 1 < DEC_B:
                        turn_ki(s + 1)
                    pe.wait_ge(turned_out, s + 2)
                    if s >= 1:
                        pe.wait_ge(relu_done, s)
                    lhs = qi[:, s, :, :].rearrange("d h t -> d (h t)")
                    pe.matmul(slot[:, 0, 0:PAST], lhs, ckiT[:, s % 2, :], start=True, stop=True)
                    pe.matmul(slot[:, 0, PAST:L], lhs, nkiT[:, s * DEC_T:(s + 1) * DEC_T], start=True, stop=True)\
                        .then_inc(qi_done, 1)
                    if s >= 1:
                        add_scores(s - 1)
                add_scores(DEC_B - 1)

                pe.wait_ge(att_in, ATT)
                pe.wait_ge(turned_out, DEC_B + 1)
                for pair in range(PAIRS):
                    mm = pe.transpose(psN[:, pair * P:(pair + 1) * P], nk[:, pair * P:(pair + 1) * P], ident[:, :])
                mm.then_inc(kT_turned, 1)

                def turn_k(n):
                    s, pair = n // PAIRS, n % PAIRS
                    if n >= 1:
                        pe.wait_ge(kT_out, n + 1)
                    for k in range(PB):
                        mm = pe.transpose(psT[:, 0, k * P:(k + 1) * P], ck[:, s, k, pair * P:(pair + 1) * P], ident[:, :])
                    mm.then_inc(kT_turned, 1)

                def logits(n):
                    s, pair = n // PAIRS, n % PAIRS
                    pe.wait_ge(kT_out, n + 2)
                    if n >= 2:
                        pe.wait_ge(exp_done, n - 1)
                    for c0, c1, rhs in ((0, PAST, ckT[:, n % 2, :]), (PAST, L, nkT[:, pair, s * DEC_T:(s + 1) * DEC_T])):
                        pe.matmul(slot[:, n % 2, c0:c1], q[:, pair, s, :], rhs, start=True, stop=False)
                        mm = pe.matmul(slot[:, n % 2, c0:c1], rows_of[:, s, :], score[:, c0:c1], start=False, stop=True)
                    mm.then_inc(qk_done, 1)

                def turn_p(n):
                    pe.wait_ge(exp_done, n + 1)
                    if n >= 1:
                        pe.wait_ge(p_out, n)
                        pe.wait_ge(pn_out, n)
                    for k in range(PB):
                        pe.transpose(psT[:, 1, k * P:(k + 1) * P], probs[:, n % 3, k * P:(k + 1) * P], ident[:, :])
                    pe.transpose(psN[0:DEC_T, 0:P], probs[:, n % 3, PAST:L], ident[:, :]).then_inc(p_turned, 1)

                def values(n):
                    s, pair = n // PAIRS, n % PAIRS
                    pe.wait_ge(p_out, n + 1)
                    pe.wait_ge(pn_out, n + 1)
                    if n >= 1:
                        pe.wait_ge(o_done, 2 * n)
                    for k in range(PB):
                        pe.matmul(pv[:, 0:P], probs_T[:, n % 2, k * P:(k + 1) * P], cv[:, s, k, pair * P:(pair + 1) * P],
                                  start=(k == 0), stop=False)
                    pe.matmul(pv[:, 0:P], probs_Tn[:, n % 2, :], nv[:, s, pair * P:(pair + 1) * P],
                              start=False, stop=True).then_inc(pv_done, 1)

                turn_k(0)
                pe.wait_ge(bias_done, 1)
                for n in range(N):
                    if n + 1 < N:
                        turn_k(n + 1)
                    logits(n)
                    if n >= 1:
                        turn_p(n - 1)
                    if n >= 2:
                        values(n - 2)
                turn_p(N - 1)
                values(N - 2)
                values(N - 1)

            @block.scalar
            def _(act):
                act.wait_ge(turned, 1)
                act.activation(nkiT[:, :], psN[0:ID, 0:P], ACT.Copy).then_inc(turned_out, 1)

                def ki_out(s):
                    act.wait_ge(turned, s + 2)
                    if s >= 2:
                        act.wait_ge(qi_done, s - 1)
                    act.activation(ckiT[:, s % 2, :], psT[0:ID, s % 2, :], ACT.Copy).then_inc(turned_out, 1)

                ki_out(0)
                for s in range(DEC_B):
                    if s + 1 < DEC_B:
                        ki_out(s + 1)
                    act.wait_ge(qi_done, s + 1)
                    if s >= 2:
                        act.wait_ge(summed, s - 1)
                    act.activation(rl[:, s % 2, :], slot[:, 0, 0:L], ACT.Relu, scale=ID ** -0.5).then_inc(relu_done, 1)
                act.wait_ge(kT_turned, 1)
                act.activation(nkT[:, :, :], psN[:, 0:PAIRS * P].rearrange("p (a n) -> p a n", n=P), ACT.Copy)\
                    .then_inc(kT_out, 1)

                def k_out(n):
                    act.wait_ge(kT_turned, n + 2)
                    if n >= 2:
                        act.wait_ge(qk_done, n - 1)
                    act.activation(ckT[:, n % 2, :], psT[:, 0, :], ACT.Copy).then_inc(kT_out, 1)

                def turn_out(n):
                    act.wait_ge(p_turned, n + 1)
                    if n >= 2:
                        act.wait_ge(pv_done, n - 1)
                    act.activation(probs_T[:, n % 2, :], psT[:, 1, :], ACT.Copy).then_inc(p_out, 1)

                k_out(0)
                for n in range(N):
                    if n + 1 < N:
                        k_out(n + 1)
                    act.wait_ge(neg_done, n + 1)
                    if n >= 3:
                        act.wait_ge(p_turned, n - 2)
                    if n >= 4:
                        act.wait_ge(rden_done, n - 3)
                    act.activation(probs[:, n % 3, :], slot[:, n % 2, 0:L], ACT.Exp, bias=nm[:, n % 4:n % 4 + 1],
                                   scale=HD ** -0.5, accum_out=den[:, n % 4:n % 4 + 1]).then_inc(exp_done, 1)
                    if n >= 1:
                        turn_out(n - 1)
                turn_out(N - 1)

            @block.vector
            def _(dve):
                dve.wait_ge(idx_in, IDX)
                dve.tensor_scalar(w[:, :], w_raw[:, :], IH ** -0.5, None, ALU.mult).then_inc(w_done, 1)
                dve.wait_ge(w_done, 1)
                for s in range(DEC_B):
                    if s >= 2:
                        dve.wait_ge(summed, s - 1)
                    dve.tensor_scalar(sel[:, s % 2, :], frame_of[:, s, :], w[:, s:s + 1], None, ALU.mult)\
                        .then_inc(sel_done, 1)
                dve.wait_ge(summed, DEC_B)
                dve.tensor_copy(score[:, 0:L], slot[:, 1, 0:L]).then_inc(score_out, 1)
                dve.wait_ge(score_out, 1)
                dve.wait_ge(pad_done, 1)
                for r in range((TOPK_S + PAD) // 8):
                    if r >= 1:
                        dve.wait_ge(replaced, r)
                    dve.max(top8[:, :], score[:, :]).then_inc(top8_done, 1)
                    dve.wait_ge(top8_done, r + 1)
                    dve.match_replace(score[:, :], top8[:, :], score[:, :], MARK).then_inc(replaced, 1)
                dve.wait_ge(replaced, (TOPK_S + PAD) // 8)
                dve.tensor_scalar(score[:, 0:L], score[:, 0:L], CUT, NEG, ALU.is_gt, ALU.mult).then_inc(bias_done, 1)

                def finish(n):
                    dve.wait_ge(exp_done, n + 1)
                    dve.reciprocal(rden[:, n % 4:n % 4 + 1], den[:, n % 4:n % 4 + 1]).then_inc(rden_done, 1)
                    dve.wait_ge(rden_done, n + 1)
                    dve.wait_ge(pv_done, n + 1)
                    if n >= 4:
                        dve.wait_ge(stored[n % 4], 16 * 8 * (n // 4))
                    for r in range(2):
                        rows, cols = slice(r * HD, (r + 1) * HD), slice(r * HD, (r + 1) * HD)
                        dve.tensor_scalar(og[rows, n % 4, cols], pv[rows, cols], rden[rows, n % 4:n % 4 + 1], None,
                                          ALU.mult).then_inc(o_done, 1)

                for n in range(N):
                    m = mx[:, n % 4:n % 4 + 1]
                    dve.wait_ge(qk_done, n + 1)
                    dve.tensor_reduce(m, slot[:, n % 2, 0:L], AX.X, ALU.max).then_inc(max_done, 1)
                    dve.wait_ge(max_done, n + 1)
                    dve.tensor_scalar(nm[:, n % 4:n % 4 + 1], m, -HD ** -0.5, None, ALU.mult).then_inc(neg_done, 1)
                    if n >= 1:
                        dve.wait_ge(p_turned, n)
                        if n >= 3:
                            dve.wait_ge(pv_done, n - 2)
                        dve.tensor_copy(probs_Tn[:, (n - 1) % 2, :], psN[0:DEC_T, 0:P]).then_inc(pn_out, 1)
                    if n >= 2:
                        finish(n - 2)
                dve.wait_ge(p_turned, N)
                dve.wait_ge(pv_done, N - 2)
                dve.tensor_copy(probs_Tn[:, (N - 1) % 2, :], psN[0:DEC_T, 0:P]).then_inc(pn_out, 1)
                finish(N - 2)
                finish(N - 1)


def same_frame_table():
    m = np.zeros((2, P, DEC_B, P), np.float32)
    for s in range(DEC_B):
        for x in range(P // DEC_T):
            for f in range(DEC_T):
                m[0, x * DEC_T + f, s, s * DEC_T + f] = 1.0
                m[1, s * DEC_T + f, s, x * DEC_T + f] = 1.0
    return m


def gla_phase(nc, name, ident, qT, kT, aT, v, sg, w_a2, b_a, b_norm, state, masks, starts, stream_of,
              o, prompt_state, sample_state):
    HW = GH * P
    NL = len(LEVELS)
    with Block(nc, name) as b:
        mask = b.sb("mask", [P, NL + 1, P])
        start = b.sb("start", [P, 2, HW])
        rows = b.sb("rows", [P, DEC_B])
        wa = b.sb("wa", [RANK + 1, HW])
        bn = b.sb("bn", [P, DV])
        q, k = b.sb("q", [P, 2, GH, P]), b.sb("k", [P, 2, GH, P])
        a = b.sb("a", [RANK + 1, 2, P])
        vt, sgt = b.sb("v", [P, 2, D]), b.sb("sg", [P, 2, D])
        az, ez, lz = b.sb("az", [P, HW]), b.sb("ez", [P, HW]), b.sb("lz", [P, HW])
        la, bcum = b.sb("la", [P, 2, HW]), b.sb("b", [P, 2, HW])
        dist, dec = b.sb("dist", [P, 2, HW]), b.sb("dec", [P, 2, HW])
        X = b.sb("X", [P, 2, HW])
        A = b.sb("A", [P, 2, HW])
        d_end, e_end, e_b = b.sb("d_end", [P, HW]), b.sb("e_end", [P, HW]), b.sb("e_b", [P, 2, HW])
        qe, kd = b.sb("qe", [P, HW]), b.sb("kd", [P, HW])
        kdT = b.sb("kdT", [P, HW])
        S = b.sb("S", [P, GH, DV])
        S_in = b.sb("S_in", [P, DEC_B, GH, DV])
        qe_s = b.sb("qe_s", [P, DEC_B, GH, P])
        kd_s = b.sb("kd_s", [P, 2, HW])
        junk, ss, ms, rstd = b.sb("junk", [P, DV]), b.sb("ss", [P, 2, GH]), b.sb("ms", [P, 2, GH]), b.sb("rstd", [P, 2, GH])
        mhalf = b.sb("mhalf", [P, GH])
        on, og = b.sb("on", [P, 2, D]), b.sb("og", [P, 2, D])
        G = b.ps("G", [P, 2, 512])
        zp, tp = b.ps("z", [P, 512]), b.ps("tp", [P, 512])
        op, dS = b.ps("o", [P, GH, DV]), b.ps("dS", [P, GH, DV])
        const_in, wa_in, sin_in = b.sem("const_in"), b.sem("wa_in"), b.sem("sin_in")
        in_a, in_qk = [b.sem("in_a0"), b.sem("in_a1")], [b.sem("in_qk0"), b.sem("in_qk1")]
        in_v, in_sg = [b.sem("in_v0"), b.sem("in_v1")], [b.sem("in_sg0"), b.sem("in_sg1")]
        ones_done, mhalf_done, qs_zero = b.sem("ones_done"), b.sem("mhalf_done"), b.sem("qs_zero")
        z_done, abs_done, ez_done, lz_done = b.sem("z_done"), b.sem("abs_done"), b.sem("ez_done"), b.sem("lz_done")
        la_done, b_done = b.sem("la_done"), b.sem("b_done")
        eb_done = b.sem("eb_done")
        dist_done, dec_done, x_done, g_done, g_out = (b.sem("dist_done"), b.sem("dec_done"), b.sem("x_done"),
                                                      b.sem("g_done"), b.sem("g_out"))
        dend_done, eend_done, qe_done, kd_done = b.sem("dend_done"), b.sem("eend_done"), b.sem("qe_done"), b.sem("kd_done")
        kd_turned, kdT_done = b.sem("kd_turned"), b.sem("kdT_done")
        o_done, dS_done, S_done = b.sem("o_done"), b.sem("dS_done"), b.sem("S_done")
        ss_done, ms_done, rstd_done, on_done, og_done = (b.sem("ss_done"), b.sem("ms_done"), b.sem("rstd_done"),
                                                         b.sem("on_done"), b.sem("og_done"))
        qs_done, kds_done = b.sem("qs_done"), b.sem("kds_done")
        o_stored = [b.sem("o_stored0"), b.sem("o_stored1")]
        s_stored = b.sem("s_stored")

        def levels_of(t):
            return [i for i, w in enumerate(LEVELS) if t < NT_P or 2 * w <= DEC_T]

        lev_no, diag_no, n = {}, {}, 0
        for t in range(NT):
            for i in levels_of(t):
                lev_no[t, i] = n
                n += 1
        g_no, m = {}, 0
        for t in range(NT):
            for i in [NL] + levels_of(t):
                g_no[t, i] = m
                m += 1
        first_lev = {t: lev_no[t, levels_of(t)[0]] for t in range(NT)}
        last_lev = {t: lev_no[t, levels_of(t)[-1]] for t in range(NT)}
        last_g = {t: g_no[t, levels_of(t)[-1]] for t in range(NT)}
        lev_tile = {lev_no[t, i]: t for t, i in lev_no}

        def halves(x, w):
            return x.rearrange("p (n two w) -> p n two w", two=2, w=w)

        with nc.Block() as block:
            @block.sync
            def _(sp):
                def load(t):
                    i, cols = t % 2, slice(t * P, (t + 1) * P)
                    if t >= 2:
                        sp.wait_ge(z_done, t - 1)
                    sp.dma_start(a[0:RANK, i, :], aT[:, cols]).then_inc(in_a[i], 16)
                    if t >= 2:
                        sp.wait_ge(kd_done, t - 1)
                        sp.wait_ge(qe_done, t - 1)
                    sp.dma_start(q[:, i, :, :], qT[:, cols].rearrange("(h p) n -> p h n", p=P)).then_inc(in_qk[i], 16)
                    sp.dma_start(k[:, i, :, :], kT[:, cols].rearrange("(h p) n -> p h n", p=P)).then_inc(in_qk[i], 16)
                    if t >= 2:
                        sp.wait_ge(dS_done, t - 1)
                    sp.dma_start(vt[:, i, :], v[cols, :]).then_inc(in_v[i], 16)
                    if t >= 2:
                        sp.wait_ge(og_done, t - 1)
                    sp.dma_start(sgt[:, i, :], sg[cols, :]).then_inc(in_sg[i], 16)

                sp.dma_start(wa[0:RANK, :], w_a2).then_inc(wa_in, 16)
                sp.dma_start(wa[RANK:RANK + 1, :], b_a.rearrange("(a n) -> a n", a=1)).then_inc(wa_in, 16)
                sp.wait_ge(ones_done, 1)
                load(0)
                sp.dma_start(start[:, :, :], starts.rearrange("(a r) n -> a r n", a=1).broadcast_to([P, 2, HW])).then_inc(const_in, 16)
                sp.dma_start(mask[:, :, :], masks.rearrange("l s t -> s l t")).then_inc(const_in, 16)
                sp.dma_start(rows[:, :], stream_of).then_inc(const_in, 16)
                sp.dma_start(bn[:, :], bc(b_norm, DV)).then_inc(const_in, 16)
                load(1)
                for s in range(DEC_B):
                    sp.dma_start(S_in[:, s, :, :], state[s].rearrange("h p n -> p h n")).then_inc(sin_in, 16)
                for t in range(NT):
                    if t >= 1 and t + 1 < NT:
                        load(t + 1)
                    sp.wait_ge(og_done, t + 1)
                    sp.dma_start(o[t * P:(t + 1) * P, :], og[:, t % 2, :]).then_inc(o_stored[t % 2], 16)
                    if t == NT_P - 1:
                        sp.wait_ge(S_done, GH * NT_P)
                        sp.dma_start(prompt_state.rearrange("h p n -> p h n"), S[:, :, :]).then_inc(s_stored, 16)
                for s in range(DEC_B):
                    sp.wait_ge(S_done, GH * (NT_P + s + 1))
                    sp.dma_start(sample_state[s].rearrange("h p n -> p h n"), S_in[:, s, :, :]).then_inc(s_stored, 16)
                sp.wait_ge(o_stored[0], 16 * ((NT + 1) // 2))
                sp.wait_ge(o_stored[1], 16 * (NT // 2))
                sp.wait_ge(s_stored, 16 * (DEC_B + 1))

            @block.gpsimd
            def _(pool):
                pool.memset(a[:, :, :], 1.0).then_inc(ones_done, 1)
                pool.memset(mhalf[:, :], -0.5).then_inc(mhalf_done, 1)
                pool.memset(qe_s[:, :, :, :], 0.0).then_inc(qs_zero, 1)
                pool.wait_ge(mhalf_done, 1)

                def level(t, i):
                    n = lev_no[t, i]
                    if i == levels_of(t)[0]:
                        pool.wait_ge(in_qk[t % 2], 32 * (t // 2 + 1))
                    pool.wait_ge(dec_done, n + 1)
                    if n >= 2:
                        tt = lev_tile[n - 2]
                        li = [j for j in levels_of(tt) if lev_no[tt, j] == n - 2][0]
                        pool.wait_ge(g_done, g_no[tt, li] + 1)
                    w = LEVELS[i]
                    xs, ds = halves(X[:, n % 2, :], w), halves(dec[:, n % 2, :], w)
                    ks = halves(k[:, t % 2, :, :].rearrange("p h n -> p (h n)"), w)
                    qs = halves(q[:, t % 2, :, :].rearrange("p h n -> p (h n)"), w)
                    pool.tensor_tensor(xs[:, :, 0, :], ks[:, :, 0, :], ds[:, :, 0, :], ALU.mult).then_inc(x_done, 1)
                    pool.tensor_tensor(xs[:, :, 1, :], qs[:, :, 1, :], ds[:, :, 1, :], ALU.mult).then_inc(x_done, 1)

                def ends(t):
                    pool.wait_ge(eb_done, t + 1)
                    if t >= 1:
                        pool.wait_ge(o_done, t)
                    pool.tensor_tensor(qe[:, :], q[:, t % 2, :, :].rearrange("p h n -> p (h n)"), e_b[:, t % 2, :], ALU.mult)\
                        .then_inc(qe_done, 1)
                    pool.wait_ge(eend_done, t + 1)
                    if t >= 1:
                        pool.wait_ge(kd_turned, t)
                    pool.tensor_tensor(kd[:, :], k[:, t % 2, :, :].rearrange("p h n -> p (h n)"), e_end[:, :], ALU.mult)\
                        .then_inc(kd_done, 1)
                    if t == NT - 1:
                        pool.wait_ge(qe_done, NT)
                        pool.wait_ge(qs_zero, 1)
                        for s in range(DEC_B):
                            cols = slice(s * DEC_T, (s + 1) * DEC_T)
                            pool.tensor_copy(qe_s[:, s, :, cols], qe[:, :].rearrange("p (h n) -> p h n", h=GH)[:, :, cols])\
                                .then_inc(qs_done, 1)

                def gate(t):
                    pool.wait_ge(ss_done, GH * (t + 1))
                    pool.tensor_scalar(ms[:, t % 2, :], ss[:, t % 2, :], 1.0 / DV, EPS, ALU.mult, ALU.add).then_inc(ms_done, 1)
                    pool.wait_ge(ms_done, t + 1)
                    pool.tensor_tensor(rstd[:, t % 2, :], ms[:, t % 2, :], mhalf[:, :], ALU.pow).then_inc(rstd_done, 1)
                    pool.wait_ge(on_done, GH * (t + 1))
                    pool.wait_ge(in_sg[t % 2], 16 * (t // 2 + 1))
                    if t >= 2:
                        pool.wait_ge(o_stored[t % 2], 16 * (t // 2))
                    pool.tensor_tensor(og[:, t % 2, :], on[:, t % 2, :], sgt[:, t % 2, :], ALU.mult).then_inc(og_done, 1)

                for t in range(NT):
                    for i in levels_of(t):
                        level(t, i)
                    ends(t)
                    gate(t)

            @block.tensor
            def _(pe):
                def gates(t):
                    if t == 0:
                        pe.wait_ge(wa_in, 32)
                        pe.wait_ge(ones_done, 1)
                    pe.wait_ge(in_a[t % 2], 16 * (t // 2 + 1))
                    if t >= 1:
                        pe.wait_ge(la_done, t)
                    for hd in range(GH):
                        mm = pe.matmul(zp[:, hd * P:(hd + 1) * P], wa[:, hd * P:(hd + 1) * P], a[:, t % 2, :],
                                       start=True, stop=True)
                    mm.then_inc(z_done, 1)

                def products(t, i):
                    m = g_no[t, i]
                    if m >= 2:
                        pe.wait_ge(g_out, m - 1)
                    if i == NL:
                        pe.wait_ge(in_qk[t % 2], 32 * (t // 2 + 1))
                    else:
                        pe.wait_ge(x_done, 2 * (lev_no[t, i] + 1))
                    for hd in range(GH):
                        cols = slice(hd * P, (hd + 1) * P)
                        if i == NL:
                            lhs, rhs = k[:, t % 2, hd, :], q[:, t % 2, hd, :]
                        else:
                            lhs = rhs = X[:, lev_no[t, i] % 2, cols]
                        mm = pe.matmul(G[:, m % 2, cols], lhs, rhs, start=True, stop=True)
                    mm.then_inc(g_done, 1)

                def post(t):
                    pe.wait_ge(kd_done, t + 1)
                    if t >= 1:
                        pe.wait_ge(kdT_done, t)
                    for hd in range(GH):
                        cols = slice(hd * P, (hd + 1) * P)
                        mm = pe.transpose(tp[:, cols], kd[:, cols], ident[:, :])
                    mm.then_inc(kd_turned, 1)
                    pe.wait_ge(in_v[t % 2], 16 * (t // 2 + 1))
                    pe.wait_ge(g_out, last_g[t] + 1)
                    if t >= 1:
                        pe.wait_ge(on_done, GH * t)
                        pe.wait_ge(ss_done, GH * t)
                    if t < NT_P:
                        pe.wait_ge(qe_done, t + 1)
                        if t >= 1:
                            pe.wait_ge(S_done, GH * t)
                    else:
                        pe.wait_ge(qs_done, DEC_B)
                        pe.wait_ge(sin_in, 16 * DEC_B)
                    for hd in range(GH):
                        cols, vs = slice(hd * P, (hd + 1) * P), vt[:, t % 2, hd * DV:(hd + 1) * DV]
                        mm = pe.matmul(op[:, hd, :], A[:, t % 2, cols], vs, start=True, stop=(t == 0))
                        if 1 <= t < NT_P:
                            mm = pe.matmul(op[:, hd, :], qe[:, cols], S[:, hd, :], start=False, stop=True)
                        if t == NT_P:
                            for s in range(DEC_B):
                                mm = pe.matmul(op[:, hd, :], qe_s[:, s, hd, :], S_in[:, s, hd, :],
                                               start=False, stop=(s == DEC_B - 1))
                    mm.then_inc(o_done, 1)
                    if t < NT_P:
                        pe.wait_ge(kdT_done, t + 1)
                        for hd in range(GH):
                            mm = pe.matmul(dS[:, hd, :], kdT[:, hd * P:(hd + 1) * P], vt[:, t % 2, hd * DV:(hd + 1) * DV],
                                           start=True, stop=True)
                        mm.then_inc(dS_done, 1)
                    else:
                        for s in range(DEC_B):
                            pe.wait_ge(kds_done, s + 1)
                            pe.wait_ge(S_done, GH * (NT_P + s))
                            for hd in range(GH):
                                mm = pe.matmul(dS[:, hd, :], kd_s[:, s % 2, hd * P:(hd + 1) * P],
                                               vt[:, t % 2, hd * DV:(hd + 1) * DV], start=True, stop=True)
                            mm.then_inc(dS_done, 1)

                gates(0)
                for t in range(NT):
                    for i in [NL] + levels_of(t):
                        products(t, i)
                    if t + 1 < NT:
                        gates(t + 1)
                    post(t)

            @block.scalar
            def _(act):
                def gates(t):
                    act.wait_ge(z_done, t + 1)
                    if t >= 1:
                        act.wait_ge(ez_done, t)
                    act.activation(az[:, :], zp[:, :], ACT.Abs).then_inc(abs_done, 1)
                    act.wait_ge(abs_done, t + 1)
                    if t >= 1:
                        act.wait_ge(lz_done, t)
                    act.activation(ez[:, :], az[:, :], ACT.Exp, scale=-1.0).then_inc(ez_done, 1)
                    act.wait_ge(ez_done, t + 1)
                    if t >= 1:
                        act.wait_ge(la_done, t)
                    act.activation(lz[:, :], ez[:, :], ACT.Ln, bias=1.0).then_inc(lz_done, 1)

                def level(t, i):
                    n = lev_no[t, i]
                    act.wait_ge(dist_done, 2 * (n + 1))
                    if n >= 2:
                        act.wait_ge(x_done, 2 * (n - 1))
                    act.activation(dec[:, n % 2, :], dist[:, n % 2, :], ACT.Exp, scale=1.0 / TAU).then_inc(dec_done, 1)

                def whole(t):
                    act.wait_ge(b_done, t + 1)
                    if t >= 2:
                        act.wait_ge(S_done, GH * (t - 1))
                        act.wait_ge(qe_done, t - 1)
                    act.activation(e_b[:, t % 2, :], bcum[:, t % 2, :], ACT.Exp, scale=1.0 / TAU).then_inc(eb_done, 1)
                    act.wait_ge(dend_done, t + 1)
                    if t >= 1:
                        act.wait_ge(kd_done, t)
                    act.activation(e_end[:, :], d_end[:, :], ACT.Exp, scale=1.0 / TAU).then_inc(eend_done, 1)

                def post(t):
                    act.wait_ge(kd_turned, t + 1)
                    if t >= 1:
                        act.wait_ge(dS_done, t)
                    act.activation(kdT[:, :], tp[:, :], ACT.Copy).then_inc(kdT_done, 1)
                    act.wait_ge(o_done, t + 1)
                    if t >= 2:
                        act.wait_ge(rstd_done, t - 1)
                    for hd in range(GH):
                        n = GH * t + hd
                        if n >= 1:
                            act.wait_ge(ss_done, n)
                        act.activation(junk[:, :], op[:, hd, :], ACT.Square, accum_out=ss[:, t % 2, hd:hd + 1])\
                            .then_inc(ss_done, 1)

                gates(0)
                for t in range(NT):
                    for i in levels_of(t):
                        level(t, i)
                    whole(t)
                    if t + 1 < NT:
                        gates(t + 1)
                    post(t)

            @block.vector
            def _(dve):
                dve.wait_ge(const_in, 16 * 4)

                def gates(t):
                    i = t % 2
                    dve.wait_ge(lz_done, t + 1)
                    dve.scalar_tensor_tensor(la[:, i, :], zp[:, :], 0.0, lz[:, :], ALU.min, ALU.subtract).then_inc(la_done, 1)
                    dve.wait_ge(la_done, t + 1)
                    if t >= 2:
                        dve.wait_ge(eb_done, t - 1)
                    dve.tensor_tensor_scan(bcum[:, i, :], start[:, int(t == NT_P), :], la[:, i, :], 0.0, ALU.mult, ALU.add)\
                        .then_inc(b_done, 1)

                def dists(t, i):
                    n, w = lev_no[t, i], LEVELS[i]
                    if n >= 2:
                        dve.wait_ge(dec_done, n - 1)
                    bs, ds = halves(bcum[:, t % 2, :], w), halves(dist[:, n % 2, :], w)
                    ref = bs[:, :, 0, w - 1:w].broadcast_to([P, HW // (2 * w), w])
                    dve.tensor_tensor(ds[:, :, 0, :], ref, bs[:, :, 0, :], ALU.subtract).then_inc(dist_done, 1)
                    dve.tensor_tensor(ds[:, :, 1, :], bs[:, :, 1, :], ref, ALU.subtract).then_inc(dist_done, 1)

                def gather(t, i):
                    m = g_no[t, i]
                    dve.wait_ge(g_done, m + 1)
                    mk = mask[:, i, :].unsqueeze(1).broadcast_to([P, GH, P])
                    g, dst = G[:, m % 2, :].rearrange("p (h n) -> p h n", h=GH), A[:, t % 2, :].rearrange("p (h n) -> p h n", h=GH)
                    if i == NL:
                        if t >= 2:
                            dve.wait_ge(o_done, t - 1)
                        dve.tensor_tensor(dst, g, mk, ALU.mult).then_inc(g_out, 1)
                    else:
                        dve.wait_ge(g_out, m)
                        dve.copy_predicated(dst, mk.bitcast(U32), g).then_inc(g_out, 1)

                def to_end(t):
                    if t >= 1:
                        dve.wait_ge(eend_done, t)
                    w = P if t < NT_P else DEC_T
                    bs = bcum[:, t % 2, :].rearrange("p (n w) -> p n w", w=w)
                    ref = bs[:, :, w - 1:w].broadcast_to([P, HW // w, w])
                    dve.tensor_tensor(d_end[:, :].rearrange("p (n w) -> p n w", w=w), ref, bs, ALU.subtract)\
                        .then_inc(dend_done, 1)

                def post(t):
                    dve.wait_ge(rstd_done, t + 1)
                    if t >= 2:
                        dve.wait_ge(og_done, t - 1)
                    for hd in range(GH):
                        dve.scalar_tensor_tensor(on[:, t % 2, hd * DV:(hd + 1) * DV], op[:, hd, :], rstd[:, t % 2, hd:hd + 1],
                                                 bn[:, :], ALU.mult, ALU.mult).then_inc(on_done, 1)

                def states(t):
                    if t < NT_P:
                        dve.wait_ge(dS_done, t + 1)
                        for hd in range(GH):
                            end = e_b[:, t % 2, hd * P + P - 1:hd * P + P]
                            if t == 0:
                                dve.tensor_copy(S[:, hd, :], dS[:, hd, :]).then_inc(S_done, 1)
                            else:
                                dve.scalar_tensor_tensor(S[:, hd, :], S[:, hd, :], end, dS[:, hd, :], ALU.mult, ALU.add)\
                                    .then_inc(S_done, 1)
                        return
                    dve.wait_ge(kdT_done, NT)
                    dve.wait_ge(eb_done, NT)

                    def rows_of(s):
                        if s >= 2:
                            dve.wait_ge(dS_done, NT_P + s - 1)
                        dve.tensor_scalar(kd_s[:, s % 2, :], kdT[:, :], rows[:, s:s + 1], None, ALU.mult).then_inc(kds_done, 1)

                    rows_of(0)
                    for s in range(DEC_B):
                        if s + 1 < DEC_B:
                            rows_of(s + 1)
                        dve.wait_ge(dS_done, NT_P + s + 1)
                        for hd in range(GH):
                            c = hd * P + (s + 1) * DEC_T - 1
                            dve.scalar_tensor_tensor(S_in[:, s, hd, :], S_in[:, s, hd, :], e_b[:, t % 2, c:c + 1],
                                                     dS[:, hd, :], ALU.mult, ALU.add).then_inc(S_done, 1)

                gates(0)
                dve.wait_ge(b_done, 1)
                for t in range(NT):
                    ls = levels_of(t)
                    dists(t, ls[0])
                    gather(t, NL)
                    for x, i in enumerate(ls):
                        if x + 1 < len(ls):
                            dists(t, ls[x + 1])
                        else:
                            to_end(t)
                        gather(t, i)
                    if t + 1 < NT:
                        gates(t + 1)
                        dve.wait_ge(b_done, t + 2)
                    states(t)
                    post(t)


def level_masks():
    s, t = np.arange(P)[:, None], np.arange(P)[None, :]
    ms = [(s // (2 * w) == t // (2 * w)) & (s % (2 * w) < w) & (t % (2 * w) >= w) for w in LEVELS]
    return np.stack(ms + [s == t]).astype(np.float32)


def scan_starts():
    c = np.arange(GH * P)
    return np.stack([c % P != 0, c % DEC_T != 0]).astype(np.float32)


def stream_rows():
    return (np.arange(P)[:, None] // DEC_T == np.arange(DEC_B)[None, :]).astype(np.float32)


def final_phase(nc, name, h, gamma, y):
    with Block(nc, name) as b:
        junk, g = b.sb("junk", [P, D]), b.sb("gamma", [P, D])
        ss, ms, rstd, mhalf = b.sb("ss", [P, NT]), b.sb("ms", [P, NT]), b.sb("rstd", [P, NT]), b.sb("mhalf", [P, 1])
        out = b.sb("out", [P, 3, D])
        gamma_in, ss_done, mhalf_done = b.sem("gamma_in"), b.sem("ss_done"), b.sem("mhalf_done")
        ms_done, rstd_done, out_done = b.sem("ms_done"), b.sem("rstd_done"), b.sem("out_done")
        stored = [b.sem(f"stored{i}") for i in range(3)]
        with nc.Block() as block:
            @block.sync
            def _(sp):
                sp.dma_start(g[:, :], bc(gamma, D)).then_inc(gamma_in, 16)
                for t in range(NT):
                    sp.wait_ge(out_done, t + 1)
                    sp.dma_start(y(t), out[:, t % 3, :]).then_inc(stored[t % 3], 16)
                for i in range(3):
                    sp.wait_ge(stored[i], 16 * NT // 3)

            @block.scalar
            def _(act):
                for t in range(NT):
                    if t >= 1:
                        act.wait_ge(ss_done, t)
                    act.activation(junk[:, :], h[:, t, :], ACT.Square, accum_out=ss[:, t:t + 1]).then_inc(ss_done, 1)

            @block.gpsimd
            def _(pool):
                pool.memset(mhalf[:, :], -0.5).then_inc(mhalf_done, 1)
                pool.wait_ge(mhalf_done, 1)
                for t in range(NT):
                    pool.wait_ge(ss_done, t + 1)
                    pool.tensor_scalar(ms[:, t:t + 1], ss[:, t:t + 1], 1.0 / D, EPS, ALU.mult, ALU.add).then_inc(ms_done, 1)
                    pool.wait_ge(ms_done, t + 1)
                    pool.tensor_tensor(rstd[:, t:t + 1], ms[:, t:t + 1], mhalf[:, :], ALU.pow).then_inc(rstd_done, 1)

            @block.vector
            def _(dve):
                dve.wait_ge(gamma_in, 16)
                for t in range(NT):
                    dve.wait_ge(rstd_done, t + 1)
                    if t >= 3:
                        dve.wait_ge(stored[t % 3], 16 * (t // 3))
                    dve.scalar_tensor_tensor(out[:, t % 3, :], h[:, t, :], rstd[:, t:t + 1], g[:, :], ALU.mult, ALU.mult)\
                        .then_inc(out_done, 1)


def encoder(nc, x_prompt, x_sample, cache_k, cache_v, cache_kidx, state_gla, norm_mix, norm_ffn, norm_final,
            a_w_in, a_w_o, b_w_in, b_w_a2, b_b_a, b_norm, b_w_o, ffn_w_up, ffn_w_down,
            ident_table, same_frame, masks, starts, stream_of,
            y_prompt, y_sample, k_prompt, v_prompt, kidx_prompt, gla_prompt,
            k_sample, v_sample, kidx_sample, gla_sample):
    xp, xs = x_prompt[0], x_sample.rearrange("b t d -> (b t) d")
    yp, ys = y_prompt[0], y_sample.rearrange("b t d -> (b t) d")

    def flat(ap, pattern):
        return ap.rearrange(pattern)

    k_p, v_p = (flat(z[0, 0], "s h d -> s (h d)") for z in (k_prompt, v_prompt))
    k_s, v_s = (flat(z[0], "b t h d -> (b t) (h d)") for z in (k_sample, v_sample))
    ki_p, ki_s = kidx_prompt[0, 0], flat(kidx_sample[0], "b t d -> (b t) d")
    c_k, c_v = (flat(z[0], "b s h d -> b s (h d)") for z in (cache_k, cache_v))
    def dram(name, rows, cols):
        return nc.dram_tensor(name, (rows, cols), F32, kind="Internal").ap()

    qT, qiT, wt, o = dram("qT", D, TOK), dram("qiT", IH * ID, TOK), dram("wt", TOK, IH), dram("o", TOK, D)
    gq, gk, ga = dram("gq", GH * DK, TOK), dram("gk", GH * DK, TOK), dram("ga", RANK, TOK)
    gv, gs, go = dram("gv", TOK, D), dram("gs", TOK, D), dram("go", TOK, D)

    def either(p, s):
        return lambda t: p[t * P:(t + 1) * P, :] if t < NT_P else s[:, :]

    def to_T(dst, r0, cols=CW):
        return lambda u: [(dst[r0 + u["j"]:r0 + u["j"] + u["m"], u["g"] * GW:(u["g"] + 1) * GW],
                           lambda s, m=u["m"]: s[0:m, :])]

    def to_N(tile, c0=0, n=CW, s0=0):
        return lambda u: [(tile(u["t"])[:, c0:c0 + n], lambda s: s[:, s0:s0 + n])]

    def both(f, g):
        return lambda u: f(u) + g(u)

    def chunk(w, c0, n, form, op, out):
        return dict(w=w[:, c0:c0 + n], form=form, op=op, out=out)

    with ExitStack() as ctx:
        ident = ctx.enter_context(nc.sbuf_tensor("ident", [P, P], F32))
        ident_in = ctx.enter_context(nc.semaphore("ident_in"))
        with nc.Block() as block:
            @block.sync
            def _(sp):
                sp.dma_start(ident[:, :], ident_table).then_inc(ident_in, 16)
                sp.wait_ge(ident_in, 16)

        QW, KW, IW = HEADS * HD, KVH * HD, IH * ID
        w0 = a_w_in[0]
        tail = A_IN - CW
        tile_of = lambda d: (lambda t: d[t * P:(t + 1) * P, :])
        chunks = [chunk(w0, tail, CW, "N", "copy",
                        both(to_N(either(ki_p, ki_s), 0, ID, CW - IH - ID), to_N(tile_of(wt), 0, IH, CW - IH)))]
        chunks += [chunk(w0, QW + 2 * KW + c, CW, "T", "copy", to_T(qiT, c)) for c in range(0, IW, CW)]
        chunks += [chunk(w0, QW, CW, "N", "copy", to_N(either(k_p, k_s))),
                   chunk(w0, QW + KW, CW, "N", "copy", to_N(either(v_p, v_s)))]
        chunks += [chunk(w0, c, CW, "T", "copy", to_T(qT, c)) for c in range(0, QW, CW)]
        gemm_phase(nc, "proj0", ident, chunks, src_dram=either(xp, xs), gamma=norm_mix[0])
        prompt_attention_phase(nc, "att", ident, qT, qiT, wt, k_p, v_p, ki_p, o)
        sample_attention_phase(nc, "satt", ident, qT, qiT, wt, c_k, c_v, cache_kidx[0], k_s, v_s, ki_s, same_frame, o)

        h = ctx.enter_context(nc.sbuf_tensor("h", [P, NT, D], F32))
        gemm_phase(nc, "out0", ident, [chunk(a_w_o[0], c, CW, "N", "resid", None) for c in range(0, D, CW)],
                   src_dram=tile_of(o), residual=either(xp, xs), h=h)
        mlp_phase(nc, "mlp0", ident, h, norm_ffn[0], ffn_w_up[0], ffn_w_down[0])
        w1 = b_w_in[0]
        HK = GH * DK
        chunks = [chunk(w1, 2 * HK + 2 * D, RANK, "T", "copy", to_T(ga, 0))]
        chunks += [chunk(w1, c, CW, "T", DK ** -0.5, to_T(gq, c)) for c in range(0, HK, CW)]
        chunks += [chunk(w1, HK + c, CW, "T", "copy", to_T(gk, c)) for c in range(0, HK, CW)]
        chunks += [chunk(w1, 2 * HK + c, CW, "N", "copy", to_N(tile_of(gv), c)) for c in range(0, D, CW)]
        chunks += [chunk(w1, 2 * HK + D + c, CW, "N", "silu", to_N(tile_of(gs), c)) for c in range(0, D, CW)]
        gemm_phase(nc, "proj1", ident, chunks, src_sb=h, gamma=norm_mix[1])
        gla_phase(nc, "gla", ident, gq, gk, ga, gv, gs, b_w_a2[0], b_b_a[0], b_norm[0], state_gla[0],
                  masks, starts, stream_of, go, gla_prompt[0, 0], gla_sample[0])
        gemm_phase(nc, "out1", ident, [chunk(b_w_o[0], c, CW, "N", "resid", None) for c in range(0, D, CW)],
                   src_dram=tile_of(go), h=h)
        mlp_phase(nc, "mlp1", ident, h, norm_ffn[1], ffn_w_up[1], ffn_w_down[1])
        final_phase(nc, "final", h, norm_final, either(yp, ys))


INPUTS = ["x_prompt", "x_sample", "cache_k", "cache_v", "cache_kidx", "state_gla", "norm_mix", "norm_ffn",
          "norm_final", "a_w_in", "a_w_o", "b_w_in", "b_w_a2", "b_b_a", "b_norm", "b_w_o", "ffn_w_up", "ffn_w_down"]
OUTPUTS = [(1, SEQ, D), (DEC_B, DEC_T, D), (1, 1, SEQ, KVH, HD), (1, 1, SEQ, KVH, HD), (1, 1, SEQ, ID),
           (1, 1, GH, DK, DV), (1, DEC_B, DEC_T, KVH, HD), (1, DEC_B, DEC_T, KVH, HD), (1, DEC_B, DEC_T, ID),
           (1, DEC_B, GH, DK, DV)]


def kernel(**inputs):
    import concourse.bacc as bacc
    from concourse.bass_utils import run_bass_kernel_spmd

    nc = bacc.Bacc("TRN2", target_bir_lowering=False, num_devices=1)
    arrays = {name: np.ascontiguousarray(inputs[name]) for name in INPUTS}
    arrays |= {"ident": np.eye(P, dtype=np.float32), "same_frame": same_frame_table(), "level_masks": level_masks(),
               "scan_starts": scan_starts(), "stream_rows": stream_rows()}
    feed = {f"in_{name}": a for name, a in arrays.items()}
    args = [nc.dram_tensor(name, a.shape, mybir.dt.from_np(a.dtype), kind="ExternalInput").ap()
            for name, a in feed.items()]
    args += [nc.dram_tensor(f"out_{i}", shape, F32, kind="ExternalOutput").ap() for i, shape in enumerate(OUTPUTS)]
    encoder(nc, *args)
    r = run_bass_kernel_spmd(nc, [feed], core_ids=[0])
    return tuple(r.results[0][f"out_{i}"] for i in range(len(OUTPUTS)))
```

```python
from contextlib import ExitStack

import numpy as np

import concourse.bass as bass
from concourse import mybir

F32 = mybir.dt.float32
F32R = mybir.dt.float32r
U32 = mybir.dt.uint32
ACT = mybir.ActivationFunctionType
ALU = mybir.AluOpType
AX = mybir.AxisListType

P = 128
D = 1024
KB = D // P
SEQ, DEC_B, DEC_T, PAST = 1024, 8, 16, 512
NT_P = SEQ // P
NT = NT_P + 1
TOK = NT * P
GRP = 3
NG = NT // GRP
GW = GRP * P
HEADS, KVH, HD = 16, 4, 64
IH, ID = 8, 64
TOPK_P, TOPK_S = 256, (PAST + DEC_T) // 4
CHUNK = 64
A_IN = HEADS * HD + 2 * KVH * HD + IH * ID + ID + IH
GH, DK, DV, RANK = 4, 128, 256, 16
TAU = 16.0
B_IN = 2 * GH * DK + GH * DV + D + RANK
FF = 4 * D
CW = 256
EPS = 1e-6
FILL = -3.0e38
MARK = -3.2e38
CUT = -3.1e38
NEG = -1.0e30
LEVELS = (64, 32, 16, 8, 4, 2, 1)


def bc(ap, n):
    return ap.rearrange("(a n) -> a n", a=1).broadcast_to([P, n])


class Block:

    def __init__(self, nc, name):
        self.nc, self.name, self.ctx, self.sems = nc, name, ExitStack(), []

    def __enter__(self):
        self.ctx.__enter__()
        return self

    def __exit__(self, *a):
        if a[0] is None:
            self.nc.clear_and_free_semaphores(self.sems)
            self.nc.all_engine_barrier()
        return self.ctx.__exit__(*a)

    def sb(self, name, shape, dt=F32):
        return self.ctx.enter_context(self.nc.sbuf_tensor(f"{self.name}_{name}", shape, dt))

    def ps(self, name, shape, dt=F32):
        return self.ctx.enter_context(self.nc.psum_tensor(f"{self.name}_{name}", shape, dt))

    def sem(self, name):
        self.sems.append(self.nc.alloc_semaphore(f"{self.name}_{name}"))
        return self.sems[-1]


class Shared:

    def __init__(self, nc, ctx, name, ident):
        def sb(what, shape, dt=F32):
            return ctx.enter_context(nc.sbuf_tensor(f"{name}_{what}", shape, dt))

        self.ident = ident
        self.xhi, self.xlo = sb("xT_hi", [P, KB, TOK], F32R), sb("xT_lo", [P, KB, TOK], F32R)
        self.raw = sb("w_raw", [P, 2, KB, CW])
        self.whi, self.wlo = sb("w_hi", [P, 2, KB, CW], F32R), sb("w_lo", [P, 2, KB, CW], F32R)


class TokenStage:

    def __init__(self, b, sh, tag="", src_dram=None, src_sb=None, ready=None, gamma=None, y=None):
        self.b, self.sh, self.src_dram, self.src_sb, self.gamma, self.y = b, sh, src_dram, src_sb, gamma, y
        self.ready = ready
        self.normed = gamma is not None
        self.tile_in = [b.sem(tag + "tile_in0"), b.sem(tag + "tile_in1")]
        if src_dram is not None:
            self.x = b.sb(tag + "x_in", [P, 2, D])
        if y is None:
            self.psT = b.ps(tag + "psT", [P, 2, 512])
        else:
            self.stored = [b.sem(tag + "y_stored0"), b.sem(tag + "y_stored1")]
        if self.normed:
            self.junk = b.sb(tag + "sq_junk", [P, D])
            self.g = b.sb(tag + "gamma", [P, D])
            self.ss, self.ms, self.rstd = b.sb(tag + "sumsq", [P, NT]), b.sb(tag + "meansq", [P, NT]), b.sb(tag + "rstd", [P, NT])
            self.mhalf = b.sb(tag + "mhalf", [P, 1])
            self.u = b.sb(tag + "u", [P, 2, D])
            self.gamma_in, self.sumsq_ready = b.sem(tag + "gamma_in"), b.sem(tag + "sumsq_ready")
            self.mhalf_ready, self.ms_ready, self.rstd_ready = b.sem(tag + "mhalf_ready"), b.sem(tag + "ms_ready"), b.sem(tag + "rstd_ready")
            self.u_ready = b.sem(tag + "u_ready")
        self.t_done, self.hi_done, self.lo_done = b.sem(tag + "t_done"), b.sem(tag + "thi_done"), b.sem(tag + "tlo_done")

    def tile(self, t):
        return self.src_sb[:, t, :] if self.src_sb is not None else self.x[:, t % 2, :]

    def wait_tile(self, e, t):
        if self.src_sb is None:
            e.wait_ge(self.tile_in[t % 2], 16 * (t // 2 + 1))
        else:
            self.ready(e, t)

    def load_gamma(self, e):
        if self.normed:
            e.dma_start(self.g[:, :], bc(self.gamma, D)).then_inc(self.gamma_in, 16)

    def load(self, e, t):
        if t >= 2:
            if self.normed:
                e.wait_ge(self.u_ready, t - 1)
            else:
                e.wait_ge(self.t_done, 2 * (t - 1))
        e.dma_start(self.x[:, t % 2, :], self.src_dram(t)).then_inc(self.tile_in[t % 2], 16)

    def act_sumsq(self, e, t):
        if self.normed:
            self.wait_tile(e, t)
            if t >= 1:
                e.wait_ge(self.sumsq_ready, t)
            e.activation(self.junk[:, :], self.tile(t), ACT.Square, accum_out=self.ss[:, t:t + 1])\
                .then_inc(self.sumsq_ready, 1)

    def act_hi(self, e, t):
        for half in range(2):
            e.wait_ge(self.t_done, 2 * t + half + 1)
            e.activation(self.sh.xhi[:, 4 * half:4 * half + 4, t * P:(t + 1) * P],
                         self.psT[:, half, :].rearrange("p (k c) -> p k c", k=4), ACT.Copy).then_inc(self.hi_done, 1)

    def pool_consts(self, e):
        if self.normed:
            e.memset(self.mhalf[:, :], -0.5).then_inc(self.mhalf_ready, 1)
            e.wait_ge(self.mhalf_ready, 1)

    def pool_rstd(self, e, t):
        if self.normed:
            e.wait_ge(self.sumsq_ready, t + 1)
            e.tensor_scalar(self.ms[:, t:t + 1], self.ss[:, t:t + 1], 1.0 / D, EPS, ALU.mult, ALU.add)\
                .then_inc(self.ms_ready, 1)
            e.wait_ge(self.ms_ready, t + 1)
            e.tensor_tensor(self.rstd[:, t:t + 1], self.ms[:, t:t + 1], self.mhalf[:, :], ALU.pow)\
                .then_inc(self.rstd_ready, 1)

    def dve_norm(self, e, t):
        if self.normed:
            if t == 0:
                e.wait_ge(self.gamma_in, 16)
            if t >= 2:
                if self.y is None:
                    e.wait_ge(self.t_done, 2 * (t - 1))
                else:
                    e.wait_ge(self.stored[t % 2], 16 * (t // 2))
            self.wait_tile(e, t)
            e.wait_ge(self.rstd_ready, t + 1)
            e.scalar_tensor_tensor(self.u[:, t % 2, :], self.tile(t), self.rstd[:, t:t + 1], self.g[:, :],
                                   ALU.mult, ALU.mult).then_inc(self.u_ready, 1)

    def dve_lo(self, e, t):
        for half in range(2):
            e.wait_ge(self.hi_done, 2 * t + half + 1)
            cols = slice(t * P, (t + 1) * P)
            e.tensor_tensor(self.sh.xlo[:, 4 * half:4 * half + 4, cols],
                            self.psT[:, half, :].rearrange("p (k c) -> p k c", k=4),
                            self.sh.xhi[:, 4 * half:4 * half + 4, cols].bitcast(F32), ALU.subtract).then_inc(self.lo_done, 1)

    def pe_transpose(self, e, t):
        if self.normed:
            e.wait_ge(self.u_ready, t + 1)
        else:
            self.wait_tile(e, t)
        src = self.u[:, t % 2, :] if self.normed else self.tile(t)
        for half in range(2):
            if t >= 1:
                e.wait_ge(self.lo_done, 2 * t + half - 1)
            for k in range(4):
                kk = 4 * half + k
                mm = e.transpose(self.psT[:, half, k * P:(k + 1) * P], src[:, kk * P:(kk + 1) * P], self.sh.ident[:, :])
            mm.then_inc(self.t_done, 1)

    def sp_store(self, e, t):
        e.wait_ge(self.u_ready, t + 1)
        e.dma_start(self.y(t), self.u[:, t % 2, :]).then_inc(self.stored[t % 2], 16)

    def sp_stored(self, e):
        e.wait_ge(self.stored[0], 16 * ((NT + 1) // 2))
        e.wait_ge(self.stored[1], 16 * (NT // 2))

    def wait_ready(self, e, tiles):
        e.wait_ge(self.lo_done, 2 * tiles)


TERMS = ((0, 0), (0, 1), (1, 0))


class Gemm:

    NB = 4

    def __init__(self, b, sh, chunks, preset, slot0=0, h=None, residual=None, next_w=None):
        self.b, self.sh, self.chunks, self.preset, self.h, self.residual = b, sh, chunks, preset, h, residual
        self.next_w, self.slot0 = next_w, slot0
        NB = self.NB
        self.acc = b.ps("acc", [P, NB, 512])
        if any(c["out"] for c in chunks):
            self.stage = b.sb("stage", [P, NB, GW])
        self.w_in = [b.sem("w_in0"), b.sem("w_in1")]
        self.whi_done, self.wlo_done = b.sem("whi_done"), b.sem("wlo_done")
        self.unit_done, self.unit_out = b.sem("unit_done"), b.sem("unit_out")
        if any(c["op"] == "silu" for c in chunks):
            self.sig, self.sig_done = b.sb("sigmoid", [P, NB, CW]), b.sem("sig_done")
        self.stored = [b.sem(f"stored{i}") for i in range(NB)]
        self.res_in = [b.sem(f"res_in{i}") for i in range(NB)]
        if residual is not None:
            self.res = b.sb("residual", [P, NB, CW])
        self.units = units = []
        for ci, c in enumerate(chunks):
            M = c["w"].shape[1]
            us = []
            for g in range(NG):
                if c["form"] == "T":
                    us += [dict(c=ci, g=g, j=j, m=min(P, M - j), n=GW) for j in range(0, M, P)]
                else:
                    us += [dict(c=ci, g=g, t=t, m=P, n=M) for t in range(GRP * g, GRP * g + GRP)]
            for u in us:
                u["i"], u["op"], u["form"] = len(units), c["op"], c["form"]
                u["stores"] = c["out"](u) if c["out"] else []
                units.append(u)
        for x, u in enumerate(u for u in units if u["op"] == "silu"):
            u["sig_before"] = x
        self.of = [[u for u in units if u["c"] == ci] for ci in range(len(chunks))]
        self.n_stores = []
        for s in range(NB):
            n = 0
            for u in units[s::NB]:
                u["stored_before"] = n
                n += 16 * len(u["stores"])
            self.n_stores.append(n)

    def slot(self, ci):
        return (self.slot0 + ci) % 2

    def width(self, ci):
        return CW if ci == len(self.chunks) else self.chunks[ci]["w"].shape[1]

    def loads_before(self, ci):
        return ci // 2 - (self.preset and ci % 2 == 0)

    def splits(self, ci):
        return ci + 1 - self.preset

    def sp_load_w(self, sp, ci):
        if ci > len(self.chunks) or (ci == len(self.chunks) and self.next_w is None):
            return
        src = self.next_w if ci == len(self.chunks) else self.chunks[ci]["w"]
        if ci >= 2 and self.splits(ci - 2) > 0:
            sp.wait_ge(self.wlo_done, self.splits(ci - 2))
        sp.dma_start(self.sh.raw[:, self.slot(ci), :, 0:self.width(ci)], src.rearrange("(k p) n -> p k n", p=P))\
            .then_inc(self.w_in[ci % 2], 16)

    def act_w_hi(self, act, ci):
        if ci > len(self.chunks) or (ci == len(self.chunks) and self.next_w is None):
            return
        M = self.width(ci)
        act.wait_ge(self.w_in[ci % 2], 16 * (self.loads_before(ci) + 1))
        if ci >= 2:
            act.wait_ge(self.unit_done, self.of[ci - 2][-1]["i"] + 1)
        act.activation(self.sh.whi[:, self.slot(ci), :, 0:M], self.sh.raw[:, self.slot(ci), :, 0:M], ACT.Copy).then_inc(self.whi_done, 1)

    def pool_w_lo(self, pool, ci):
        if ci > len(self.chunks) or (ci == len(self.chunks) and self.next_w is None):
            return
        M = self.width(ci)
        pool.wait_ge(self.whi_done, self.splits(ci))
        pool.tensor_tensor(self.sh.wlo[:, self.slot(ci), :, 0:M], self.sh.raw[:, self.slot(ci), :, 0:M],
                           self.sh.whi[:, self.slot(ci), :, 0:M].bitcast(F32), ALU.subtract).then_inc(self.wlo_done, 1)

    def sp_load_res(self, sp, u):
        if self.residual is not None:
            if u["i"] >= self.NB:
                sp.wait_ge(self.unit_out, u["i"] - self.NB + 1)
            c0 = u["c"] * CW
            sp.dma_start(self.res[:, u["i"] % self.NB, :], self.residual(u["t"])[:, c0:c0 + CW])\
                .then_inc(self.res_in[u["i"] % self.NB], 16)

    def sp_store(self, sp, u):
        if u["stores"]:
            sp.wait_ge(self.unit_out, u["i"] + 1)
        for dst, view in u["stores"]:
            sp.dma_start(dst, view(self.stage[:, u["i"] % self.NB, :])).then_inc(self.stored[u["i"] % self.NB], 16)

    def sp_chunks(self, sp):
        for u in self.units[:self.NB]:
            self.sp_load_res(sp, u)
        for ci in range(len(self.chunks)):
            self.sp_load_w(sp, ci + 2)
            for u in self.of[ci]:
                self.sp_store(sp, u)
                if u["i"] + self.NB < len(self.units):
                    self.sp_load_res(sp, self.units[u["i"] + self.NB])

    def sp_end(self, sp):
        for s in range(self.NB):
            if self.n_stores[s]:
                sp.wait_ge(self.stored[s], self.n_stores[s])

    def pe_unit(self, pe, u):
        i, NB = u["i"], self.NB
        if u is self.of[u["c"]][0] and self.splits(u["c"]) > 0:
            pe.wait_ge(self.wlo_done, self.splits(u["c"]))
        if i >= NB:
            pe.wait_ge(self.unit_out, i - NB + 1)
        s, last, n = self.slot(u["c"]), KB * len(TERMS) - 1, 0
        w, x = (self.sh.whi, self.sh.wlo), (self.sh.xhi, self.sh.xlo)
        for k in range(KB):
            for a, c in TERMS:
                if u["form"] == "T":
                    mm = pe.matmul(self.acc[0:u["m"], i % NB, 0:GW], w[a][:, s, k, u["j"]:u["j"] + u["m"]],
                                   x[c][:, k, u["g"] * GW:(u["g"] + 1) * GW], start=(n == 0), stop=(n == last))
                else:
                    mm = pe.matmul(self.acc[:, i % NB, 0:u["n"]], x[c][:, k, u["t"] * P:(u["t"] + 1) * P],
                                   w[a][:, s, k, 0:u["n"]], start=(n == 0), stop=(n == last))
                n += 1
        mm.then_inc(self.unit_done, 1)

    def wait_unit(self, e, u):
        i, NB = u["i"], self.NB
        e.wait_ge(self.unit_done, i + 1)
        if i >= NB:
            e.wait_ge(self.unit_out, i - NB + 1)
        if u["stored_before"]:
            e.wait_ge(self.stored[i % NB], u["stored_before"])

    def act_evacuate(self, act, u):
        self.wait_unit(act, u)
        m, n, s = u["m"], u["n"], u["i"] % self.NB
        scale = 1.0 if u["op"] == "copy" else u["op"]
        act.activation(self.stage[0:m, s, 0:n], self.acc[0:m, s, 0:n], ACT.Copy, scale=scale).then_inc(self.unit_out, 1)

    def act_sigmoid(self, act, u):
        i, s = u["i"], u["i"] % self.NB
        act.wait_ge(self.unit_done, i + 1)
        if i >= self.NB:
            act.wait_ge(self.unit_out, i - self.NB + 1)
        act.activation(self.sig[:, s, 0:u["n"]], self.acc[:, s, 0:u["n"]], ACT.Sigmoid).then_inc(self.sig_done, 1)

    def dve_evacuate(self, dve, u):
        self.wait_unit(dve, u)
        i, m, n, s = u["i"], u["m"], u["n"], u["i"] % self.NB
        src = self.acc[0:m, s, 0:n]
        if u["op"] == "resid":
            cols = self.h[:, u["t"], u["c"] * CW:u["c"] * CW + n]
            if self.residual is not None:
                dve.wait_ge(self.res_in[s], 16 * (i // self.NB + 1))
                dve.tensor_tensor(cols, src, self.res[:, s, 0:n], ALU.add).then_inc(self.unit_out, 1)
            else:
                dve.tensor_tensor(cols, src, cols, ALU.add).then_inc(self.unit_out, 1)
        elif u["op"] == "silu":
            dve.wait_ge(self.sig_done, u["sig_before"] + 1)
            dve.tensor_tensor(self.stage[0:m, s, 0:n], src, self.sig[0:m, s, 0:n], ALU.mult).then_inc(self.unit_out, 1)
        elif u["op"] == "copy":
            dve.tensor_copy(self.stage[0:m, s, 0:n], src).then_inc(self.unit_out, 1)
        else:
            dve.tensor_scalar(self.stage[0:m, s, 0:n], src, u["op"], None, ALU.mult).then_inc(self.unit_out, 1)


def gemm_phase(nc, name, sh, chunks, preset=False, slot0=0, src_dram=None, gamma=None, residual=None, h=None, next_w=None,
               next_gamma=None, spill=()):
    with Block(nc, name) as b:
        st = tail = None
        gm = Gemm(b, sh, chunks, preset, slot0, h, residual, next_w)
        if src_dram is not None:
            st = TokenStage(b, sh, src_dram=src_dram, gamma=gamma)
        if next_gamma is not None:
            last = {u["t"]: u for u in gm.of[-1]}
            tail = TokenStage(b, sh, tag="next_", src_sb=h, ready=lambda e, t: e.wait_ge(gm.unit_out, last[t]["i"] + 1),
                              gamma=next_gamma)
        spilled = b.sem("spilled") if spill else None
        NCH = len(chunks)
        head_units = gm.of[0] if st is not None else []
        body_units = [u for u in gm.units if not (st is not None and u["c"] == 0) and not (tail and u["c"] == NCH - 1)]
        tail_units = gm.of[-1] if tail else []

        with nc.Block() as block:
            @block.sync
            def _(sp):
                if st:
                    st.load(sp, 0)
                    st.load_gamma(sp)
                    st.load(sp, 1)
                if tail:
                    tail.load_gamma(sp)
                if not preset:
                    gm.sp_load_w(sp, 0)
                if NCH > 1 or next_w is not None:
                    gm.sp_load_w(sp, 1)
                if st:
                    for t in range(2, NT):
                        st.load(sp, t)
                for dst, src in spill:
                    sp.dma_start(dst, src).then_inc(spilled, 16)
                gm.sp_chunks(sp)
                gm.sp_end(sp)
                if spill:
                    sp.wait_ge(spilled, 16 * len(spill))

            @block.scalar
            def _(act):
                if st:
                    for t in range(NT):
                        st.act_sumsq(act, t)
                        if t >= 1:
                            st.act_hi(act, t - 1)
                        if t == 1 and not preset:
                            gm.act_w_hi(act, 0)
                    st.act_hi(act, NT - 1)
                elif not preset:
                    gm.act_w_hi(act, 0)
                for ci in range(1, NCH + 1):
                    gm.act_w_hi(act, ci)
                    if chunks[ci - 1]["op"] == "silu":
                        for u in gm.of[ci - 1]:
                            gm.act_sigmoid(act, u)
                if tail:
                    for t in range(NT):
                        tail.act_sumsq(act, t)
                        if t >= 2:
                            tail.act_hi(act, t - 2)
                    tail.act_hi(act, NT - 2)
                    tail.act_hi(act, NT - 1)

            @block.gpsimd
            def _(pool):
                if st:
                    st.pool_consts(pool)
                    for t in range(NT):
                        st.pool_rstd(pool, t)
                        if t == 2 and not preset:
                            gm.pool_w_lo(pool, 0)
                elif not preset:
                    gm.pool_w_lo(pool, 0)
                for ci in range(1, NCH + 1):
                    gm.pool_w_lo(pool, ci)
                if tail:
                    tail.pool_consts(pool)
                    for t in range(NT):
                        tail.pool_rstd(pool, t)

            @block.tensor
            def _(pe):
                if st:
                    for t in range(NT):
                        st.pe_transpose(pe, t)
                        if t % GRP == GRP - 1 and t >= 2 * GRP - 1:
                            g = t // GRP - 1
                            st.wait_ready(pe, GRP * (g + 1))
                            for u in head_units:
                                if u["g"] == g:
                                    gm.pe_unit(pe, u)
                    st.wait_ready(pe, NT)
                    for u in head_units:
                        if u["g"] == NG - 1:
                            gm.pe_unit(pe, u)
                for u in body_units:
                    gm.pe_unit(pe, u)
                for u in tail_units:
                    gm.pe_unit(pe, u)
                    if u["t"] >= 2:
                        tail.pe_transpose(pe, u["t"] - 2)
                if tail:
                    tail.pe_transpose(pe, NT - 2)
                    tail.pe_transpose(pe, NT - 1)

            @block.vector
            def _(dve):
                if st:
                    for t in range(NT):
                        st.dve_norm(dve, t)
                        if t >= 1:
                            st.dve_lo(dve, t - 1)
                        if t % GRP == 0 and t >= 2 * GRP:
                            for u in head_units:
                                if u["g"] == t // GRP - 2:
                                    gm.dve_evacuate(dve, u)
                    st.dve_lo(dve, NT - 1)
                    for u in head_units:
                        if u["g"] >= NG - 2:
                            gm.dve_evacuate(dve, u)
                for u in body_units:
                    gm.dve_evacuate(dve, u)
                for u in tail_units:
                    gm.dve_evacuate(dve, u)
                    if u["t"] >= 1:
                        tail.dve_norm(dve, u["t"] - 1)
                    if u["t"] >= 2:
                        tail.dve_lo(dve, u["t"] - 2)
                if tail:
                    tail.dve_norm(dve, NT - 1)
                    tail.dve_lo(dve, NT - 2)
                    tail.dve_lo(dve, NT - 1)


def mlp_phase(nc, name, sh, h, w_up, w_down, next_gamma, next_w=None, y=None):
    NCH = FF // CW
    FB = CW // P
    UU = NG * FB
    DU = NT * (D // 512)
    with Block(nc, name) as b:
        up_raw, up_hi, up_lo = (z[:, 0, :, :] for z in (sh.raw, sh.whi, sh.wlo))
        dn_raw, dn_hi, dn_lo = (z[:, 1, :, :].rearrange("p k c -> p (k c)").rearrange("p (f n) -> p f n", f=FB)
                                for z in (sh.raw, sh.whi, sh.wlo))
        hid_hi, hid_lo = b.sb("hid_hi", [P, FB, TOK], F32R), b.sb("hid_lo", [P, FB, TOK], F32R)
        relu, sq = b.sb("relu", [P, 2, GW]), b.sb("sq", [P, 2, GW])
        up_acc, dn_acc = b.ps("up_acc", [P, 3, 512]), b.ps("dn_acc", [P, 3, 512])
        up_in, dn_in = b.sem("up_in"), b.sem("dn_in")
        up_hi_done, up_lo_done = b.sem("up_hi_done"), b.sem("up_lo_done")
        dn_hi_done, dn_lo_done = b.sem("dn_hi_done"), b.sem("dn_lo_done")
        up_done, dn_done, added = b.sem("up_done"), b.sem("dn_done"), b.sem("added")
        relu_done, sq_done = b.sem("relu_done"), b.sem("sq_done")
        hid_hi_done, hid_lo_done = b.sem("hid_hi_done"), b.sem("hid_lo_done")
        tail = TokenStage(b, sh, src_sb=h, gamma=next_gamma, y=y,
                          ready=lambda e, t: e.wait_ge(added, (NCH - 1) * DU + 2 * (t + 1)))

        def up_src(i):
            return w_up[:, bass.ds(i * CW, CW)].rearrange("(k p) n -> p k n", p=P)

        def dn_src(i):
            return w_down[bass.ds(i * CW, CW), :].rearrange("(k p) n -> p k n", p=P)

        def chunks_loop(e, body):
            body(0, True, False)
            with e.Fori(1, NCH - 1) as i:
                body(i, False, False)
            body(NCH - 1, False, True)

        with nc.Block() as block:
            @block.sync
            def _(sp):
                sp.dma_start(dn_raw, dn_src(0)).then_inc(dn_in, 16)
                tail.load_gamma(sp)
                if y is not None:
                    for t in range(NT):
                        tail.sp_store(sp, t)
                    tail.sp_stored(sp)

            @block.scalar
            def _(act):
                act.dma_start(up_raw, up_src(1)).then_inc(up_in, 16)

                def body(i, first, last):
                    act.wait_ge(dn_in, i * 16 + 16)
                    if not first:
                        act.wait_ge(dn_done, i * DU)
                    act.activation(dn_hi, dn_raw, ACT.Copy).then_inc(dn_hi_done, 1)
                    for u in range(UU):
                        g, j = u // FB, u % FB
                        act.wait_ge(up_done, i * UU + (u + 1))
                        if not (first and u < 2):
                            act.wait_ge(hid_lo_done, i * UU + (u - 1))
                        act.activation(relu[:, u % 2, :], up_acc[:, u % 3, 0:GW], ACT.Relu).then_inc(relu_done, 1)
                        act.wait_ge(relu_done, i * UU + (u + 1))
                        act.activation(hid_hi[:, j, g * GW:(g + 1) * GW], relu[:, u % 2, :], ACT.Square)\
                            .then_inc(hid_hi_done, 1)
                    if last and next_w is None:
                        return
                    act.wait_ge(up_in, i * 16 + 16)
                    act.activation(up_hi, up_raw, ACT.Copy).then_inc(up_hi_done, 1)
                    if not last:
                        act.wait_ge(dn_lo_done, i + 1)
                        act.dma_start(dn_raw, dn_src(i + 1)).then_inc(dn_in, 16)

                def next_up(i, src):
                    act.wait_ge(up_lo_done, i + 1)
                    act.dma_start(up_raw, src).then_inc(up_in, 16)

                body(0, True, False)
                with act.Fori(1, NCH - 1) as i:
                    next_up(i - 1, up_src(i + 1))
                    body(i, False, False)
                if next_w is not None:
                    next_up(NCH - 2, next_w.rearrange("(k p) n -> p k n", p=P))
                body(NCH - 1, False, True)
                for t in range(NT):
                    tail.act_sumsq(act, t)
                    if t >= 2 and y is None:
                        tail.act_hi(act, t - 2)
                if y is None:
                    tail.act_hi(act, NT - 2)
                    tail.act_hi(act, NT - 1)

            @block.gpsimd
            def _(pool):
                def body(i, first, last):
                    pool.wait_ge(dn_hi_done, i + 1)
                    pool.tensor_tensor(dn_lo, dn_raw, dn_hi.bitcast(F32), ALU.subtract).then_inc(dn_lo_done, 1)
                    if not last or next_w is not None:
                        pool.wait_ge(up_hi_done, i + 1)
                        pool.tensor_tensor(up_lo, up_raw, up_hi.bitcast(F32), ALU.subtract).then_inc(up_lo_done, 1)

                tail.pool_consts(pool)
                chunks_loop(pool, body)
                for t in range(NT):
                    tail.pool_rstd(pool, t)

            @block.tensor
            def _(pe):
                w_up_s, w_dn_s = (up_hi, up_lo), (dn_hi, dn_lo)
                x_s, hid_s = (sh.xhi, sh.xlo), (hid_hi, hid_lo)

                def body(i, first, last):
                    if not first:
                        pe.wait_ge(up_lo_done, i)
                    for u in range(UU):
                        g, j = u // FB, u % FB
                        if not (first and u < 3):
                            pe.wait_ge(relu_done, i * UU + (u - 2))
                        n = 0
                        for k in range(KB):
                            for a, c in TERMS:
                                mm = pe.matmul(up_acc[:, u % 3, 0:GW], w_up_s[a][:, k, j * P:(j + 1) * P],
                                               x_s[c][:, k, g * GW:(g + 1) * GW],
                                               start=(n == 0), stop=(n == len(TERMS) * KB - 1))
                                n += 1
                        mm.then_inc(up_done, 1)
                    pe.wait_ge(dn_lo_done, i + 1)
                    for v in range(DU):
                        t, half = v // 2, v % 2
                        if v % (2 * GRP) == 0:
                            pe.wait_ge(hid_lo_done, i * UU + FB * (t // GRP + 1))
                        if not (first and v < 3):
                            pe.wait_ge(added, i * DU + (v - 2))
                        n = 0
                        for k in range(FB):
                            for a, c in TERMS:
                                mm = pe.matmul(dn_acc[:, v % 3, :], hid_s[c][:, k, t * P:(t + 1) * P],
                                               w_dn_s[a][:, k, half * 512:(half + 1) * 512],
                                               start=(n == 0), stop=(n == len(TERMS) * FB - 1))
                                n += 1
                        mm.then_inc(dn_done, 1)
                        if last and y is None and half == 1 and t >= 2:
                            tail.pe_transpose(pe, t - 2)

                chunks_loop(pe, body)
                if y is None:
                    tail.pe_transpose(pe, NT - 2)
                    tail.pe_transpose(pe, NT - 1)

            @block.vector
            def _(dve):
                def body(i, first, last):
                    for u in range(UU):
                        g, j = u // FB, u % FB
                        dve.wait_ge(relu_done, i * UU + (u + 1))
                        dve.tensor_tensor(sq[:, u % 2, :], relu[:, u % 2, :], relu[:, u % 2, :], ALU.mult)\
                            .then_inc(sq_done, 1)
                        dve.wait_ge(sq_done, i * UU + (u + 1))
                        dve.wait_ge(hid_hi_done, i * UU + (u + 1))
                        dve.tensor_tensor(hid_lo[:, j, g * GW:(g + 1) * GW], sq[:, u % 2, :],
                                          hid_hi[:, j, g * GW:(g + 1) * GW].bitcast(F32), ALU.subtract)\
                            .then_inc(hid_lo_done, 1)
                    for v in range(DU):
                        t, half = v // 2, v % 2
                        cols = h[:, t, half * 512:(half + 1) * 512]
                        dve.wait_ge(dn_done, i * DU + (v + 1))
                        dve.tensor_tensor(cols, dn_acc[:, v % 3, :], cols, ALU.add).then_inc(added, 1)
                        if last and half == 1:
                            if t >= 1:
                                tail.dve_norm(dve, t - 1)
                            if t >= 2 and y is None:
                                tail.dve_lo(dve, t - 2)

                chunks_loop(dve, body)
                tail.dve_norm(dve, NT - 1)
                if y is None:
                    tail.dve_lo(dve, NT - 2)
                    tail.dve_lo(dve, NT - 1)


T0 = TOPK_P // P
ROUNDS = TOPK_P // 8
SCORE_AT = {t: sum((i + 1) * P for i in range(T0, t)) for t in range(T0, NT_P + 1)}


def pieces(x, L):
    n = 1 if L <= 512 else 2
    return x[:, 0:n, 0:L // n] if len(x.shape) == 3 else x.rearrange("p (n c) -> p n c", n=n)


class Choice:

    def __init__(self, b, score):
        self.score, self.top8 = score, b.sb("top8", [P, 8])
        self.top8_done, self.replaced, self.bias_done = b.sem("top8_done"), b.sem("replaced"), b.sem("bias_done")
        self.rounds = self.biased = 0

    def scores(self, t):
        return self.score[:, SCORE_AT[t]:SCORE_AT[t] + (t + 1) * P]

    def dve_round(self, dve, t):
        r, sc = self.rounds, self.scores(t)
        if r >= 1:
            dve.wait_ge(self.replaced, r)
        dve.max(self.top8[:, :], sc).then_inc(self.top8_done, 1)
        dve.wait_ge(self.top8_done, r + 1)
        dve.match_replace(sc, self.top8[:, :], sc, MARK).then_inc(self.replaced, 1)
        self.rounds += 1

    def dve_bias(self, dve, t):
        sc = self.scores(t)
        dve.wait_ge(self.replaced, self.rounds)
        dve.tensor_scalar(sc, sc, CUT, NEG, ALU.is_gt, ALU.mult).then_inc(self.bias_done, 1)
        self.biased += 1


def project_and_score_phase(nc, name, sh, chunks, preset, slot0, qiT, wt, ki_out, score):
    with Block(nc, name) as b:
        gm = Gemm(b, sh, chunks, preset, slot0)
        ch = Choice(b, score)
        kiin = b.sb("ki_in", [P, NT_P, 2, ID])
        ki_hi, ki_lo = b.sb("ki_hi", [P, SEQ], F32R), b.sb("ki_lo", [P, SEQ], F32R)
        q_in, q_split = b.sb("q_in", [P, 2, IH, P]), b.sb("q_split", [P, 2, IH, P], F32R)
        w_raw, w = b.sb("w_raw", [P, NT_P, IH]), b.sb("w", [P, NT_P, IH])
        RR = 3
        rl = b.sb("relu", [P, RR, SEQ])
        slot = b.ps("slot", [P, 2, 2, 512])
        ki_loaded, w_loaded = b.sem("ki_loaded"), b.sem("w_loaded")
        q_loaded = [b.sem("q_loaded0"), b.sem("q_loaded1")]
        q_hi_done, q_lo_done = b.sem("q_hi_done"), b.sem("q_lo_done")
        w_done, turned, ki_hi_done, ki_lo_done = b.sem("w_done"), b.sem("turned"), b.sem("ki_hi_done"), b.sem("ki_lo_done")
        dots_done, relu_done, scored, filled = b.sem("dots_done"), b.sem("relu_done"), b.sem("scored"), b.sem("filled")

        plan, units = [], list(gm.units)
        late = NT_P - 2
        for t in range(T0, NT_P):
            for ih in range(IH):
                plan.append(("index", t, ih))
                if t >= T0 + 2:
                    plan += [("round", t - 2, r) for r in range(ROUNDS // IH)]
                    for _ in range(1 if t < late or ih % 2 else 2):
                        if units:
                            plan.append(("unit", units.pop(0), 0))
        plan += [("unit", u, 0) for u in units]
        heads = [(t, ih) for kind, t, ih in plan if kind == "index"]

        with nc.Block() as block:
            @block.sync
            def _(sp):
                def load_q(t):
                    if t >= T0 + 2:
                        sp.wait_ge(q_hi_done, t - T0 - 1)
                        sp.wait_ge(q_lo_done, t - T0 - 1)
                    for r in range(2):
                        sp.dma_start(q_in[r * ID:(r + 1) * ID, t % 2, :, :],
                                     qiT[:, t * P:(t + 1) * P].rearrange("(h d) n -> d h n", d=ID))\
                            .then_inc(q_loaded[t % 2], 16)

                for r in range(2):
                    sp.dma_start(kiin[:, :, r, :], ki_out.rearrange("(t p) c -> p t c", p=P)).then_inc(ki_loaded, 16)
                load_q(T0)
                sp.dma_start(w_raw[:, :, :], wt[0:SEQ, :].rearrange("(t p) c -> p t c", p=P)).then_inc(w_loaded, 16)
                load_q(T0 + 1)
                if not preset:
                    gm.sp_load_w(sp, 0)
                gm.sp_load_w(sp, 1)
                for t in range(T0 + 2, NT_P):
                    load_q(t)
                    if t == T0 + 2:
                        gm.sp_load_w(sp, 2)
                for ci in range(len(chunks)):
                    if ci >= 1:
                        gm.sp_load_w(sp, ci + 2)
                    for u in gm.of[ci]:
                        gm.sp_store(sp, u)
                gm.sp_end(sp)

            @block.gpsimd
            def _(pool):
                def q_lo(t):
                    pool.wait_ge(q_hi_done, t - T0 + 1)
                    pool.tensor_tensor(q_split[ID:P, t % 2, :, :], q_in[ID:P, t % 2, :, :],
                                       q_split[ID:P, t % 2, :, :].bitcast(F32), ALU.subtract).then_inc(q_lo_done, 1)

                q_lo(T0)
                q_lo(T0 + 1)
                pool.wait_ge(q_lo_done, 2)
                if not preset:
                    gm.pool_w_lo(pool, 0)
                gm.pool_w_lo(pool, 1)
                pool.wait_ge(gm.wlo_done, gm.splits(1))
                for t in range(T0 + 2, NT_P):
                    q_lo(t)
                pool.wait_ge(q_lo_done, NT_P - T0)
                for ci in range(2, len(chunks) + 1):
                    gm.pool_w_lo(pool, ci)

            @block.tensor
            def _(pe):
                pe.wait_ge(ki_loaded, 32)
                for r in range(2):
                    for c in range(4):
                        mm = pe.transpose(slot[:, r, 0, c * P:(c + 1) * P],
                                          kiin[:, 4 * r + c, :, :].rearrange("p r d -> p (r d)"), sh.ident[:, :])
                    mm.then_inc(turned, 1)
                pe.wait_ge(ki_lo_done, 2)
                n = 0
                for kind, t, ih in plan:
                    if kind == "unit":
                        gm.pe_unit(pe, t)
                    elif kind == "index":
                        if ih == 0:
                            pe.wait_ge(q_lo_done, t - T0 + 1)
                        if n >= 2:
                            pe.wait_ge(relu_done, n - 1)
                        L = (t + 1) * P
                        k = 1 if L <= 512 else 2
                        for j in range(k):
                            cols = slice(j * L // k, (j + 1) * L // k)
                            for x, keys in enumerate((ki_hi, ki_lo)):
                                mm = pe.matmul(slot[:, n % 2, j, 0:L // k], q_split[:, t % 2, ih, :], keys[:, cols],
                                               start=(x == 0), stop=(x == 1))
                        mm.then_inc(dots_done, 1)
                        n += 1

            @block.scalar
            def _(act):
                def q_hi(t):
                    act.wait_ge(q_loaded[t % 2], 32 * ((t - T0) // 2 + 1))
                    if t >= T0 + 2:
                        act.wait_ge(dots_done, IH * (t - T0 - 1))
                    act.activation(q_split[:, t % 2, :, :], q_in[:, t % 2, :, :], ACT.Copy).then_inc(q_hi_done, 1)

                for r in range(2):
                    act.wait_ge(turned, r + 1)
                    act.activation(ki_hi[:, r * 512:(r + 1) * 512], slot[:, r, 0, :], ACT.Copy).then_inc(ki_hi_done, 1)
                q_hi(T0)
                q_hi(T0 + 1)
                if not preset:
                    gm.act_w_hi(act, 0)
                gm.act_w_hi(act, 1)
                n = 0
                for kind, t, ih in plan:
                    if kind == "unit":
                        gm.act_evacuate(act, t)
                        if t is gm.of[t["c"]][-1] and t["c"] + 2 < len(chunks):
                            gm.act_w_hi(act, t["c"] + 2)
                    elif kind == "index":
                        L = (t + 1) * P
                        act.wait_ge(dots_done, n + 1)
                        if n >= RR:
                            act.wait_ge(scored, n - RR + 1)
                        act.activation(pieces(rl[:, n % RR, 0:L], L), pieces(slot[:, n % 2, :, :], L), ACT.Relu,
                                       scale=ID ** -0.5).then_inc(relu_done, 1)
                        n += 1
                        if ih == IH - 1 and t + 2 < NT_P:
                            q_hi(t + 2)

            @block.vector
            def _(dve):
                dve.wait_ge(w_loaded, 16)
                dve.tensor_scalar(w[:, :, :], w_raw[:, :, :], IH ** -0.5, None, ALU.mult).then_inc(w_done, 1)
                for r in range(2):
                    dve.wait_ge(ki_hi_done, r + 1)
                    cols = slice(r * 512, (r + 1) * 512)
                    dve.tensor_tensor(ki_lo[:, cols], slot[:, r, 0, :], ki_hi[:, cols].bitcast(F32), ALU.subtract)\
                        .then_inc(ki_lo_done, 1)
                dve.wait_ge(w_done, 1)
                n = 0
                for kind, t, x in plan:
                    if kind == "index":
                        sc, L = ch.scores(t), (t + 1) * P
                        dve.wait_ge(relu_done, n + 1)
                        if x == 0:
                            dve.tensor_scalar(sc, rl[:, n % RR, 0:L], w[:, t, 0:1], None, ALU.mult).then_inc(scored, 1)
                        else:
                            dve.wait_ge(scored, n)
                            dve.scalar_tensor_tensor(sc, rl[:, n % RR, 0:L], w[:, t, x:x + 1], sc, ALU.mult, ALU.add)\
                                .then_inc(scored, 1)
                        n += 1
                        if x == IH - 1:
                            dve.wait_ge(scored, n)
                            dve.memset(sc[0:CHUNK, L - CHUNK:L], FILL).then_inc(filled, 1)
                    elif kind == "round":
                        if x == 0:
                            dve.wait_ge(filled, t - T0 + 1)
                        ch.dve_round(dve, t)
                        if ch.rounds % ROUNDS == 0:
                            ch.dve_bias(dve, t)


def prompt_attention_phase(nc, name, ident, qT, k_out, v_out, score, o):
    ORDER = [5, 4, 6, 3, 7, 2, 1, 0]
    LATE = {5: 6, 4: 6, 6: 7, 3: 7}
    GH4 = HEADS // KVH
    with Block(nc, name) as b:
        ch = Choice(b, score)
        kin = b.sb("k_in", [P, NT_P, KVH, 2, HD])
        vin = b.sb("v_in", [P, NT_P, KVH * HD])
        k_hi, k_lo = b.sb("k_hi", [P, KVH, SEQ], F32R), b.sb("k_lo", [P, KVH, SEQ], F32R)
        q_in, q_split = b.sb("q_in", [P, 2, HEADS, P]), b.sb("q_split", [P, 2, HEADS, P], F32R)
        open_ = b.sb("open", [P, T0, T0 * P])
        LR = 4
        lg = b.sb("logits", [P, LR, SEQ])
        probs_T = b.sb("probs_T", [P, 2, SEQ])
        nm = b.sb("neg_max", [P, 4])
        den, rden = b.sb("den", [P, 4, GH4]), b.sb("rden", [P, 2, GH4])
        ot = b.sb("o_tile", [P, 2, D])
        slot = b.ps("slot", [P, 2, 2, 512])
        psT = b.ps("psT", [P, 2, 512])
        pv = b.ps("pv", [P, 2, GH4, P])
        k_loaded, v_loaded = b.sem("k_loaded"), b.sem("v_loaded")
        q_loaded = [b.sem("q_loaded0"), b.sem("q_loaded1")]
        q_hi_done, q_lo_done = b.sem("q_hi_done"), b.sem("q_lo_done")
        k_turned, k_hi_done, k_lo_done = b.sem("k_turned"), b.sem("k_hi_done"), b.sem("k_lo_done")
        opened = b.sem("opened")
        qk_done, masked, exp_done = b.sem("qk_done"), b.sem("masked"), b.sem("exp_done")
        turned, turned_out, pv_done = b.sem("turned"), b.sem("turned_out"), b.sem("pv_done")
        rden_done, o_done = b.sem("rden_done"), b.sem("o_done")
        o_stored = [b.sem("o_stored0"), b.sem("o_stored1")]

        N = NT_P * HEADS
        tile_at = lambda n: ORDER[n // HEADS]
        bank_of, banks = {}, 0
        for n in range(N):
            nb = (tile_at(n) + 4) // 4
            bank_of[n] = list(range(banks, banks + nb))
            banks += nb

        with nc.Block() as block:
            @block.sync
            def _(sp):
                def load_q(i):
                    t = ORDER[i]
                    if i >= 2:
                        sp.wait_ge(q_hi_done, i - 1)
                        sp.wait_ge(q_lo_done, i - 1)
                    for r in range(2):
                        sp.dma_start(q_in[r * HD:(r + 1) * HD, i % 2, :, :],
                                     qT[:, t * P:(t + 1) * P].rearrange("(h d) n -> d h n", d=HD))\
                            .then_inc(q_loaded[i % 2], 16)

                for r in range(2):
                    for t in range(NT_P):
                        sp.dma_start(kin[:, t, :, r, :], k_out[t * P:(t + 1) * P, :].rearrange("p (v d) -> p v d", d=HD))\
                            .then_inc(k_loaded, 16)
                    if r == 0:
                        load_q(0)
                sp.dma_start(vin[:, :, :], v_out.rearrange("(t p) c -> p t c", p=P)).then_inc(v_loaded, 16)
                load_q(1)
                for i, t in enumerate(ORDER):
                    if i + 2 < NT_P:
                        load_q(i + 2)
                    sp.wait_ge(o_done, KVH * (i + 1))
                    sp.dma_start(o[t * P:(t + 1) * P, :], ot[:, i % 2, :]).then_inc(o_stored[i % 2], 16)
                for i in range(2):
                    sp.wait_ge(o_stored[i], 16 * NT_P // 2)

            @block.gpsimd
            def _(pool):
                pool.memset(open_[:, :, :], 0.0).then_inc(opened, 1)
                pool.wait_ge(opened, 1)
                for t in range(T0):
                    pool.memset(open_[0:CHUNK, t, (t + 1) * P - CHUNK:(t + 1) * P], NEG).then_inc(opened, 1)
                pool.wait_ge(opened, 1 + T0)
                for i in range(NT_P):
                    pool.wait_ge(q_hi_done, i + 1)
                    pool.tensor_tensor(q_split[HD:P, i % 2, :, :], q_in[HD:P, i % 2, :, :],
                                       q_split[HD:P, i % 2, :, :].bitcast(F32), ALU.subtract).then_inc(q_lo_done, 1)

            @block.tensor
            def _(pe):
                pe.wait_ge(k_loaded, 32 * NT_P)
                for r in range(NT_P):
                    if r >= 2:
                        pe.wait_ge(k_lo_done, r - 1)
                    for v in range(KVH):
                        mm = pe.transpose(psT[:, r % 2, v * P:(v + 1) * P],
                                          kin[:, r, v, :, :].rearrange("p r d -> p (r d)"), ident[:, :])
                    mm.then_inc(k_turned, 1)
                pe.wait_ge(k_lo_done, NT_P)
                pe.wait_ge(v_loaded, 16)

                def turn(n):
                    pe.wait_ge(exp_done, n + 1)
                    for x, i in enumerate(bank_of[n]):
                        if i >= 2:
                            pe.wait_ge(turned_out, i - 1)
                        for j in range(4 * x, min(4 * x + 4, tile_at(n) + 1)):
                            mm = pe.transpose(psT[:, i % 2, (j % 4) * P:(j % 4 + 1) * P],
                                              lg[:, n % LR, j * P:(j + 1) * P], ident[:, :])
                        mm.then_inc(turned, 1)

                def values(n):
                    t, hd = tile_at(n), n % HEADS
                    pair = hd // (2 * GH4)
                    pe.wait_ge(turned_out, bank_of[n][-1] + 1)
                    if n >= 2 * GH4 and n % GH4 == 0:
                        pe.wait_ge(o_done, n // GH4 - 1)
                    for j in range(t + 1):
                        mm = pe.matmul(pv[:, n // GH4 % 2, n % GH4, :], probs_T[:, n % 2, j * P:(j + 1) * P],
                                       vin[:, j, pair * P:(pair + 1) * P], start=(j == 0), stop=(j == t))
                    mm.then_inc(pv_done, 1)

                for n in range(N + 3):
                    if n < N:
                        t, i, hd = tile_at(n), n // HEADS, n % HEADS
                        if hd == 0:
                            pe.wait_ge(q_lo_done, i + 1)
                        if n >= 2:
                            pe.wait_ge(masked, n - 1)
                        L = (t + 1) * P
                        k = 1 if L <= 512 else 2
                        for j in range(k):
                            cols = slice(j * L // k, (j + 1) * L // k)
                            for x, keys in enumerate((k_hi, k_lo)):
                                mm = pe.matmul(slot[:, n % 2, j, 0:L // k], q_split[:, i % 2, hd, :],
                                               keys[:, hd // GH4, cols], start=(x == 0), stop=(x == 1))
                        mm.then_inc(qk_done, 1)
                    if 2 <= n < N + 2:
                        turn(n - 2)
                    if n >= 3:
                        values(n - 3)

            @block.scalar
            def _(act):
                def q_hi(i):
                    act.wait_ge(q_loaded[i % 2], 32 * (i // 2 + 1))
                    if i >= 2:
                        act.wait_ge(qk_done, HEADS * (i - 1))
                    act.activation(q_split[:, i % 2, :, :], q_in[:, i % 2, :, :], ACT.Copy).then_inc(q_hi_done, 1)

                q_hi(0)
                for r in range(NT_P):
                    act.wait_ge(k_turned, r + 1)
                    act.activation(k_hi[:, :, r * P:(r + 1) * P], psT[:, r % 2, :].rearrange("p (v n) -> p v n", v=KVH),
                                   ACT.Copy).then_inc(k_hi_done, 1)
                q_hi(1)

                def turn_out(n):
                    for x, i in enumerate(bank_of[n]):
                        nb = min(4, tile_at(n) + 1 - 4 * x)
                        act.wait_ge(turned, i + 1)
                        if n >= 2:
                            act.wait_ge(pv_done, n - 1)
                        act.activation(probs_T[:, n % 2, 4 * x * P:(4 * x + nb) * P], psT[:, i % 2, 0:nb * P], ACT.Copy)\
                            .then_inc(turned_out, 1)

                for n in range(N + 2):
                    if n < N:
                        L = (tile_at(n) + 1) * P
                        act.wait_ge(masked, n + 1)
                        if n >= 4 * GH4:
                            act.wait_ge(rden_done, n // GH4 - 3)
                        x = lg[:, n % LR, 0:L]
                        act.activation(x, x, ACT.Exp, bias=nm[:, n % 4:n % 4 + 1], scale=-1.0,
                                       accum_out=den[:, n // GH4 % 4, n % GH4:n % GH4 + 1]).then_inc(exp_done, 1)
                        if n % HEADS == HEADS - 1 and n // HEADS + 2 < NT_P:
                            q_hi(n // HEADS + 2)
                    if n >= 2:
                        turn_out(n - 2)

            @block.vector
            def _(dve):
                for r in range(NT_P):
                    dve.wait_ge(k_hi_done, r + 1)
                    cols = slice(r * P, (r + 1) * P)
                    dve.tensor_tensor(k_lo[:, :, cols], psT[:, r % 2, :].rearrange("p (v n) -> p v n", v=KVH),
                                      k_hi[:, :, cols].bitcast(F32), ALU.subtract).then_inc(k_lo_done, 1)

                def finish(g):
                    i, v = g // KVH, g % KVH
                    dve.wait_ge(exp_done, GH4 * (g + 1))
                    dve.reciprocal(rden[:, g % 2, :], den[:, g % 4, :]).then_inc(rden_done, 1)
                    dve.wait_ge(rden_done, g + 1)
                    dve.wait_ge(pv_done, GH4 * (g + 1))
                    if i >= 2 and v == 0:
                        dve.wait_ge(o_stored[i % 2], 16 * (i // 2))
                    dve.tensor_tensor(ot[:, i % 2, v * GH4 * HD:(v + 1) * GH4 * HD].rearrange("p (h d) -> p h d", d=HD),
                                      pv[:, g % 2, :, (v % 2) * HD:(v % 2 + 1) * HD],
                                      rden[:, g % 2, :].unsqueeze(2).broadcast_to([P, GH4, HD]), ALU.mult)\
                        .then_inc(o_done, 1)

                biases = 0
                for n in range(N + 4):
                    if n < N:
                        t, L, hd = tile_at(n), (tile_at(n) + 1) * P, n % HEADS
                        dve.wait_ge(qk_done, n + 1)
                        if t < T0 and hd == 0:
                            dve.wait_ge(opened, 1 + T0)
                        if t in LATE.values() and hd == 0:
                            biases += 1
                            dve.wait_ge(ch.bias_done, biases)
                        if n >= LR:
                            dve.wait_ge(turned, bank_of[n - LR][-1] + 1)
                            dve.wait_ge(exp_done, n - LR + 1)
                        bias = open_[:, t, 0:L] if t < T0 else ch.scores(t)
                        dve.tensor_tensor_reduce(pieces(lg[:, n % LR, 0:L], L), pieces(slot[:, n % 2, :, :], L),
                                                 pieces(bias, L), -1.0, -FILL, ALU.add, ALU.min,
                                                 nm[:, n % 4:n % 4 + 1]).then_inc(masked, 1)
                        if t in LATE:
                            ch.dve_round(dve, LATE[t])
                            if ch.rounds % ROUNDS == 0:
                                ch.dve_bias(dve, LATE[t])
                    if n >= GH4 and n % GH4 == GH4 - 1:
                        finish(n // GH4 - 1)


def sample_attention_phase(nc, name, ident, qT, qiT, wt, cache_k, cache_v, cache_ki, k_new, v_new, ki_new,
                           same_frame, o):
    L = PAST + DEC_T
    PB = PAST // P
    PAIRS = KVH // 2
    N = DEC_B * PAIRS
    with Block(nc, name) as b:
        frame_of, rows_of = b.sb("frame_of", [P, DEC_B, P]), b.sb("rows_of", [P, DEC_B, P])
        qi = b.sb("qi", [ID, DEC_B, IH, DEC_T])
        q = b.sb("q", [P, PAIRS, DEC_B, P])
        w_raw, w = b.sb("w_raw", [P, DEC_B]), b.sb("w", [P, DEC_B])
        cki = b.sb("cki", [P, DEC_B, PB, ID])
        nki, nk = b.sb("nki", [P, ID]), b.sb("nk", [P, KVH * HD])
        ck, cv = b.sb("ck", [P, DEC_B, PB, KVH * HD]), b.sb("cv", [P, DEC_B, PB, KVH * HD])
        nv = b.sb("nv", [DEC_T, DEC_B, KVH * HD])
        nkiT, nkT = b.sb("nkiT", [ID, P]), b.sb("nkT", [P, PAIRS, P])
        ckiT, ckT = b.sb("ckiT", [ID, 2, PAST]), b.sb("ckT", [P, 2, PAST])
        rl, sel = b.sb("relu", [P, 2, L]), b.sb("sel", [P, 2, P])
        PAD = (-TOPK_S) % 8
        score = b.sb("score", [P, L + PAD])
        top8 = b.sb("top8", [P, 8])
        probs = b.sb("probs", [P, 3, L])
        probs_T, probs_Tn = b.sb("probs_T", [P, 2, PAST]), b.sb("probs_Tn", [DEC_T, 2, P])
        mx, nm = b.sb("max", [P, 4]), b.sb("neg_max", [P, 4])
        den, rden = b.sb("den", [P, 4]), b.sb("rden", [P, 4])
        og = b.sb("o_group", [P, 4, P])
        slot = b.ps("slot", [P, 2, 1024])
        psT = b.ps("psT", [P, 2, 512])
        psN, pv = b.ps("psN", [P, 512]), b.ps("pv", [P, 512])
        idx_in, att_in = b.sem("idx_in"), b.sem("att_in")
        q_zero, w_done = b.sem("q_zero"), b.sem("w_done")
        turned, turned_out = b.sem("turned"), b.sem("turned_out")
        qi_done, relu_done, sel_done, summed = b.sem("qi_done"), b.sem("relu_done"), b.sem("sel_done"), b.sem("summed")
        score_out, pad_done = b.sem("score_out"), b.sem("pad_done")
        top8_done, replaced, bias_done = b.sem("top8_done"), b.sem("replaced"), b.sem("bias_done")
        kT_turned, kT_out = b.sem("kT_turned"), b.sem("kT_out")
        qk_done, neg_done, max_done, exp_done = b.sem("qk_done"), b.sem("neg_done"), b.sem("max_done"), b.sem("exp_done")
        p_turned, p_out, pn_out = b.sem("p_turned"), b.sem("p_out"), b.sem("pn_out")
        pv_done, rden_done, o_done = b.sem("pv_done"), b.sem("rden_done"), b.sem("o_done")
        stored = [b.sem(f"stored{i}") for i in range(4)]
        idx_loads, att_loads = [], []

        with nc.Block() as block:
            @block.sync
            def _(sp):
                def load(group, dst, src, **how):
                    sp.dma_start(dst, src, **how).then_inc(idx_in if group is idx_loads else att_in, 16)
                    group.append(dst)

                for s in range(DEC_B):
                    load(idx_loads, cki[:, s, :, :], cache_ki[s].rearrange("(k p) d -> p k d", p=P))
                load(idx_loads, nki[:, :], ki_new)
                for hh in range(IH):
                    load(idx_loads, qi[:, :, hh, :],
                         qiT[hh * ID:(hh + 1) * ID, SEQ:TOK].rearrange("d (b t) -> d b t", t=DEC_T))
                    load(idx_loads, w_raw[hh * DEC_T:(hh + 1) * DEC_T, :],
                         wt[SEQ:TOK, hh:hh + 1].rearrange("(b t) a -> t (b a)", t=DEC_T),
                         allow_slow_non_contiguous=True)
                load(idx_loads, frame_of[:, :, :], same_frame[0])
                load(idx_loads, rows_of[:, :, :], same_frame[1])
                sp.wait_ge(q_zero, 1)
                for v in range(KVH):
                    for g in range(HEADS // KVH):
                        r0 = (v * (HEADS // KVH) + g) * HD
                        c0 = (v % 2) * HD + g * DEC_T
                        load(att_loads, q[(v % 2) * HD:(v % 2 + 1) * HD, v // 2, :, c0:c0 + DEC_T],
                             qT[r0:r0 + HD, SEQ:TOK].rearrange("d (b t) -> d b t", t=DEC_T))
                load(att_loads, nk[:, :], k_new)
                load(att_loads, nv[:, :, :], v_new.rearrange("(b t) c -> t b c", t=DEC_T))
                for s in range(DEC_B):
                    load(att_loads, ck[:, s, :, :], cache_k[s].rearrange("(k p) c -> p k c", p=P))
                    load(att_loads, cv[:, s, :, :], cache_v[s].rearrange("(k p) c -> p k c", p=P))
                for n in range(N):
                    s, pair = n // PAIRS, n % PAIRS
                    sp.wait_ge(o_done, 2 * (n + 1))
                    for r in range(2):
                        v = 2 * pair + r
                        rows = o[SEQ + s * DEC_T:SEQ + (s + 1) * DEC_T, v * 4 * HD:(v + 1) * 4 * HD]
                        for g in range(HEADS // KVH):
                            sp.dma_start(rows[:, g * HD:(g + 1) * HD],
                                         og[r * HD + g * DEC_T:r * HD + (g + 1) * DEC_T, n % 4, r * HD:(r + 1) * HD])\
                                .then_inc(stored[n % 4], 16)
                for i in range(4):
                    sp.wait_ge(stored[i], 16 * 8 * N // 4)

            @block.gpsimd
            def _(pool):
                pool.memset(q[:, :, :, :], 0.0).then_inc(q_zero, 1)
                pool.memset(score[:, L:L + PAD], -FILL).then_inc(pad_done, 1)

            IDX, ATT = 16 * (3 + DEC_B + 2 * IH), 16 * (HEADS + 2 + 2 * DEC_B)

            @block.tensor
            def _(pe):
                pe.wait_ge(idx_in, IDX)
                pe.transpose(psN[0:ID, 0:P], nki[:, :], ident[:, :]).then_inc(turned, 1)

                def turn_ki(s):
                    if s >= 2:
                        pe.wait_ge(turned_out, s)
                    for k in range(PB):
                        mm = pe.transpose(psT[0:ID, s % 2, k * P:(k + 1) * P], cki[:, s, k, :], ident[:, :])
                    mm.then_inc(turned, 1)

                def add_scores(s):
                    pe.wait_ge(sel_done, s + 1)
                    pe.wait_ge(relu_done, s + 1)
                    pe.matmul(slot[:, 1, 0:PAST], sel[:, s % 2, :], rl[:, s % 2, 0:PAST],
                              start=(s == 0), stop=(s == DEC_B - 1))
                    pe.matmul(slot[:, 1, PAST:L], sel[:, s % 2, :], rl[:, s % 2, PAST:L],
                              start=(s == 0), stop=(s == DEC_B - 1)).then_inc(summed, 1)

                turn_ki(0)
                for s in range(DEC_B):
                    if s + 1 < DEC_B:
                        turn_ki(s + 1)
                    pe.wait_ge(turned_out, s + 2)
                    if s >= 1:
                        pe.wait_ge(relu_done, s)
                    lhs = qi[:, s, :, :].rearrange("d h t -> d (h t)")
                    pe.matmul(slot[:, 0, 0:PAST], lhs, ckiT[:, s % 2, :], start=True, stop=True)
                    pe.matmul(slot[:, 0, PAST:L], lhs, nkiT[:, s * DEC_T:(s + 1) * DEC_T], start=True, stop=True)\
                        .then_inc(qi_done, 1)
                    if s >= 1:
                        add_scores(s - 1)
                add_scores(DEC_B - 1)

                pe.wait_ge(att_in, ATT)
                pe.wait_ge(turned_out, DEC_B + 1)
                for pair in range(PAIRS):
                    mm = pe.transpose(psN[:, pair * P:(pair + 1) * P], nk[:, pair * P:(pair + 1) * P], ident[:, :])
                mm.then_inc(kT_turned, 1)

                def turn_k(n):
                    s, pair = n // PAIRS, n % PAIRS
                    if n >= 1:
                        pe.wait_ge(kT_out, n + 1)
                    for k in range(PB):
                        mm = pe.transpose(psT[:, 0, k * P:(k + 1) * P], ck[:, s, k, pair * P:(pair + 1) * P], ident[:, :])
                    mm.then_inc(kT_turned, 1)

                def logits(n):
                    s, pair = n // PAIRS, n % PAIRS
                    pe.wait_ge(kT_out, n + 2)
                    if n >= 2:
                        pe.wait_ge(exp_done, n - 1)
                    for c0, c1, rhs in ((0, PAST, ckT[:, n % 2, :]), (PAST, L, nkT[:, pair, s * DEC_T:(s + 1) * DEC_T])):
                        pe.matmul(slot[:, n % 2, c0:c1], q[:, pair, s, :], rhs, start=True, stop=False)
                        mm = pe.matmul(slot[:, n % 2, c0:c1], rows_of[:, s, :], score[:, c0:c1], start=False, stop=True)
                    mm.then_inc(qk_done, 1)

                def turn_p(n):
                    pe.wait_ge(exp_done, n + 1)
                    if n >= 1:
                        pe.wait_ge(p_out, n)
                        pe.wait_ge(pn_out, n)
                    for k in range(PB):
                        pe.transpose(psT[:, 1, k * P:(k + 1) * P], probs[:, n % 3, k * P:(k + 1) * P], ident[:, :])
                    pe.transpose(psN[0:DEC_T, 0:P], probs[:, n % 3, PAST:L], ident[:, :]).then_inc(p_turned, 1)

                def values(n):
                    s, pair = n // PAIRS, n % PAIRS
                    pe.wait_ge(p_out, n + 1)
                    pe.wait_ge(pn_out, n + 1)
                    if n >= 1:
                        pe.wait_ge(o_done, 2 * n)
                    for k in range(PB):
                        pe.matmul(pv[:, 0:P], probs_T[:, n % 2, k * P:(k + 1) * P], cv[:, s, k, pair * P:(pair + 1) * P],
                                  start=(k == 0), stop=False)
                    pe.matmul(pv[:, 0:P], probs_Tn[:, n % 2, :], nv[:, s, pair * P:(pair + 1) * P],
                              start=False, stop=True).then_inc(pv_done, 1)

                turn_k(0)
                pe.wait_ge(bias_done, 1)
                for n in range(N):
                    if n + 1 < N:
                        turn_k(n + 1)
                    logits(n)
                    if n >= 1:
                        turn_p(n - 1)
                    if n >= 2:
                        values(n - 2)
                turn_p(N - 1)
                values(N - 2)
                values(N - 1)

            @block.scalar
            def _(act):
                act.wait_ge(turned, 1)
                act.activation(nkiT[:, :], psN[0:ID, 0:P], ACT.Copy).then_inc(turned_out, 1)

                def ki_out(s):
                    act.wait_ge(turned, s + 2)
                    if s >= 2:
                        act.wait_ge(qi_done, s - 1)
                    act.activation(ckiT[:, s % 2, :], psT[0:ID, s % 2, :], ACT.Copy).then_inc(turned_out, 1)

                ki_out(0)
                for s in range(DEC_B):
                    if s + 1 < DEC_B:
                        ki_out(s + 1)
                    act.wait_ge(qi_done, s + 1)
                    if s >= 2:
                        act.wait_ge(summed, s - 1)
                    act.activation(rl[:, s % 2, :], slot[:, 0, 0:L], ACT.Relu, scale=ID ** -0.5).then_inc(relu_done, 1)
                act.wait_ge(kT_turned, 1)
                act.activation(nkT[:, :, :], psN[:, 0:PAIRS * P].rearrange("p (a n) -> p a n", n=P), ACT.Copy)\
                    .then_inc(kT_out, 1)

                def k_out(n):
                    act.wait_ge(kT_turned, n + 2)
                    if n >= 2:
                        act.wait_ge(qk_done, n - 1)
                    act.activation(ckT[:, n % 2, :], psT[:, 0, :], ACT.Copy).then_inc(kT_out, 1)

                def turn_out(n):
                    act.wait_ge(p_turned, n + 1)
                    if n >= 2:
                        act.wait_ge(pv_done, n - 1)
                    act.activation(probs_T[:, n % 2, :], psT[:, 1, :], ACT.Copy).then_inc(p_out, 1)

                k_out(0)
                for n in range(N):
                    if n + 1 < N:
                        k_out(n + 1)
                    act.wait_ge(neg_done, n + 1)
                    if n >= 3:
                        act.wait_ge(p_turned, n - 2)
                    if n >= 4:
                        act.wait_ge(rden_done, n - 3)
                    act.activation(probs[:, n % 3, :], slot[:, n % 2, 0:L], ACT.Exp, bias=nm[:, n % 4:n % 4 + 1],
                                   accum_out=den[:, n % 4:n % 4 + 1]).then_inc(exp_done, 1)
                    if n >= 1:
                        turn_out(n - 1)
                turn_out(N - 1)

            @block.vector
            def _(dve):
                dve.wait_ge(idx_in, IDX)
                dve.tensor_scalar(w[:, :], w_raw[:, :], IH ** -0.5, None, ALU.mult).then_inc(w_done, 1)
                dve.wait_ge(w_done, 1)
                for s in range(DEC_B):
                    if s >= 2:
                        dve.wait_ge(summed, s - 1)
                    dve.tensor_scalar(sel[:, s % 2, :], frame_of[:, s, :], w[:, s:s + 1], None, ALU.mult)\
                        .then_inc(sel_done, 1)
                dve.wait_ge(summed, DEC_B)
                dve.tensor_copy(score[:, 0:L], slot[:, 1, 0:L]).then_inc(score_out, 1)
                dve.wait_ge(score_out, 1)
                dve.wait_ge(pad_done, 1)
                for r in range((TOPK_S + PAD) // 8):
                    if r >= 1:
                        dve.wait_ge(replaced, r)
                    dve.max(top8[:, :], score[:, :]).then_inc(top8_done, 1)
                    dve.wait_ge(top8_done, r + 1)
                    dve.match_replace(score[:, :], top8[:, :], score[:, :], MARK).then_inc(replaced, 1)
                dve.wait_ge(replaced, (TOPK_S + PAD) // 8)
                dve.tensor_scalar(score[:, 0:L], score[:, 0:L], CUT, NEG, ALU.is_gt, ALU.mult).then_inc(bias_done, 1)

                def finish(n):
                    dve.wait_ge(exp_done, n + 1)
                    dve.reciprocal(rden[:, n % 4:n % 4 + 1], den[:, n % 4:n % 4 + 1]).then_inc(rden_done, 1)
                    dve.wait_ge(rden_done, n + 1)
                    dve.wait_ge(pv_done, n + 1)
                    if n >= 4:
                        dve.wait_ge(stored[n % 4], 16 * 8 * (n // 4))
                    for r in range(2):
                        rows, cols = slice(r * HD, (r + 1) * HD), slice(r * HD, (r + 1) * HD)
                        dve.tensor_scalar(og[rows, n % 4, cols], pv[rows, cols], rden[rows, n % 4:n % 4 + 1], None,
                                          ALU.mult).then_inc(o_done, 1)

                for n in range(N):
                    m = mx[:, n % 4:n % 4 + 1]
                    dve.wait_ge(qk_done, n + 1)
                    dve.tensor_reduce(m, slot[:, n % 2, 0:L], AX.X, ALU.max).then_inc(max_done, 1)
                    dve.wait_ge(max_done, n + 1)
                    dve.tensor_scalar(nm[:, n % 4:n % 4 + 1], m, -HD ** -0.5, None, ALU.mult).then_inc(neg_done, 1)
                    if n >= 1:
                        dve.wait_ge(p_turned, n)
                        if n >= 3:
                            dve.wait_ge(pv_done, n - 2)
                        dve.tensor_copy(probs_Tn[:, (n - 1) % 2, :], psN[0:DEC_T, 0:P]).then_inc(pn_out, 1)
                    if n >= 2:
                        finish(n - 2)
                dve.wait_ge(p_turned, N)
                dve.wait_ge(pv_done, N - 2)
                dve.tensor_copy(probs_Tn[:, (N - 1) % 2, :], psN[0:DEC_T, 0:P]).then_inc(pn_out, 1)
                finish(N - 2)
                finish(N - 1)


def same_frame_table():
    m = np.zeros((2, P, DEC_B, P), np.float32)
    for s in range(DEC_B):
        for x in range(P // DEC_T):
            for f in range(DEC_T):
                m[0, x * DEC_T + f, s, s * DEC_T + f] = 1.0
                m[1, s * DEC_T + f, s, x * DEC_T + f] = 1.0
    return m


def project_and_level_phase(nc, name, sh, chunks, slot0, qT, kT, aT, w_a2, b_a, masks, starts, ends, A_d, qe_d, kdT_d):
    HW = GH * P
    NL = len(LEVELS)
    XR = 3
    with Block(nc, name) as b:
        gm = Gemm(b, sh, chunks, True, slot0)
        mask, start = b.sb("mask", [P, NL + 1, P]), b.sb("start", [P, 2, HW])
        wa, a = b.sb("wa", [RANK + 1, HW]), b.sb("a", [RANK + 1, 2, P])
        q, k = b.sb("q", [P, 2, GH, P]), b.sb("k", [P, 2, GH, P])
        az, ez, lz = b.sb("az", [P, HW]), b.sb("ez", [P, HW]), b.sb("lz", [P, HW])
        la, bcum = b.sb("la", [P, HW]), b.sb("b", [P, 2, HW])
        dist, dec = b.sb("dist", [P, 2, HW]), b.sb("dec", [P, 2, HW])
        X, A = b.sb("X", [P, XR, HW]), b.sb("A", [P, 2, HW])
        e_b, d_end, e_end = b.sb("e_b", [P, HW]), b.sb("d_end", [P, HW]), b.sb("e_end", [P, HW])
        qe, kd, kdT = b.sb("qe", [P, 2, HW]), b.sb("kd", [P, HW]), b.sb("kdT", [P, 2, HW])
        G = b.ps("G", [P, 2, 512])
        zp, tp = b.ps("z", [P, 512]), b.ps("tp", [P, 512])
        const_in, wa_in, ones_done = b.sem("const_in"), b.sem("wa_in"), b.sem("ones_done")
        in_a, in_qk = [b.sem("in_a0"), b.sem("in_a1")], [b.sem("in_qk0"), b.sem("in_qk1")]
        z_done, abs_done, ez_done, lz_done = b.sem("z_done"), b.sem("abs_done"), b.sem("ez_done"), b.sem("lz_done")
        la_done, b_done, eb_done = b.sem("la_done"), b.sem("b_done"), b.sem("eb_done")
        dist_done, dec_done, x_done = b.sem("dist_done"), b.sem("dec_done"), b.sem("x_done")
        g_done, g_out = b.sem("g_done"), b.sem("g_out")
        dend_done, eend_done = b.sem("dend_done"), b.sem("eend_done")
        qe_done, kd_done = b.sem("qe_done"), b.sem("kd_done")
        kd_turned, kdT_done, ends_done = b.sem("kd_turned"), b.sem("kdT_done"), b.sem("ends_done")
        A_stored, qe_stored = [b.sem("A_stored0"), b.sem("A_stored1")], [b.sem("qe_stored0"), b.sem("qe_stored1")]
        kdT_stored = [b.sem("kdT_stored0"), b.sem("kdT_stored1")]

        def levels_of(t):
            return [i for i, w in enumerate(LEVELS) if t < NT_P or 2 * w <= DEC_T]

        level_list = [(t, i) for t in range(NT) for i in levels_of(t)]
        product_list = [(t, i) for t in range(NT) for i in [NL] + levels_of(t)]
        lev_no = {x: n for n, x in enumerate(level_list)}
        g_no = {x: m for m, x in enumerate(product_list)}
        last_lev = {t: lev_no[t, levels_of(t)[-1]] for t in range(NT)}
        last_g = {t: g_no[t, levels_of(t)[-1]] for t in range(NT)}

        units, plan = list(gm.units), []

        def step(*what):
            plan.append(what)

        def unit():
            if units:
                step("unit", units.pop(0))

        def prepare(n, upto):
            if n < len(level_list):
                for what in ("dist", "decay", "operands")[:upto]:
                    step(what, n)

        unit(), step("z", 0), unit(), step("log", 0), step("sums", 0)
        prepare(0, 3), unit(), prepare(1, 3), prepare(2, 2), unit()
        for t in range(NT):
            for x, i in enumerate([NL] + levels_of(t)):
                if x >= 1:
                    prepare(lev_no[t, i] + 3, 2)
                    if lev_no[t, i] + 2 < len(level_list):
                        step("operands", lev_no[t, i] + 2)
                if x == 1:
                    step("from_start", t), step("to_end", t)
                if x == 3:
                    step("decayed", t)
                if x == 4:
                    step("turn", t)
                if t + 1 < NT and x in (2, 3, 4):
                    step({2: "z", 3: "log", 4: "sums"}[x], t + 1)
                step("product", t, i)
                unit()
            step("turned", t), step("store", t)
        while units:
            unit()

        def halves(x, w):
            return x.rearrange("p (n two w) -> p n two w", two=2, w=w)

        with nc.Block() as block:
            @block.sync
            def _(sp):
                def load(t):
                    i, cols = t % 2, slice(t * P, (t + 1) * P)
                    if t >= 2:
                        sp.wait_ge(z_done, t - 1)
                    sp.dma_start(a[0:RANK, i, :], aT[:, cols]).then_inc(in_a[i], 16)
                    if t >= 2:
                        sp.wait_ge(x_done, 2 * (last_lev[t - 2] + 1))
                        sp.wait_ge(kd_done, t - 1)
                        sp.wait_ge(qe_done, t - 1)
                        sp.wait_ge(g_done, g_no[t - 2, NL] + 1)
                    sp.dma_start(q[:, i, :, :], qT[:, cols].rearrange("(h p) n -> p h n", p=P)).then_inc(in_qk[i], 16)
                    sp.dma_start(k[:, i, :, :], kT[:, cols].rearrange("(h p) n -> p h n", p=P)).then_inc(in_qk[i], 16)

                sp.dma_start(wa[0:RANK, :], w_a2).then_inc(wa_in, 16)
                sp.dma_start(wa[RANK:RANK + 1, :], b_a.rearrange("(a n) -> a n", a=1)).then_inc(wa_in, 16)
                sp.wait_ge(ones_done, 1)
                load(0)
                gm.sp_load_w(sp, 1)
                sp.dma_start(start[:, :, :], starts.rearrange("(a r) n -> a r n", a=1).broadcast_to([P, 2, HW])).then_inc(const_in, 16)
                sp.dma_start(mask[:, :, :], masks.rearrange("l s t -> s l t")).then_inc(const_in, 16)
                load(1)
                for kind, x, *_ in plan:
                    if kind == "unit":
                        if x is gm.of[x["c"]][0]:
                            gm.sp_load_w(sp, x["c"] + 2)
                        gm.sp_store(sp, x)
                    elif kind == "store":
                        i, rows = x % 2, slice(x * P, (x + 1) * P)
                        sp.wait_ge(g_out, last_g[x] + 1)
                        sp.dma_start(A_d[rows, :], A[:, i, :]).then_inc(A_stored[i], 16)
                        sp.wait_ge(qe_done, x + 1)
                        sp.dma_start(qe_d[rows, :], qe[:, i, :]).then_inc(qe_stored[i], 16)
                        sp.wait_ge(kdT_done, x + 1)
                        sp.dma_start(kdT_d[rows, :], kdT[:, i, :]).then_inc(kdT_stored[i], 16)
                        if x + 2 < NT:
                            load(x + 2)
                for stored in (A_stored, qe_stored, kdT_stored):
                    sp.wait_ge(stored[0], 16 * ((NT + 1) // 2))
                    sp.wait_ge(stored[1], 16 * (NT // 2))
                gm.sp_end(sp)

            @block.gpsimd
            def _(pool):
                pool.memset(a[:, :, :], 1.0).then_inc(ones_done, 1)
                pool.wait_ge(ones_done, 1)
                gm.pool_w_lo(pool, 1)
                for kind, x, *_ in plan:
                    if kind == "operands":
                        n, (t, i) = x, level_list[x]
                        if i == levels_of(t)[0]:
                            pool.wait_ge(in_qk[t % 2], 32 * (t // 2 + 1))
                        pool.wait_ge(dec_done, n + 1)
                        if n >= XR:
                            pool.wait_ge(g_done, g_no[level_list[n - XR]] + 1)
                        w = LEVELS[i]
                        xs, ds = halves(X[:, n % XR, :], w), halves(dec[:, n % 2, :], w)
                        ks = halves(k[:, t % 2, :, :].rearrange("p h n -> p (h n)"), w)
                        qs = halves(q[:, t % 2, :, :].rearrange("p h n -> p (h n)"), w)
                        pool.tensor_tensor(xs[:, :, 0, :], ks[:, :, 0, :], ds[:, :, 0, :], ALU.mult).then_inc(x_done, 1)
                        pool.tensor_tensor(xs[:, :, 1, :], qs[:, :, 1, :], ds[:, :, 1, :], ALU.mult).then_inc(x_done, 1)
                    elif kind == "decayed":
                        t, i = x, x % 2
                        pool.wait_ge(eb_done, t + 1)
                        if t >= 2:
                            pool.wait_ge(qe_stored[i], 16 * (t // 2))
                        pool.tensor_tensor(qe[:, i, :], q[:, i, :, :].rearrange("p h n -> p (h n)"), e_b[:, :], ALU.mult)\
                            .then_inc(qe_done, 1)
                        pool.wait_ge(eend_done, t + 1)
                        if t >= 1:
                            pool.wait_ge(kd_turned, t)
                        pool.tensor_tensor(kd[:, :], k[:, i, :, :].rearrange("p h n -> p (h n)"), e_end[:, :], ALU.mult)\
                            .then_inc(kd_done, 1)
                    elif kind == "unit" and x is gm.of[x["c"]][-1]:
                        gm.pool_w_lo(pool, x["c"] + 2)

            @block.tensor
            def _(pe):
                for kind, t, *more in plan:
                    if kind == "unit":
                        gm.pe_unit(pe, t)
                    elif kind == "z":
                        if t == 0:
                            pe.wait_ge(wa_in, 32)
                            pe.wait_ge(ones_done, 1)
                        pe.wait_ge(in_a[t % 2], 16 * (t // 2 + 1))
                        if t >= 1:
                            pe.wait_ge(la_done, t)
                        for hd in range(GH):
                            mm = pe.matmul(zp[:, hd * P:(hd + 1) * P], wa[:, hd * P:(hd + 1) * P], a[:, t % 2, :],
                                           start=True, stop=True)
                        mm.then_inc(z_done, 1)
                    elif kind == "product":
                        i, m = more[0], g_no[t, more[0]]
                        if m >= 2:
                            pe.wait_ge(g_out, m - 1)
                        if i == NL:
                            pe.wait_ge(in_qk[t % 2], 32 * (t // 2 + 1))
                        else:
                            pe.wait_ge(x_done, 2 * (lev_no[t, i] + 1))
                        for hd in range(GH):
                            cols = slice(hd * P, (hd + 1) * P)
                            if i == NL:
                                lhs, rhs = k[:, t % 2, hd, :], q[:, t % 2, hd, :]
                            else:
                                lhs = rhs = X[:, lev_no[t, i] % XR, cols]
                            mm = pe.matmul(G[:, m % 2, cols], lhs, rhs, start=True, stop=True)
                        mm.then_inc(g_done, 1)
                    elif kind == "turn":
                        pe.wait_ge(kd_done, t + 1)
                        if t >= 1:
                            pe.wait_ge(kdT_done, t)
                        for hd in range(GH):
                            cols = slice(hd * P, (hd + 1) * P)
                            mm = pe.transpose(tp[:, cols], kd[:, cols], sh.ident[:, :])
                        mm.then_inc(kd_turned, 1)

            @block.scalar
            def _(act):
                gm.act_w_hi(act, 1)
                for kind, t, *_ in plan:
                    if kind == "unit":
                        gm.act_evacuate(act, t)
                        if t is gm.of[t["c"]][-1]:
                            gm.act_w_hi(act, t["c"] + 2)
                    elif kind == "log":
                        act.wait_ge(z_done, t + 1)
                        if t >= 1:
                            act.wait_ge(ez_done, t)
                        act.activation(az[:, :], zp[:, :], ACT.Abs).then_inc(abs_done, 1)
                        act.wait_ge(abs_done, t + 1)
                        if t >= 1:
                            act.wait_ge(lz_done, t)
                        act.activation(ez[:, :], az[:, :], ACT.Exp, scale=-1.0).then_inc(ez_done, 1)
                        act.wait_ge(ez_done, t + 1)
                        if t >= 1:
                            act.wait_ge(la_done, t)
                        act.activation(lz[:, :], ez[:, :], ACT.Ln, bias=1.0).then_inc(lz_done, 1)
                    elif kind == "decay":
                        n = t
                        act.wait_ge(dist_done, 2 * (n + 1))
                        if n >= 2:
                            act.wait_ge(x_done, 2 * (n - 1))
                        act.activation(dec[:, n % 2, :], dist[:, n % 2, :], ACT.Exp, scale=1.0 / TAU).then_inc(dec_done, 1)
                    elif kind == "from_start":
                        act.wait_ge(b_done, t + 1)
                        if t >= 1:
                            act.wait_ge(qe_done, t)
                        act.activation(e_b[:, :], bcum[:, t % 2, :], ACT.Exp, scale=1.0 / TAU).then_inc(eb_done, 1)
                        w = P if t < NT_P else DEC_T
                        act.activation(ends[:, GH * t:GH * t + HW // w], bcum[:, t % 2, w - 1::w], ACT.Exp,
                                       scale=1.0 / TAU).then_inc(ends_done, 1)
                    elif kind == "to_end":
                        act.wait_ge(dend_done, t + 1)
                        if t >= 1:
                            act.wait_ge(kd_done, t)
                        act.activation(e_end[:, :], d_end[:, :], ACT.Exp, scale=1.0 / TAU).then_inc(eend_done, 1)
                    elif kind == "turned":
                        act.wait_ge(kd_turned, t + 1)
                        if t >= 2:
                            act.wait_ge(kdT_stored[t % 2], 16 * (t // 2))
                        act.activation(kdT[:, t % 2, :], tp[:, :], ACT.Copy).then_inc(kdT_done, 1)

            @block.vector
            def _(dve):
                dve.wait_ge(const_in, 16 * 2)
                for kind, t, *more in plan:
                    if kind == "sums":
                        dve.wait_ge(lz_done, t + 1)
                        if t >= 1:
                            dve.wait_ge(b_done, t)
                        dve.scalar_tensor_tensor(la[:, :], zp[:, :], 0.0, lz[:, :], ALU.min, ALU.subtract).then_inc(la_done, 1)
                        dve.wait_ge(la_done, t + 1)
                        if t >= 2:
                            dve.wait_ge(eb_done, t - 1)
                            dve.wait_ge(ends_done, t - 1)
                        dve.tensor_tensor_scan(bcum[:, t % 2, :], start[:, int(t == NT_P), :], la[:, :], 0.0, ALU.mult, ALU.add)\
                            .then_inc(b_done, 1)
                    elif kind == "dist":
                        n, (tt, i) = t, level_list[t]
                        w = LEVELS[i]
                        if i == levels_of(tt)[0]:
                            dve.wait_ge(b_done, tt + 1)
                        if n >= 2:
                            dve.wait_ge(dec_done, n - 1)
                        bs, ds = halves(bcum[:, tt % 2, :], w), halves(dist[:, n % 2, :], w)
                        ref = bs[:, :, 0, w - 1:w].broadcast_to([P, HW // (2 * w), w])
                        dve.tensor_tensor(ds[:, :, 0, :], ref, bs[:, :, 0, :], ALU.subtract).then_inc(dist_done, 1)
                        dve.tensor_tensor(ds[:, :, 1, :], bs[:, :, 1, :], ref, ALU.subtract).then_inc(dist_done, 1)
                    elif kind == "product":
                        i, m = more[0], g_no[t, more[0]]
                        dve.wait_ge(g_done, m + 1)
                        mk = mask[:, i, :].unsqueeze(1).broadcast_to([P, GH, P])
                        g, dst = (z.rearrange("p (h n) -> p h n", h=GH) for z in (G[:, m % 2, :], A[:, t % 2, :]))
                        if i == NL:
                            if t >= 2:
                                dve.wait_ge(A_stored[t % 2], 16 * (t // 2))
                            dve.tensor_tensor(dst, g, mk, ALU.mult).then_inc(g_out, 1)
                        else:
                            dve.wait_ge(g_out, m)
                            dve.copy_predicated(dst, mk.bitcast(U32), g).then_inc(g_out, 1)
                    elif kind == "to_end":
                        if t >= 1:
                            dve.wait_ge(eend_done, t)
                        w = P if t < NT_P else DEC_T
                        bs = bcum[:, t % 2, :].rearrange("p (n w) -> p n w", w=w)
                        ref = bs[:, :, w - 1:w].broadcast_to([P, HW // w, w])
                        dve.tensor_tensor(d_end[:, :].rearrange("p (n w) -> p n w", w=w), ref, bs, ALU.subtract)\
                            .then_inc(dend_done, 1)


def state_phase(nc, name, A_d, qe_d, kdT_d, v, g, ends, b_norm, state, stream_of, o, prompt_state, sample_state):
    HW = GH * P
    R = 3
    with Block(nc, name) as b:
        rows, bn, mhalf = b.sb("rows", [P, DEC_B]), b.sb("bn", [P, DV]), b.sb("mhalf", [P, GH])
        A, qe, kdT = b.sb("A", [P, R, HW]), b.sb("qe", [P, R, HW]), b.sb("kdT", [P, R, HW])
        vt, gt, gate = b.sb("v", [P, R, D]), b.sb("g", [P, R, D]), b.sb("gate", [P, 2, D])
        S, S_in = b.sb("S", [P, 2, GH, DV]), b.sb("S_in", [P, DEC_B, GH, DV])
        qe_s, kd_s = b.sb("qe_s", [P, DEC_B, GH, P]), b.sb("kd_s", [P, 2, HW])
        junk, ss, ms, rstd = b.sb("junk", [P, DV]), b.sb("ss", [P, 2, GH]), b.sb("ms", [P, 2, GH]), b.sb("rstd", [P, 2, GH])
        og = b.sb("og", [P, 2, D])
        op, dS = b.ps("o", [P, 2, GH, DV]), b.ps("dS", [P, 2, GH, DV])
        const_in, sin_in = b.sem("const_in"), b.sem("sin_in")
        att_in, v_in, g_in = ([b.sem(f"{what}_in{i}") for i in range(R)] for what in ("att", "v", "g"))
        mhalf_done, qs_zero = b.sem("mhalf_done"), b.sem("qs_zero")
        sig_done, silu_done, gate_done = b.sem("sig_done"), b.sem("silu_done"), b.sem("gate_done")
        dS_done, S_done, o_done = b.sem("dS_done"), b.sem("S_done"), b.sem("o_done")
        ss_done, ms_done, rstd_done, og_done = b.sem("ss_done"), b.sem("ms_done"), b.sem("rstd_done"), b.sem("og_done")
        qs_done, kds_done = b.sem("qs_done"), b.sem("kds_done")
        o_stored, s_stored = [b.sem("o_stored0"), b.sem("o_stored1")], b.sem("s_stored")

        with nc.Block() as block:
            @block.sync
            def _(sp):
                def load(t):
                    i, rw = t % R, slice(t * P, (t + 1) * P)
                    if t >= R:
                        sp.wait_ge(dS_done, t - R + 1)
                        sp.wait_ge(o_done, t - R + 1)
                    for dst, src in ((kdT, kdT_d), (A, A_d), (qe, qe_d)):
                        sp.dma_start(dst[:, i, :], src[rw, :]).then_inc(att_in[i], 16)
                    sp.dma_start(vt[:, i, :], v[rw, :]).then_inc(v_in[i], 16)
                    if t >= R:
                        sp.wait_ge(silu_done, t - R + 1)
                    sp.dma_start(gt[:, i, :], g[rw, :]).then_inc(g_in[i], 16)

                load(0)
                sp.dma_start(rows[:, :], stream_of).then_inc(const_in, 16)
                sp.dma_start(bn[:, :], bc(b_norm, DV)).then_inc(const_in, 16)
                for t in range(1, R):
                    load(t)
                for s in range(DEC_B):
                    sp.dma_start(S_in[:, s, :, :], state[s].rearrange("h p n -> p h n")).then_inc(sin_in, 16)
                for t in range(NT):
                    if t + R < NT:
                        load(t + R)
                    sp.wait_ge(og_done, GH * (t + 1))
                    sp.dma_start(o[t * P:(t + 1) * P, :], og[:, t % 2, :]).then_inc(o_stored[t % 2], 16)
                    if t == NT_P - 1:
                        sp.wait_ge(S_done, GH * NT_P)
                        sp.dma_start(prompt_state.rearrange("h p n -> p h n"), S[:, (NT_P - 1) % 2, :, :]).then_inc(s_stored, 16)
                for s in range(DEC_B):
                    sp.wait_ge(S_done, GH * (NT_P + s + 1))
                    sp.dma_start(sample_state[s].rearrange("h p n -> p h n"), S_in[:, s, :, :]).then_inc(s_stored, 16)
                sp.wait_ge(o_stored[0], 16 * ((NT + 1) // 2))
                sp.wait_ge(o_stored[1], 16 * (NT // 2))
                sp.wait_ge(s_stored, 16 * (DEC_B + 1))

            @block.gpsimd
            def _(pool):
                pool.memset(mhalf[:, :], -0.5).then_inc(mhalf_done, 1)
                pool.wait_ge(mhalf_done, 1)

                def gates(t):
                    x = gate[:, t % 2, :]
                    pool.wait_ge(sig_done, t + 1)
                    pool.tensor_tensor(x, x, gt[:, t % R, :], ALU.mult).then_inc(silu_done, 1)
                    if t == 0:
                        pool.wait_ge(const_in, 32)
                    pool.wait_ge(silu_done, t + 1)
                    x = x.rearrange("p (h n) -> p h n", h=GH)
                    pool.tensor_tensor(x, x, bn[:, :].unsqueeze(1).broadcast_to([P, GH, DV]), ALU.mult)\
                        .then_inc(gate_done, 1)

                gates(0)
                for t in range(NT):
                    if t + 1 < NT:
                        gates(t + 1)
                    pool.wait_ge(ss_done, GH * (t + 1))
                    if t >= 2:
                        pool.wait_ge(og_done, GH * (t - 1))
                    pool.tensor_scalar(ms[:, t % 2, :], ss[:, t % 2, :], 1.0 / DV, EPS, ALU.mult, ALU.add).then_inc(ms_done, 1)
                    pool.wait_ge(ms_done, t + 1)
                    pool.tensor_tensor(rstd[:, t % 2, :], ms[:, t % 2, :], mhalf[:, :], ALU.pow).then_inc(rstd_done, 1)
                    if t == 1:
                        pool.memset(qe_s[:, :, :, :], 0.0).then_inc(qs_zero, 1)
                    if t == NT_P - 2:
                        pool.wait_ge(qs_zero, 1)
                        pool.wait_ge(att_in[NT_P % R], 48 * (NT_P // R + 1))
                        for s in range(DEC_B):
                            cols = slice(s * DEC_T, (s + 1) * DEC_T)
                            src = qe[:, NT_P % R, :].rearrange("p (h n) -> p h n", h=GH)
                            pool.tensor_copy(qe_s[:, s, :, cols], src[:, :, cols]).then_inc(qs_done, 1)

            @block.tensor
            def _(pe):
                def gains(n, t, keys):
                    if n >= 2:
                        pe.wait_ge(S_done, GH * (n - 1))
                    for hd in range(GH):
                        mm = pe.matmul(dS[:, n % 2, hd, :], keys[:, hd * P:(hd + 1) * P],
                                       vt[:, t % R, hd * DV:(hd + 1) * DV], start=True, stop=True)
                    mm.then_inc(dS_done, 1)

                for t in range(NT):
                    pe.wait_ge(att_in[t % R], 48 * (t // R + 1))
                    pe.wait_ge(v_in[t % R], 16 * (t // R + 1))
                    if t < NT_P:
                        gains(t, t, kdT[:, t % R, :])
                    else:
                        pe.wait_ge(qs_done, DEC_B)
                        pe.wait_ge(sin_in, 16 * DEC_B)
                    if t >= 2:
                        pe.wait_ge(og_done, GH * (t - 1))
                        pe.wait_ge(ss_done, GH * (t - 1))
                    for hd in range(GH):
                        cols, vs = slice(hd * P, (hd + 1) * P), vt[:, t % R, hd * DV:(hd + 1) * DV]
                        mm = pe.matmul(op[:, t % 2, hd, :], A[:, t % R, cols], vs, start=True, stop=(t == 0))
                        if 1 <= t < NT_P:
                            if hd == 0:
                                pe.wait_ge(S_done, GH * t)
                            mm = pe.matmul(op[:, t % 2, hd, :], qe[:, t % R, cols], S[:, (t - 1) % 2, hd, :],
                                           start=False, stop=True)
                        if t == NT_P:
                            for s in range(DEC_B):
                                mm = pe.matmul(op[:, t % 2, hd, :], qe_s[:, s, hd, :], S_in[:, s, hd, :],
                                               start=False, stop=(s == DEC_B - 1))
                    mm.then_inc(o_done, 1)
                for s in range(DEC_B):
                    pe.wait_ge(kds_done, s + 1)
                    gains(NT_P + s, NT_P, kd_s[:, s % 2, :])

            @block.scalar
            def _(act):
                def sigmoid(t):
                    act.wait_ge(g_in[t % R], 16 * (t // R + 1))
                    if t >= 2:
                        act.wait_ge(og_done, GH * (t - 1))
                    act.activation(gate[:, t % 2, :], gt[:, t % R, :], ACT.Sigmoid).then_inc(sig_done, 1)

                sigmoid(0)
                for t in range(NT):
                    if t + 1 < NT:
                        sigmoid(t + 1)
                    act.wait_ge(o_done, t + 1)
                    if t >= 2:
                        act.wait_ge(ms_done, t - 1)
                    for hd in range(GH):
                        n = GH * t + hd
                        if n >= 1:
                            act.wait_ge(ss_done, n)
                        act.activation(junk[:, :], op[:, t % 2, hd, :], ACT.Square, accum_out=ss[:, t % 2, hd:hd + 1])\
                            .then_inc(ss_done, 1)

            @block.vector
            def _(dve):
                def states(t):
                    dve.wait_ge(dS_done, t + 1)
                    if t >= 2:
                        dve.wait_ge(o_done, t)
                    for hd in range(GH):
                        if t == 0:
                            dve.tensor_copy(S[:, 0, hd, :], dS[:, 0, hd, :]).then_inc(S_done, 1)
                        else:
                            if hd == 0:
                                dve.wait_ge(S_done, GH * t)
                            dve.scalar_tensor_tensor(S[:, t % 2, hd, :], S[:, (t - 1) % 2, hd, :],
                                                     ends[:, GH * t + hd:GH * t + hd + 1], dS[:, t % 2, hd, :],
                                                     ALU.mult, ALU.add).then_inc(S_done, 1)

                def post(t):
                    dve.wait_ge(rstd_done, t + 1)
                    dve.wait_ge(gate_done, t + 1)
                    if t >= 2:
                        dve.wait_ge(o_stored[t % 2], 16 * (t // 2))
                    for hd in range(GH):
                        cols = slice(hd * DV, (hd + 1) * DV)
                        dve.scalar_tensor_tensor(og[:, t % 2, cols], op[:, t % 2, hd, :], rstd[:, t % 2, hd:hd + 1],
                                                 gate[:, t % 2, cols], ALU.mult, ALU.mult).then_inc(og_done, 1)

                def keys_of(s):
                    if s >= 2:
                        dve.wait_ge(dS_done, NT_P + s - 1)
                    dve.tensor_scalar(kd_s[:, s % 2, :], kdT[:, NT_P % R, :], rows[:, s:s + 1], None, ALU.mult)\
                        .then_inc(kds_done, 1)

                for t in range(NT_P):
                    states(t)
                    if t >= 1:
                        post(t - 1)
                post(NT_P - 1)
                dve.wait_ge(const_in, 32)
                dve.wait_ge(att_in[NT_P % R], 48 * (NT_P // R + 1))
                keys_of(0)
                keys_of(1)
                post(NT_P)
                for s in range(DEC_B):
                    dve.wait_ge(dS_done, NT_P + s + 1)
                    dve.wait_ge(o_done, NT)
                    for hd in range(GH):
                        c = GH * NT_P + hd * DEC_B + s
                        dve.scalar_tensor_tensor(S_in[:, s, hd, :], S_in[:, s, hd, :], ends[:, c:c + 1],
                                                 dS[:, (NT_P + s) % 2, hd, :], ALU.mult, ALU.add).then_inc(S_done, 1)
                    if s + 2 < DEC_B:
                        keys_of(s + 2)


def level_masks():
    s, t = np.arange(P)[:, None], np.arange(P)[None, :]
    ms = [(s // (2 * w) == t // (2 * w)) & (s % (2 * w) < w) & (t % (2 * w) >= w) for w in LEVELS]
    return np.stack(ms + [s == t]).astype(np.float32)


def scan_starts():
    c = np.arange(GH * P)
    return np.stack([c % P != 0, c % DEC_T != 0]).astype(np.float32)


def stream_rows():
    return (np.arange(P)[:, None] // DEC_T == np.arange(DEC_B)[None, :]).astype(np.float32)


def encoder(nc, x_prompt, x_sample, cache_k, cache_v, cache_kidx, state_gla, norm_mix, norm_ffn, norm_final,
            a_w_in, a_w_o, b_w_in, b_w_a2, b_b_a, b_norm, b_w_o, ffn_w_up, ffn_w_down,
            ident_table, same_frame, masks, starts, stream_of,
            y_prompt, y_sample, k_prompt, v_prompt, kidx_prompt, gla_prompt,
            k_sample, v_sample, kidx_sample, gla_sample):
    xp, xs = x_prompt[0], x_sample.rearrange("b t d -> (b t) d")
    yp, ys = y_prompt[0], y_sample.rearrange("b t d -> (b t) d")

    def flat(ap, pattern):
        return ap.rearrange(pattern)

    k_p, v_p = (flat(z[0, 0], "s h d -> s (h d)") for z in (k_prompt, v_prompt))
    k_s, v_s = (flat(z[0], "b t h d -> (b t) (h d)") for z in (k_sample, v_sample))
    ki_p, ki_s = kidx_prompt[0, 0], flat(kidx_sample[0], "b t d -> (b t) d")
    c_k, c_v = (flat(z[0], "b s h d -> b s (h d)") for z in (cache_k, cache_v))
    def dram(name, rows, cols):
        return nc.dram_tensor(name, (rows, cols), F32, kind="Internal").ap()

    qT, qiT, wt, o = dram("qT", D, TOK), dram("qiT", IH * ID, TOK), dram("wt", TOK, IH), dram("o", TOK, D)
    gq, gk, ga = dram("gq", GH * DK, TOK), dram("gk", GH * DK, TOK), dram("ga", RANK, TOK)
    gv, gg, go, hd = dram("gv", TOK, D), dram("gg", TOK, D), dram("go", TOK, D), dram("hd", TOK, D)
    A_d, qe_d, kdT_d = dram("A", TOK, GH * P), dram("qe", TOK, GH * P), dram("kdT", TOK, GH * P)

    def either(p, s):
        return lambda t: p[t * P:(t + 1) * P, :] if t < NT_P else s[:, :]

    def to_T(dst, r0, cols=CW):
        return lambda u: [(dst[r0 + u["j"]:r0 + u["j"] + u["m"], u["g"] * GW:(u["g"] + 1) * GW],
                           lambda s, m=u["m"]: s[0:m, :])]

    def to_N(tile, c0=0, n=CW, s0=0):
        return lambda u: [(tile(u["t"])[:, c0:c0 + n], lambda s: s[:, s0:s0 + n])]

    def both(f, g):
        return lambda u: f(u) + g(u)

    def chunk(w, c0, n, form, op, out):
        return dict(w=w[:, c0:c0 + n], form=form, op=op, out=out)

    with ExitStack() as ctx:
        ident = ctx.enter_context(nc.sbuf_tensor("ident", [P, P], F32))
        ident_in = ctx.enter_context(nc.semaphore("ident_in"))
        with nc.Block() as block:
            @block.sync
            def _(sp):
                sp.dma_start(ident[:, :], ident_table).then_inc(ident_in, 16)
                sp.wait_ge(ident_in, 16)

        tile_of = lambda d: (lambda t: d[t * P:(t + 1) * P, :])

        QW, KW, IW = HEADS * HD, KVH * HD, IH * ID
        w0 = a_w_in[0]
        tail = A_IN - CW
        first = [chunk(w0, tail, CW, "N", "copy",
                       both(to_N(either(ki_p, ki_s), 0, ID, CW - IH - ID), to_N(tile_of(wt), 0, IH, CW - IH)))]
        first += [chunk(w0, QW + 2 * KW + c, CW, "T", "copy", to_T(qiT, c)) for c in range(0, IW, CW)]
        rest = [chunk(w0, QW, CW, "N", "copy", to_N(either(k_p, k_s))),
                chunk(w0, QW + KW, CW, "N", "copy", to_N(either(v_p, v_s)))]
        rest += [chunk(w0, c, CW, "T", HD ** -0.5, to_T(qT, c)) for c in range(0, QW, CW)]
        with ExitStack() as scope:
            score = scope.enter_context(nc.sbuf_tensor("score", [P, SCORE_AT[NT_P]], F32))
            with ExitStack() as inner:
                sh = Shared(nc, inner, "proj0", ident)
                gemm_phase(nc, "proj0a", sh, first, src_dram=either(xp, xs), gamma=norm_mix[0], next_w=rest[0]["w"])
                project_and_score_phase(nc, "proj0b", sh, rest, True, len(first) % 2, qiT, wt, ki_p, score)
            prompt_attention_phase(nc, "att", ident, qT, k_p, v_p, score, o)
        sample_attention_phase(nc, "satt", ident, qT, qiT, wt, c_k, c_v, cache_kidx[0], k_s, v_s, ki_s, same_frame, o)

        w1 = b_w_in[0]
        HK = GH * DK
        first = [chunk(w1, c, CW, "T", DK ** -0.5, to_T(gq, c)) for c in range(0, HK, CW)]
        first += [chunk(w1, HK + c, CW, "T", "copy", to_T(gk, c)) for c in range(0, HK, CW)]
        first += [chunk(w1, 2 * HK + 2 * D, RANK, "T", "copy", to_T(ga, 0))]
        rest = [chunk(w1, 2 * HK + c, CW, "N", "copy", to_N(tile_of(gv), c)) for c in range(0, D, CW)]
        rest += [chunk(w1, 2 * HK + D + c, CW, "N", "copy", to_N(tile_of(gg), c)) for c in range(0, D, CW)]
        with ExitStack() as gla:
            ends = gla.enter_context(nc.sbuf_tensor("ends", [P, GH * (NT_P + DEC_B)], F32))
            with ExitStack() as scope:
                sh = Shared(nc, scope, "mid", ident)
                with ExitStack() as inner:
                    h = inner.enter_context(nc.sbuf_tensor("h0", [P, NT, D], F32))
                    gemm_phase(nc, "out0", sh, [chunk(a_w_o[0], c, CW, "N", "resid", None) for c in range(0, D, CW)],
                               src_dram=tile_of(o), residual=either(xp, xs), h=h, next_w=ffn_w_up[0][:, 0:CW],
                               next_gamma=norm_ffn[0])
                    mlp_phase(nc, "mlp0", sh, h, ffn_w_up[0], ffn_w_down[0], norm_mix[1], next_w=first[0]["w"])
                    gemm_phase(nc, "proj1a", sh, first, preset=True, next_w=rest[0]["w"],
                               spill=[(tile_of(hd)(t), h[:, t, :]) for t in range(NT)])
                project_and_level_phase(nc, "proj1b", sh, rest, len(first) % 2, gq, gk, ga, b_w_a2[0], b_b_a[0],
                                        masks, starts, ends, A_d, qe_d, kdT_d)
            state_phase(nc, "state", A_d, qe_d, kdT_d, gv, gg, ends, b_norm[0], state_gla[0], stream_of, go,
                        gla_prompt[0, 0], gla_sample[0])
        with ExitStack() as scope:
            sh = Shared(nc, scope, "end", ident)
            h = scope.enter_context(nc.sbuf_tensor("h1", [P, NT, D], F32))
            gemm_phase(nc, "out1", sh, [chunk(b_w_o[0], c, CW, "N", "resid", None) for c in range(0, D, CW)],
                       src_dram=tile_of(go), residual=tile_of(hd), h=h, next_w=ffn_w_up[1][:, 0:CW],
                       next_gamma=norm_ffn[1])
            mlp_phase(nc, "mlp1", sh, h, ffn_w_up[1], ffn_w_down[1], norm_final, y=either(yp, ys))


INPUTS = ["x_prompt", "x_sample", "cache_k", "cache_v", "cache_kidx", "state_gla", "norm_mix", "norm_ffn",
          "norm_final", "a_w_in", "a_w_o", "b_w_in", "b_w_a2", "b_b_a", "b_norm", "b_w_o", "ffn_w_up", "ffn_w_down"]
OUTPUTS = [(1, SEQ, D), (DEC_B, DEC_T, D), (1, 1, SEQ, KVH, HD), (1, 1, SEQ, KVH, HD), (1, 1, SEQ, ID),
           (1, 1, GH, DK, DV), (1, DEC_B, DEC_T, KVH, HD), (1, DEC_B, DEC_T, KVH, HD), (1, DEC_B, DEC_T, ID),
           (1, DEC_B, GH, DK, DV)]


def kernel(**inputs):
    import concourse.bacc as bacc
    from concourse.bass_utils import run_bass_kernel_spmd

    nc = bacc.Bacc("TRN2", target_bir_lowering=False, num_devices=1)
    arrays = {name: np.ascontiguousarray(inputs[name]) for name in INPUTS}
    arrays |= {"ident": np.eye(P, dtype=np.float32), "same_frame": same_frame_table(), "level_masks": level_masks(),
               "scan_starts": scan_starts(), "stream_rows": stream_rows()}
    feed = {f"in_{name}": a for name, a in arrays.items()}
    args = [nc.dram_tensor(name, a.shape, mybir.dt.from_np(a.dtype), kind="ExternalInput").ap()
            for name, a in feed.items()]
    args += [nc.dram_tensor(f"out_{i}", shape, F32, kind="ExternalOutput").ap() for i, shape in enumerate(OUTPUTS)]
    encoder(nc, *args)
    r = run_bass_kernel_spmd(nc, [feed], core_ids=[0])
    return tuple(r.results[0][f"out_{i}"] for i in range(len(OUTPUTS)))
```

```python
from contextlib import ExitStack

import numpy as np

import concourse.bass as bass
from concourse import mybir

F32 = mybir.dt.float32
F32R = mybir.dt.float32r
U32 = mybir.dt.uint32
ACT = mybir.ActivationFunctionType
ALU = mybir.AluOpType
AX = mybir.AxisListType

P = 128
D = 1024
KB = D // P
SEQ, DEC_B, DEC_T, PAST = 1024, 8, 16, 512
NT_P = SEQ // P
NT = NT_P + 1
TOK = NT * P
GRP = 3
NG = NT // GRP
GW = GRP * P
HEADS, KVH, HD = 16, 4, 64
IH, ID = 8, 64
TOPK_P, TOPK_S = 256, (PAST + DEC_T) // 4
CHUNK = 64
A_IN = HEADS * HD + 2 * KVH * HD + IH * ID + ID + IH
GH, DK, DV, RANK = 4, 128, 256, 16
TAU = 16.0
B_IN = 2 * GH * DK + GH * DV + D + RANK
FF = 4 * D
CW = 256
EPS = 1e-6
FILL = -3.0e38
MARK = -3.2e38
CUT = -3.1e38
NEG = -1.0e30
LEVELS = (64, 32, 16, 8, 4, 2, 1)


def bc(ap, n):
    return ap.rearrange("(a n) -> a n", a=1).broadcast_to([P, n])


class Block:

    def __init__(self, nc, name):
        self.nc, self.name, self.ctx, self.sems = nc, name, ExitStack(), []

    def __enter__(self):
        self.ctx.__enter__()
        return self

    def __exit__(self, *a):
        if a[0] is None:
            self.nc.clear_and_free_semaphores(self.sems)
            self.nc.all_engine_barrier()
        return self.ctx.__exit__(*a)

    def sb(self, name, shape, dt=F32):
        return self.ctx.enter_context(self.nc.sbuf_tensor(f"{self.name}_{name}", shape, dt))

    def ps(self, name, shape, dt=F32):
        return self.ctx.enter_context(self.nc.psum_tensor(f"{self.name}_{name}", shape, dt))

    def sem(self, name):
        self.sems.append(self.nc.alloc_semaphore(f"{self.name}_{name}"))
        return self.sems[-1]


class Shared:

    def __init__(self, nc, ctx, name, ident, weights=True):
        def sb(what, shape, dt=F32):
            return ctx.enter_context(nc.sbuf_tensor(f"{name}_{what}", shape, dt))

        self.ident, self.sb = ident, sb
        self.xhi, self.xlo = sb("xT_hi", [P, KB, TOK], F32R), sb("xT_lo", [P, KB, TOK], F32R)
        if weights:
            self.add_weights()

    def add_weights(self):
        sb = self.sb
        self.raw = sb("w_raw", [P, 2, KB, CW])
        self.whi, self.wlo = sb("w_hi", [P, 2, KB, CW], F32R), sb("w_lo", [P, 2, KB, CW], F32R)


class TokenStage:

    XS = 4

    def __init__(self, b, sh, tag="", src_dram=None, src_sb=None, ready=None, gamma=None, y=None):
        self.b, self.sh, self.src_dram, self.src_sb, self.gamma, self.y = b, sh, src_dram, src_sb, gamma, y
        self.ready = ready
        self.normed = gamma is not None
        self.tile_in = [b.sem(f"{tag}tile_in{i}") for i in range(self.XS)]
        if src_dram is not None:
            self.x = b.sb(tag + "x_in", [P, self.XS, D])
        if y is None:
            self.psT = b.ps(tag + "psT", [P, 2, 512])
        else:
            self.stored = [b.sem(tag + "y_stored0"), b.sem(tag + "y_stored1")]
        if self.normed:
            self.junk = b.sb(tag + "sq_junk", [P, D])
            self.g = b.sb(tag + "gamma", [P, D])
            self.ss, self.ms, self.rstd = b.sb(tag + "sumsq", [P, NT]), b.sb(tag + "meansq", [P, NT]), b.sb(tag + "rstd", [P, NT])
            self.mhalf = b.sb(tag + "mhalf", [P, 1])
            self.u = b.sb(tag + "u", [P, 2, D])
            self.gamma_in, self.sumsq_ready = b.sem(tag + "gamma_in"), b.sem(tag + "sumsq_ready")
            self.mhalf_ready, self.ms_ready, self.rstd_ready = b.sem(tag + "mhalf_ready"), b.sem(tag + "ms_ready"), b.sem(tag + "rstd_ready")
            self.u_ready = b.sem(tag + "u_ready")
        self.t_done, self.hi_done, self.lo_done = b.sem(tag + "t_done"), b.sem(tag + "thi_done"), b.sem(tag + "tlo_done")

    def tile(self, t):
        if callable(self.src_sb):
            return self.src_sb(t)
        return self.src_sb[:, t, :] if self.src_sb is not None else self.x[:, t % self.XS, :]

    def wait_tile(self, e, t):
        if self.src_sb is None:
            e.wait_ge(self.tile_in[t % self.XS], 16 * (t // self.XS + 1))
        else:
            self.ready(e, t)

    def load_gamma(self, e):
        if self.normed:
            e.dma_start(self.g[:, :], bc(self.gamma, D)).then_inc(self.gamma_in, 16)

    def load(self, e, t):
        if t >= self.XS:
            if self.normed:
                e.wait_ge(self.u_ready, t - self.XS + 1)
            else:
                e.wait_ge(self.t_done, 2 * (t - self.XS + 1))
        e.dma_start(self.x[:, t % self.XS, :], self.src_dram(t)).then_inc(self.tile_in[t % self.XS], 16)

    def act_sumsq(self, e, t):
        if self.normed:
            self.wait_tile(e, t)
            if t >= 1:
                e.wait_ge(self.sumsq_ready, t)
            e.activation(self.junk[:, :], self.tile(t), ACT.Square, accum_out=self.ss[:, t:t + 1])\
                .then_inc(self.sumsq_ready, 1)

    def act_hi(self, e, t):
        for half in range(2):
            e.wait_ge(self.t_done, 2 * t + half + 1)
            e.activation(self.sh.xhi[:, 4 * half:4 * half + 4, t * P:(t + 1) * P],
                         self.psT[:, half, :].rearrange("p (k c) -> p k c", k=4), ACT.Copy).then_inc(self.hi_done, 1)

    def pool_consts(self, e):
        if self.normed:
            e.memset(self.mhalf[:, :], -0.5).then_inc(self.mhalf_ready, 1)
            e.wait_ge(self.mhalf_ready, 1)

    def pool_rstd(self, e, t):
        if self.normed:
            e.wait_ge(self.sumsq_ready, t + 1)
            e.tensor_scalar(self.ms[:, t:t + 1], self.ss[:, t:t + 1], 1.0 / D, EPS, ALU.mult, ALU.add)\
                .then_inc(self.ms_ready, 1)
            e.wait_ge(self.ms_ready, t + 1)
            e.tensor_tensor(self.rstd[:, t:t + 1], self.ms[:, t:t + 1], self.mhalf[:, :], ALU.pow)\
                .then_inc(self.rstd_ready, 1)

    def dve_norm(self, e, t):
        if self.normed:
            if t == 0:
                e.wait_ge(self.gamma_in, 16)
            if t >= 2:
                if self.y is None:
                    e.wait_ge(self.t_done, 2 * (t - 1))
                else:
                    e.wait_ge(self.stored[t % 2], 16 * (t // 2))
            self.wait_tile(e, t)
            e.wait_ge(self.rstd_ready, t + 1)
            e.scalar_tensor_tensor(self.u[:, t % 2, :], self.tile(t), self.rstd[:, t:t + 1], self.g[:, :],
                                   ALU.mult, ALU.mult).then_inc(self.u_ready, 1)

    def dve_lo(self, e, t):
        for half in range(2):
            e.wait_ge(self.hi_done, 2 * t + half + 1)
            cols = slice(t * P, (t + 1) * P)
            e.tensor_tensor(self.sh.xlo[:, 4 * half:4 * half + 4, cols],
                            self.psT[:, half, :].rearrange("p (k c) -> p k c", k=4),
                            self.sh.xhi[:, 4 * half:4 * half + 4, cols].bitcast(F32), ALU.subtract).then_inc(self.lo_done, 1)

    def pe_transpose(self, e, t):
        if self.normed:
            e.wait_ge(self.u_ready, t + 1)
        else:
            self.wait_tile(e, t)
        src = self.u[:, t % 2, :] if self.normed else self.tile(t)
        for half in range(2):
            if t >= 1:
                e.wait_ge(self.lo_done, 2 * t + half - 1)
            for k in range(4):
                kk = 4 * half + k
                mm = e.transpose(self.psT[:, half, k * P:(k + 1) * P], src[:, kk * P:(kk + 1) * P], self.sh.ident[:, :])
            mm.then_inc(self.t_done, 1)

    def sp_store(self, e, t):
        e.wait_ge(self.u_ready, t + 1)
        e.dma_start(self.y(t), self.u[:, t % 2, :]).then_inc(self.stored[t % 2], 16)

    def sp_stored(self, e):
        e.wait_ge(self.stored[0], 16 * ((NT + 1) // 2))
        e.wait_ge(self.stored[1], 16 * (NT // 2))

    def wait_ready(self, e, tiles):
        e.wait_ge(self.lo_done, 2 * tiles)


TERMS = ((0, 0), (0, 1), (1, 0))


class Gemm:

    NB = 4

    def __init__(self, b, sh, chunks, preset, slot0=0, h=None, residual=None, next_w=None):
        self.b, self.sh, self.chunks, self.preset, self.h, self.residual = b, sh, chunks, preset, h, residual
        self.next_w, self.slot0 = next_w, slot0
        NB = self.NB
        self.acc = b.ps("acc", [P, NB, 512])
        if any(c["out"] for c in chunks):
            self.stage = b.sb("stage", [P, NB, GW])
        self.w_in = [b.sem("w_in0"), b.sem("w_in1")]
        self.whi_done, self.wlo_done = b.sem("whi_done"), b.sem("wlo_done")
        self.unit_done, self.unit_out = b.sem("unit_done"), b.sem("unit_out")
        if any(c["op"] == "silu" for c in chunks):
            self.sig, self.sig_done = b.sb("sigmoid", [P, NB, CW]), b.sem("sig_done")
        self.stored = [b.sem(f"stored{i}") for i in range(NB)]
        self.res_in = [b.sem(f"res_in{i}") for i in range(NB)]
        if residual is not None:
            self.res = b.sb("residual", [P, NB, CW])
        self.units = units = []
        for ci, c in enumerate(chunks):
            M = c["w"].shape[1]
            us = []
            for g in range(NG):
                if c["form"] == "T":
                    us += [dict(c=ci, g=g, j=j, m=min(P, M - j), n=GW) for j in range(0, M, P)]
                else:
                    us += [dict(c=ci, g=g, t=t, m=P, n=M) for t in range(GRP * g, GRP * g + GRP)]
            for u in us:
                u["i"], u["op"], u["form"] = len(units), c["op"], c["form"]
                u["stores"] = c["out"](u) if c["out"] else []
                units.append(u)
        for x, u in enumerate(u for u in units if u["op"] == "silu"):
            u["sig_before"] = x
        self.of = [[u for u in units if u["c"] == ci] for ci in range(len(chunks))]
        self.n_stores = []
        for s in range(NB):
            n = 0
            for u in units[s::NB]:
                u["stored_before"] = n
                n += 16 * len(u["stores"])
            self.n_stores.append(n)

    def slot(self, ci):
        return (self.slot0 + ci) % 2

    def width(self, ci):
        return CW if ci == len(self.chunks) else self.chunks[ci]["w"].shape[1]

    def loads_before(self, ci):
        return ci // 2 - (self.preset and ci % 2 == 0)

    def splits(self, ci):
        return ci + 1 - self.preset

    def sp_load_w(self, sp, ci):
        if ci > len(self.chunks) or (ci == len(self.chunks) and self.next_w is None):
            return
        src = self.next_w if ci == len(self.chunks) else self.chunks[ci]["w"]
        if ci >= 2 and self.splits(ci - 2) > 0:
            sp.wait_ge(self.wlo_done, self.splits(ci - 2))
        sp.dma_start(self.sh.raw[:, self.slot(ci), :, 0:self.width(ci)], src.rearrange("(k p) n -> p k n", p=P))\
            .then_inc(self.w_in[ci % 2], 16)

    def act_w_hi(self, act, ci):
        if ci > len(self.chunks) or (ci == len(self.chunks) and self.next_w is None):
            return
        M = self.width(ci)
        act.wait_ge(self.w_in[ci % 2], 16 * (self.loads_before(ci) + 1))
        if ci >= 2:
            act.wait_ge(self.unit_done, self.of[ci - 2][-1]["i"] + 1)
        act.activation(self.sh.whi[:, self.slot(ci), :, 0:M], self.sh.raw[:, self.slot(ci), :, 0:M], ACT.Copy).then_inc(self.whi_done, 1)

    def pool_w_lo(self, pool, ci):
        if ci > len(self.chunks) or (ci == len(self.chunks) and self.next_w is None):
            return
        M = self.width(ci)
        pool.wait_ge(self.whi_done, self.splits(ci))
        pool.tensor_tensor(self.sh.wlo[:, self.slot(ci), :, 0:M], self.sh.raw[:, self.slot(ci), :, 0:M],
                           self.sh.whi[:, self.slot(ci), :, 0:M].bitcast(F32), ALU.subtract).then_inc(self.wlo_done, 1)

    def sp_load_res(self, sp, u):
        if self.residual is not None:
            if u["i"] >= self.NB:
                sp.wait_ge(self.unit_out, u["i"] - self.NB + 1)
            c0 = u["c"] * CW
            sp.dma_start(self.res[:, u["i"] % self.NB, :], self.residual(u["t"])[:, c0:c0 + CW])\
                .then_inc(self.res_in[u["i"] % self.NB], 16)

    def sp_store(self, sp, u):
        if u["stores"]:
            sp.wait_ge(self.unit_out, u["i"] + 1)
        for dst, view in u["stores"]:
            sp.dma_start(dst, view(self.stage[:, u["i"] % self.NB, :])).then_inc(self.stored[u["i"] % self.NB], 16)

    def sp_chunks(self, sp):
        for u in self.units[:self.NB]:
            self.sp_load_res(sp, u)
        for ci in range(len(self.chunks)):
            self.sp_load_w(sp, ci + 2)
            for u in self.of[ci]:
                self.sp_store(sp, u)
                if u["i"] + self.NB < len(self.units):
                    self.sp_load_res(sp, self.units[u["i"] + self.NB])

    def sp_end(self, sp):
        for s in range(self.NB):
            if self.n_stores[s]:
                sp.wait_ge(self.stored[s], self.n_stores[s])

    def pe_unit(self, pe, u):
        i, NB = u["i"], self.NB
        if u is self.of[u["c"]][0] and self.splits(u["c"]) > 0:
            pe.wait_ge(self.wlo_done, self.splits(u["c"]))
        if i >= NB:
            pe.wait_ge(self.unit_out, i - NB + 1)
        s, last, n = self.slot(u["c"]), KB * len(TERMS) - 1, 0
        w, x = (self.sh.whi, self.sh.wlo), (self.sh.xhi, self.sh.xlo)
        for k in range(KB):
            for a, c in TERMS:
                if u["form"] == "T":
                    mm = pe.matmul(self.acc[0:u["m"], i % NB, 0:GW], w[a][:, s, k, u["j"]:u["j"] + u["m"]],
                                   x[c][:, k, u["g"] * GW:(u["g"] + 1) * GW], start=(n == 0), stop=(n == last))
                else:
                    mm = pe.matmul(self.acc[:, i % NB, 0:u["n"]], x[c][:, k, u["t"] * P:(u["t"] + 1) * P],
                                   w[a][:, s, k, 0:u["n"]], start=(n == 0), stop=(n == last))
                n += 1
        mm.then_inc(self.unit_done, 1)

    def wait_unit(self, e, u):
        i, NB = u["i"], self.NB
        e.wait_ge(self.unit_done, i + 1)
        if i >= NB:
            e.wait_ge(self.unit_out, i - NB + 1)
        if u["stored_before"]:
            e.wait_ge(self.stored[i % NB], u["stored_before"])

    def act_evacuate(self, act, u):
        self.wait_unit(act, u)
        m, n, s = u["m"], u["n"], u["i"] % self.NB
        scale = 1.0 if u["op"] == "copy" else u["op"]
        act.activation(self.stage[0:m, s, 0:n], self.acc[0:m, s, 0:n], ACT.Copy, scale=scale).then_inc(self.unit_out, 1)

    def act_sigmoid(self, act, u):
        i, s = u["i"], u["i"] % self.NB
        act.wait_ge(self.unit_done, i + 1)
        if i >= self.NB:
            act.wait_ge(self.unit_out, i - self.NB + 1)
        act.activation(self.sig[:, s, 0:u["n"]], self.acc[:, s, 0:u["n"]], ACT.Sigmoid).then_inc(self.sig_done, 1)

    def dve_evacuate(self, dve, u):
        self.wait_unit(dve, u)
        i, m, n, s = u["i"], u["m"], u["n"], u["i"] % self.NB
        src = self.acc[0:m, s, 0:n]
        if u["op"] == "resid":
            cols = self.h[:, u["t"], u["c"] * CW:u["c"] * CW + n]
            if self.residual is not None:
                dve.wait_ge(self.res_in[s], 16 * (i // self.NB + 1))
                dve.tensor_tensor(cols, src, self.res[:, s, 0:n], ALU.add).then_inc(self.unit_out, 1)
            else:
                dve.tensor_tensor(cols, src, cols, ALU.add).then_inc(self.unit_out, 1)
        elif u["op"] == "silu":
            dve.wait_ge(self.sig_done, u["sig_before"] + 1)
            dve.tensor_tensor(self.stage[0:m, s, 0:n], src, self.sig[0:m, s, 0:n], ALU.mult).then_inc(self.unit_out, 1)
        elif u["op"] == "copy":
            dve.tensor_copy(self.stage[0:m, s, 0:n], src).then_inc(self.unit_out, 1)
        else:
            dve.tensor_scalar(self.stage[0:m, s, 0:n], src, u["op"], None, ALU.mult).then_inc(self.unit_out, 1)


def gemm_phase(nc, name, sh, chunks, preset=False, slot0=0, src_dram=None, gamma=None, residual=None, h=None, next_w=None,
               next_gamma=None, spill=()):
    with Block(nc, name) as b:
        st = tail = None
        gm = Gemm(b, sh, chunks, preset, slot0, h, residual, next_w)
        if src_dram is not None:
            st = TokenStage(b, sh, src_dram=src_dram, gamma=gamma)
        if next_gamma is not None:
            last = {u["t"]: u for u in gm.of[-1]}
            tail = TokenStage(b, sh, tag="next_", src_sb=h, ready=lambda e, t: e.wait_ge(gm.unit_out, last[t]["i"] + 1),
                              gamma=next_gamma)
        spilled = b.sem("spilled") if spill else None
        NCH = len(chunks)
        head_units = gm.of[0] if st is not None else []
        body_units = [u for u in gm.units if not (st is not None and u["c"] == 0) and not (tail and u["c"] == NCH - 1)]
        tail_units = gm.of[-1] if tail else []

        with nc.Block() as block:
            @block.sync
            def _(sp):
                if st:
                    st.load(sp, 0)
                    st.load_gamma(sp)
                    st.load(sp, 1)
                    st.load(sp, 2)
                if not preset:
                    gm.sp_load_w(sp, 0)
                if st:
                    for t in range(3, 6):
                        st.load(sp, t)
                if NCH > 1 or next_w is not None:
                    gm.sp_load_w(sp, 1)
                if st:
                    for t in range(6, NT):
                        st.load(sp, t)
                if tail:
                    tail.load_gamma(sp)
                for dst, src in spill:
                    sp.dma_start(dst, src).then_inc(spilled, 16)
                gm.sp_chunks(sp)
                gm.sp_end(sp)
                if spill:
                    sp.wait_ge(spilled, 16 * len(spill))

            @block.scalar
            def _(act):
                if st:
                    for t in range(NT):
                        st.act_sumsq(act, t)
                        if t >= 1:
                            st.act_hi(act, t - 1)
                        if t == 3 and not preset:
                            gm.act_w_hi(act, 0)
                    st.act_hi(act, NT - 1)
                elif not preset:
                    gm.act_w_hi(act, 0)
                for ci in range(1, NCH + 1):
                    gm.act_w_hi(act, ci)
                    if chunks[ci - 1]["op"] == "silu":
                        for u in gm.of[ci - 1]:
                            gm.act_sigmoid(act, u)
                if tail:
                    for t in range(NT):
                        tail.act_sumsq(act, t)
                        if t >= 2:
                            tail.act_hi(act, t - 2)
                    tail.act_hi(act, NT - 2)
                    tail.act_hi(act, NT - 1)

            @block.gpsimd
            def _(pool):
                if st:
                    st.pool_consts(pool)
                    for t in range(NT):
                        st.pool_rstd(pool, t)
                        if t == 4 and not preset:
                            gm.pool_w_lo(pool, 0)
                elif not preset:
                    gm.pool_w_lo(pool, 0)
                for ci in range(1, NCH + 1):
                    gm.pool_w_lo(pool, ci)
                if tail:
                    tail.pool_consts(pool)
                    for t in range(NT):
                        tail.pool_rstd(pool, t)

            @block.tensor
            def _(pe):
                if st:
                    for t in range(NT):
                        st.pe_transpose(pe, t)
                        if t % GRP == GRP - 1 and t >= 2 * GRP - 1:
                            g = t // GRP - 1
                            st.wait_ready(pe, GRP * (g + 1))
                            for u in head_units:
                                if u["g"] == g:
                                    gm.pe_unit(pe, u)
                    st.wait_ready(pe, NT)
                    for u in head_units:
                        if u["g"] == NG - 1:
                            gm.pe_unit(pe, u)
                for u in body_units:
                    gm.pe_unit(pe, u)
                for u in tail_units:
                    gm.pe_unit(pe, u)
                    if u["t"] >= 2:
                        tail.pe_transpose(pe, u["t"] - 2)
                if tail:
                    tail.pe_transpose(pe, NT - 2)
                    tail.pe_transpose(pe, NT - 1)

            @block.vector
            def _(dve):
                if st:
                    for t in range(NT):
                        st.dve_norm(dve, t)
                        if t >= 1:
                            st.dve_lo(dve, t - 1)
                        if t % GRP == 0 and t >= 2 * GRP:
                            for u in head_units:
                                if u["g"] == t // GRP - 2:
                                    gm.dve_evacuate(dve, u)
                    st.dve_lo(dve, NT - 1)
                    for u in head_units:
                        if u["g"] >= NG - 2:
                            gm.dve_evacuate(dve, u)
                for u in body_units:
                    gm.dve_evacuate(dve, u)
                for u in tail_units:
                    gm.dve_evacuate(dve, u)
                    if u["t"] >= 1:
                        tail.dve_norm(dve, u["t"] - 1)
                    if u["t"] >= 2:
                        tail.dve_lo(dve, u["t"] - 2)
                if tail:
                    tail.dve_norm(dve, NT - 1)
                    tail.dve_lo(dve, NT - 2)
                    tail.dve_lo(dve, NT - 1)


def mlp_phase(nc, name, sh, h, w_up, w_down, next_gamma, next_w=None, y=None):
    NCH = FF // CW
    FB = CW // P
    UU = NG * FB
    DU = NT * (D // 512)
    with Block(nc, name) as b:
        up_raw, up_hi, up_lo = (z[:, 0, :, :] for z in (sh.raw, sh.whi, sh.wlo))
        dn_raw, dn_hi, dn_lo = (z[:, 1, :, :].rearrange("p k c -> p (k c)").rearrange("p (f n) -> p f n", f=FB)
                                for z in (sh.raw, sh.whi, sh.wlo))
        hid_hi, hid_lo = b.sb("hid_hi", [P, FB, TOK], F32R), b.sb("hid_lo", [P, FB, TOK], F32R)
        relu, sq = b.sb("relu", [P, 2, GW]), b.sb("sq", [P, 2, GW])
        up_acc, dn_acc = b.ps("up_acc", [P, 3, 512]), b.ps("dn_acc", [P, 3, 512])
        up_in, dn_in = b.sem("up_in"), b.sem("dn_in")
        up_hi_done, up_lo_done = b.sem("up_hi_done"), b.sem("up_lo_done")
        dn_hi_done, dn_lo_done = b.sem("dn_hi_done"), b.sem("dn_lo_done")
        up_done, dn_done, added = b.sem("up_done"), b.sem("dn_done"), b.sem("added")
        relu_done, sq_done = b.sem("relu_done"), b.sem("sq_done")
        hid_hi_done, hid_lo_done = b.sem("hid_hi_done"), b.sem("hid_lo_done")
        tail = TokenStage(b, sh, src_sb=h, gamma=next_gamma, y=y,
                          ready=lambda e, t: e.wait_ge(added, (NCH - 1) * DU + 2 * (t + 1)))

        def up_src(i):
            return w_up[:, bass.ds(i * CW, CW)].rearrange("(k p) n -> p k n", p=P)

        def dn_src(i):
            return w_down[bass.ds(i * CW, CW), :].rearrange("(k p) n -> p k n", p=P)

        def chunks_loop(e, body):
            body(0, True, False)
            with e.Fori(1, NCH - 1) as i:
                body(i, False, False)
            body(NCH - 1, False, True)

        with nc.Block() as block:
            @block.sync
            def _(sp):
                sp.dma_start(dn_raw, dn_src(0)).then_inc(dn_in, 16)
                tail.load_gamma(sp)
                if y is not None:
                    for t in range(NT):
                        tail.sp_store(sp, t)
                    tail.sp_stored(sp)

            @block.scalar
            def _(act):
                act.dma_start(up_raw, up_src(1)).then_inc(up_in, 16)

                def body(i, first, last):
                    act.wait_ge(dn_in, i * 16 + 16)
                    if not first:
                        act.wait_ge(dn_done, i * DU)
                    act.activation(dn_hi, dn_raw, ACT.Copy).then_inc(dn_hi_done, 1)
                    for u in range(UU):
                        g, j = u // FB, u % FB
                        act.wait_ge(up_done, i * UU + (u + 1))
                        if not (first and u < 2):
                            act.wait_ge(hid_lo_done, i * UU + (u - 1))
                        act.activation(relu[:, u % 2, :], up_acc[:, u % 3, 0:GW], ACT.Relu).then_inc(relu_done, 1)
                        act.wait_ge(relu_done, i * UU + (u + 1))
                        act.activation(hid_hi[:, j, g * GW:(g + 1) * GW], relu[:, u % 2, :], ACT.Square)\
                            .then_inc(hid_hi_done, 1)
                    if last and next_w is None:
                        return
                    act.wait_ge(up_in, i * 16 + 16)
                    act.activation(up_hi, up_raw, ACT.Copy).then_inc(up_hi_done, 1)
                    if not last:
                        act.wait_ge(dn_lo_done, i + 1)
                        act.dma_start(dn_raw, dn_src(i + 1)).then_inc(dn_in, 16)

                def next_up(i, src):
                    act.wait_ge(up_lo_done, i + 1)
                    act.dma_start(up_raw, src).then_inc(up_in, 16)

                body(0, True, False)
                with act.Fori(1, NCH - 1) as i:
                    next_up(i - 1, up_src(i + 1))
                    body(i, False, False)
                if next_w is not None:
                    next_up(NCH - 2, next_w.rearrange("(k p) n -> p k n", p=P))
                body(NCH - 1, False, True)
                for t in range(NT):
                    tail.act_sumsq(act, t)
                    if t >= 2 and y is None:
                        tail.act_hi(act, t - 2)
                if y is None:
                    tail.act_hi(act, NT - 2)
                    tail.act_hi(act, NT - 1)

            @block.gpsimd
            def _(pool):
                def body(i, first, last):
                    pool.wait_ge(dn_hi_done, i + 1)
                    pool.tensor_tensor(dn_lo, dn_raw, dn_hi.bitcast(F32), ALU.subtract).then_inc(dn_lo_done, 1)
                    if not last or next_w is not None:
                        pool.wait_ge(up_hi_done, i + 1)
                        pool.tensor_tensor(up_lo, up_raw, up_hi.bitcast(F32), ALU.subtract).then_inc(up_lo_done, 1)

                tail.pool_consts(pool)
                chunks_loop(pool, body)
                for t in range(NT):
                    tail.pool_rstd(pool, t)

            @block.tensor
            def _(pe):
                w_up_s, w_dn_s = (up_hi, up_lo), (dn_hi, dn_lo)
                x_s, hid_s = (sh.xhi, sh.xlo), (hid_hi, hid_lo)

                def body(i, first, last):
                    if not first:
                        pe.wait_ge(up_lo_done, i)
                    for u in range(UU):
                        g, j = u // FB, u % FB
                        if not (first and u < 3):
                            pe.wait_ge(relu_done, i * UU + (u - 2))
                        n = 0
                        for k in range(KB):
                            for a, c in TERMS:
                                mm = pe.matmul(up_acc[:, u % 3, 0:GW], w_up_s[a][:, k, j * P:(j + 1) * P],
                                               x_s[c][:, k, g * GW:(g + 1) * GW],
                                               start=(n == 0), stop=(n == len(TERMS) * KB - 1))
                                n += 1
                        mm.then_inc(up_done, 1)
                    pe.wait_ge(dn_lo_done, i + 1)
                    for v in range(DU):
                        t, half = v // 2, v % 2
                        if v % (2 * GRP) == 0:
                            pe.wait_ge(hid_lo_done, i * UU + FB * (t // GRP + 1))
                        if not (first and v < 3):
                            pe.wait_ge(added, i * DU + (v - 2))
                        n = 0
                        for k in range(FB):
                            for a, c in TERMS:
                                mm = pe.matmul(dn_acc[:, v % 3, :], hid_s[c][:, k, t * P:(t + 1) * P],
                                               w_dn_s[a][:, k, half * 512:(half + 1) * 512],
                                               start=(n == 0), stop=(n == len(TERMS) * FB - 1))
                                n += 1
                        mm.then_inc(dn_done, 1)
                        if last and y is None and half == 1 and t >= 2:
                            tail.pe_transpose(pe, t - 2)

                chunks_loop(pe, body)
                if y is None:
                    tail.pe_transpose(pe, NT - 2)
                    tail.pe_transpose(pe, NT - 1)

            @block.vector
            def _(dve):
                def body(i, first, last):
                    for u in range(UU):
                        g, j = u // FB, u % FB
                        dve.wait_ge(relu_done, i * UU + (u + 1))
                        dve.tensor_tensor(sq[:, u % 2, :], relu[:, u % 2, :], relu[:, u % 2, :], ALU.mult)\
                            .then_inc(sq_done, 1)
                        dve.wait_ge(sq_done, i * UU + (u + 1))
                        dve.wait_ge(hid_hi_done, i * UU + (u + 1))
                        dve.tensor_tensor(hid_lo[:, j, g * GW:(g + 1) * GW], sq[:, u % 2, :],
                                          hid_hi[:, j, g * GW:(g + 1) * GW].bitcast(F32), ALU.subtract)\
                            .then_inc(hid_lo_done, 1)
                    for v in range(DU):
                        t, half = v // 2, v % 2
                        cols = h[:, t, half * 512:(half + 1) * 512]
                        dve.wait_ge(dn_done, i * DU + (v + 1))
                        dve.tensor_tensor(cols, dn_acc[:, v % 3, :], cols, ALU.add).then_inc(added, 1)
                        if last and half == 1:
                            if t >= 1:
                                tail.dve_norm(dve, t - 1)
                            if t >= 2 and y is None:
                                tail.dve_lo(dve, t - 2)

                chunks_loop(dve, body)
                tail.dve_norm(dve, NT - 1)
                if y is None:
                    tail.dve_lo(dve, NT - 2)
                    tail.dve_lo(dve, NT - 1)


T0 = TOPK_P // P
CHOICE = list(range(T0, NT_P))[::-1]
NUMBER = {t: x for x, t in enumerate(CHOICE)}
ROUNDS = TOPK_P // 8
LEAD = 1.0
SCORE_AT = {t: sum((i + 1) * P for i in range(T0, t)) for t in range(T0, NT_P + 1)}


def pieces(x, L):
    n = 1 if L <= 512 else 2
    return x[:, 0:n, 0:L // n] if len(x.shape) == 3 else x.rearrange("p (n c) -> p n c", n=n)


class Choice:

    def __init__(self, b, score, done=None):
        self.score, self.top8 = score, b.sb("top8", [P, 8])
        self.top8_done, self.replaced, self.bias_done = b.sem("top8_done"), b.sem("replaced"), b.sem("bias_done")
        self.rounds = 0
        self.done = dict(done or {})

    def scores(self, t):
        return self.score[:, SCORE_AT[t]:SCORE_AT[t] + (t + 1) * P]

    def dve_round(self, dve, t):
        r, sc = self.rounds, self.scores(t)
        if r >= 1:
            dve.wait_ge(self.replaced, r)
        dve.max(self.top8[:, :], sc).then_inc(self.top8_done, 1)
        dve.wait_ge(self.top8_done, r + 1)
        dve.match_replace(sc, self.top8[:, :], sc, MARK).then_inc(self.replaced, 1)
        self.rounds += 1
        self.done[t] = self.done.get(t, 0) + 1
        if self.done[t] == ROUNDS:
            dve.wait_ge(self.replaced, self.rounds)
            dve.tensor_scalar(sc, sc, CUT, NEG, ALU.is_gt, ALU.mult).then_inc(self.bias_done, 1)


def project_and_score_phase(nc, name, sh, chunks, preset, slot0, qiT, wt, ki_out, score):
    with Block(nc, name) as b:
        gm = Gemm(b, sh, chunks, preset, slot0)
        ch = Choice(b, score)
        kiin = b.sb("ki_in", [P, NT_P, 2, ID])
        ki_hi, ki_lo = b.sb("ki_hi", [P, SEQ], F32R), b.sb("ki_lo", [P, SEQ], F32R)
        q_in, q_split = b.sb("q_in", [P, 2, IH, P]), b.sb("q_split", [P, 2, IH, P], F32R)
        w_raw, w = b.sb("w_raw", [P, NT_P, IH]), b.sb("w", [P, NT_P, IH])
        RR = 3
        rl = b.sb("relu", [P, RR, SEQ])
        slot = b.ps("slot", [P, 2, 2, 512])
        ki_loaded, w_loaded = b.sem("ki_loaded"), b.sem("w_loaded")
        q_loaded = [b.sem("q_loaded0"), b.sem("q_loaded1")]
        q_hi_done, q_lo_done = b.sem("q_hi_done"), b.sem("q_lo_done")
        w_done, turned, ki_hi_done, ki_lo_done = b.sem("w_done"), b.sem("turned"), b.sem("ki_hi_done"), b.sem("ki_lo_done")
        dots_done, relu_done, scored, filled = b.sem("dots_done"), b.sem("relu_done"), b.sem("scored"), b.sem("filled")

        plan, units = [], list(gm.units)
        rounds = [t for t in CHOICE for _ in range(ROUNDS)]
        pe_time = dve_time = 0.0

        def round_of(t):
            plan.append(("round", t, 0))
            return 0.285 * (t + 1) + 0.18

        for t in CHOICE:
            for ih in range(IH):
                plan.append(("index", t, ih))
                pe_time, dve_time = pe_time + 0.11 * (t + 1), dve_time + 0.16 * (t + 1)
                while dve_time < pe_time + LEAD and NUMBER[rounds[0]] < NUMBER[t]:
                    dve_time += round_of(rounds.pop(0))
                while units and pe_time < dve_time:
                    pe_time += 2.8 if units[0]["form"] == "N" else 3.9
                    plan.append(("unit", units.pop(0), 0))
        while units:
            pe_time += 2.8 if units[0]["form"] == "N" else 3.9
            plan.append(("unit", units.pop(0), 0))
            while dve_time < pe_time and rounds:
                dve_time += round_of(rounds.pop(0))

        with nc.Block() as block:
            @block.sync
            def _(sp):
                def load_q(x):
                    t = CHOICE[x]
                    if x >= 2:
                        sp.wait_ge(q_hi_done, x - 1)
                        sp.wait_ge(q_lo_done, x - 1)
                    for r in range(2):
                        sp.dma_start(q_in[r * ID:(r + 1) * ID, x % 2, :, :],
                                     qiT[:, t * P:(t + 1) * P].rearrange("(h d) n -> d h n", d=ID))\
                            .then_inc(q_loaded[x % 2], 16)

                for r in range(2):
                    sp.dma_start(kiin[:, :, r, :], ki_out.rearrange("(t p) c -> p t c", p=P)).then_inc(ki_loaded, 16)
                load_q(0)
                sp.dma_start(w_raw[:, :, :], wt[0:SEQ, :].rearrange("(t p) c -> p t c", p=P)).then_inc(w_loaded, 16)
                load_q(1)
                if not preset:
                    gm.sp_load_w(sp, 0)
                gm.sp_load_w(sp, 1)
                for kind, t, ih in plan:
                    if kind == "index" and ih == 0 and NUMBER[t] + 2 < len(CHOICE):
                        load_q(NUMBER[t] + 2)
                    elif kind == "unit":
                        if t is gm.of[t["c"]][0]:
                            gm.sp_load_w(sp, t["c"] + 2)
                        gm.sp_store(sp, t)
                gm.sp_end(sp)

            @block.gpsimd
            def _(pool):
                def q_lo(x):
                    pool.wait_ge(q_hi_done, x + 1)
                    pool.tensor_tensor(q_split[ID:P, x % 2, :, :], q_in[ID:P, x % 2, :, :],
                                       q_split[ID:P, x % 2, :, :].bitcast(F32), ALU.subtract).then_inc(q_lo_done, 1)

                q_lo(0)
                q_lo(1)
                pool.wait_ge(q_lo_done, 2)
                if not preset:
                    gm.pool_w_lo(pool, 0)
                gm.pool_w_lo(pool, 1)
                splits = 1
                for kind, t, ih in plan:
                    if kind == "index" and ih == IH - 1 and NUMBER[t] + 2 < len(CHOICE):
                        pool.wait_ge(gm.wlo_done, gm.splits(splits))
                        q_lo(NUMBER[t] + 2)
                        pool.wait_ge(q_lo_done, NUMBER[t] + 3)
                    elif kind == "unit" and t is gm.of[t["c"]][-1] and t["c"] + 2 < len(chunks):
                        splits = t["c"] + 2
                        gm.pool_w_lo(pool, splits)

            @block.tensor
            def _(pe):
                pe.wait_ge(ki_loaded, 32)
                for r in range(2):
                    for c in range(4):
                        mm = pe.transpose(slot[:, r, 0, c * P:(c + 1) * P],
                                          kiin[:, 4 * r + c, :, :].rearrange("p r d -> p (r d)"), sh.ident[:, :])
                    mm.then_inc(turned, 1)
                pe.wait_ge(ki_lo_done, 2)
                n = 0
                for kind, t, ih in plan:
                    if kind == "unit":
                        gm.pe_unit(pe, t)
                    elif kind == "index":
                        if ih == 0:
                            pe.wait_ge(q_lo_done, NUMBER[t] + 1)
                        if n >= 2:
                            pe.wait_ge(relu_done, n - 1)
                        L = (t + 1) * P
                        k = 1 if L <= 512 else 2
                        for j in range(k):
                            cols = slice(j * L // k, (j + 1) * L // k)
                            for x, keys in enumerate((ki_hi, ki_lo)):
                                mm = pe.matmul(slot[:, n % 2, j, 0:L // k], q_split[:, NUMBER[t] % 2, ih, :], keys[:, cols],
                                               start=(x == 0), stop=(x == 1))
                        mm.then_inc(dots_done, 1)
                        n += 1

            @block.scalar
            def _(act):
                def q_hi(x):
                    act.wait_ge(q_loaded[x % 2], 32 * (x // 2 + 1))
                    if x >= 2:
                        act.wait_ge(dots_done, IH * (x - 1))
                    act.activation(q_split[:, x % 2, :, :], q_in[:, x % 2, :, :], ACT.Copy).then_inc(q_hi_done, 1)

                for r in range(2):
                    act.wait_ge(turned, r + 1)
                    act.activation(ki_hi[:, r * 512:(r + 1) * 512], slot[:, r, 0, :], ACT.Copy).then_inc(ki_hi_done, 1)
                q_hi(0)
                q_hi(1)
                if not preset:
                    gm.act_w_hi(act, 0)
                gm.act_w_hi(act, 1)
                n = 0
                for kind, t, ih in plan:
                    if kind == "unit":
                        gm.act_evacuate(act, t)
                        if t is gm.of[t["c"]][-1] and t["c"] + 2 < len(chunks):
                            gm.act_w_hi(act, t["c"] + 2)
                    elif kind == "index":
                        L = (t + 1) * P
                        act.wait_ge(dots_done, n + 1)
                        if n >= RR:
                            act.wait_ge(scored, n - RR + 1)
                        act.activation(pieces(rl[:, n % RR, 0:L], L), pieces(slot[:, n % 2, :, :], L), ACT.Relu,
                                       scale=ID ** -0.5).then_inc(relu_done, 1)
                        n += 1
                        if ih == IH - 1 and NUMBER[t] + 2 < len(CHOICE):
                            q_hi(NUMBER[t] + 2)

            @block.vector
            def _(dve):
                dve.wait_ge(w_loaded, 16)
                dve.tensor_scalar(w[:, :, :], w_raw[:, :, :], IH ** -0.5, None, ALU.mult).then_inc(w_done, 1)
                for r in range(2):
                    dve.wait_ge(ki_hi_done, r + 1)
                    cols = slice(r * 512, (r + 1) * 512)
                    dve.tensor_tensor(ki_lo[:, cols], slot[:, r, 0, :], ki_hi[:, cols].bitcast(F32), ALU.subtract)\
                        .then_inc(ki_lo_done, 1)
                dve.wait_ge(w_done, 1)
                n = 0
                for kind, t, x in plan:
                    if kind == "index":
                        sc, L = ch.scores(t), (t + 1) * P
                        dve.wait_ge(relu_done, n + 1)
                        if x == 0:
                            dve.tensor_scalar(sc, rl[:, n % RR, 0:L], w[:, t, 0:1], None, ALU.mult).then_inc(scored, 1)
                        else:
                            dve.wait_ge(scored, n)
                            dve.scalar_tensor_tensor(sc, rl[:, n % RR, 0:L], w[:, t, x:x + 1], sc, ALU.mult, ALU.add)\
                                .then_inc(scored, 1)
                        n += 1
                        if x == IH - 1:
                            dve.wait_ge(scored, n)
                            dve.memset(sc[0:CHUNK, L - CHUNK:L], FILL).then_inc(filled, 1)
                    elif kind == "round":
                        if t not in ch.done:
                            dve.wait_ge(filled, NUMBER[t] + 1)
                        ch.dve_round(dve, t)
        return ch.done


def attention_phase(nc, name, ident, qT, k_out, v_out, score, cache_k, cache_v, k_new, v_new, s_bias, o, begun):
    SAMPLE = NT_P
    ORDER = [SAMPLE, 7, 6, 5, 4, 1, 3, 0, 2]
    PROMPT = [t for t in ORDER if t != SAMPLE]
    GH4 = HEADS // KVH
    PAIRS, PB, L_S = KVH // 2, PAST // P, PAST + DEC_T
    assert DEC_B * PAIRS == HEADS
    SR = 3
    N = NT * HEADS
    tile_at = lambda n: ORDER[n // HEADS]
    start_of = {t: HEADS * i for i, t in enumerate(ORDER)}
    prompt_no = {t: i for i, t in enumerate(PROMPT)}
    length = lambda n: L_S if tile_at(n) == SAMPLE else (tile_at(n) + 1) * P
    stream = lambda n: ((n - start_of[SAMPLE]) // PAIRS, n % PAIRS)

    key_bank, bank_of, banks = {}, {}, 0
    for n in range(-1, N + 2):
        if n + 1 < N and tile_at(n + 1) == SAMPLE:
            key_bank[n + 1] = banks
            banks += 1
        if n >= 2:
            nb = -(-length(n - 2) // (4 * P))
            bank_of[n - 2] = list(range(banks, banks + nb))
            banks += nb

    def outs(g):
        first = start_of[SAMPLE] // GH4
        return g + max(0, min(g - first, HEADS // GH4))

    STORES = lambda t: PAIRS * 2 * GH4 if t == SAMPLE else 1

    def stored_before(i):
        return 16 * sum(STORES(ORDER[j]) for j in range(i % 2, i, 2))

    left = [t for t in CHOICE for _ in range(ROUNDS - begun.get(t, 0))]
    late = [t for t in CHOICE if t in left]
    rounds_at, slack = [], 0.0
    for n in range(N):
        t = tile_at(n)
        slack += 2.2 if t == SAMPLE else 0.33 * (t + 1) - 0.25
        now = []
        while left and len(now) < 4 and n < start_of[left[0]] and (
                slack > 0 or left.count(left[0]) > 3 * (start_of[left[0]] - 1 - n)):
            slack -= 0.27 * (left[0] + 1) + 0.1
            now.append(left.pop(0))
        rounds_at.append(now)
    assert not left

    with Block(nc, name) as b:
        ch = Choice(b, score, begun)
        kin = b.sb("k_in", [P, NT_P, KVH, HD])
        twice = b.sb("k_twice", [P, 2, KVH, 2, HD])
        vin = b.sb("v_in", [P, NT_P, KVH * HD])
        k_hi, k_lo = b.sb("k_hi", [P, KVH, SEQ], F32R), b.sb("k_lo", [P, KVH, SEQ], F32R)
        q_in, q_split = b.sb("q_in", [P, 2, HEADS, P]), b.sb("q_split", [P, 2, HEADS, P], F32R)
        q_s = b.sb("q_streams", [P, PAIRS, DEC_B, P])
        ck, cv = b.sb("cached_k", [P, SR, PB, KVH * HD]), b.sb("cached_v", [P, SR, PB, KVH * HD])
        nk, nkT = b.sb("new_k", [P, KVH * HD]), b.sb("new_kT", [P, PAIRS, P])
        nv, ckT = b.sb("new_v", [DEC_T, DEC_B, KVH * HD]), b.sb("cached_kT", [P, 2, PAST])
        open_ = b.sb("open", [P, T0, T0 * P])
        LR = 4
        lg = b.sb("logits", [P, LR, SEQ])
        probs_T = b.sb("probs_T", [P, 2, SEQ])
        nm = b.sb("neg_max", [P, 4])
        den, rden = b.sb("den", [P, 4, GH4]), b.sb("rden", [P, 2, GH4])
        ot = b.sb("o_tile", [P, 2, D])
        slot = b.ps("slot", [P, 2, 2, 512])
        psT = b.ps("psT", [P, 2, 512])
        pv = b.ps("pv", [P, 2, GH4, P])
        k_loaded, v_loaded, new_in = b.sem("k_loaded"), b.sem("v_loaded"), b.sem("new_in")
        q_loaded = [b.sem("q_loaded0"), b.sem("q_loaded1")]
        qs_zero, qs_in = b.sem("qs_zero"), b.sem("qs_in")
        ck_in, cv_in = ([b.sem(f"{what}_in{i}") for i in range(SR)] for what in ("ck", "cv"))
        q_hi_done, q_lo_done = b.sem("q_hi_done"), b.sem("q_lo_done")
        k_doubled, k_turned, k_hi_done, k_lo_done = b.sem("k_doubled"), b.sem("k_turned"), b.sem("k_hi_done"), b.sem("k_lo_done")
        opened = b.sem("opened")
        qk_done, masked, exp_done = b.sem("qk_done"), b.sem("masked"), b.sem("exp_done")
        turned, turned_out, pv_done = b.sem("turned"), b.sem("turned_out"), b.sem("pv_done")
        rden_done, o_done = b.sem("rden_done"), b.sem("o_done")
        o_stored = [b.sem("o_stored0"), b.sem("o_stored1")]

        with nc.Block() as block:
            @block.sync
            def _(sp):
                def load_q(x):
                    t = PROMPT[x]
                    if x >= 2:
                        sp.wait_ge(q_hi_done, x - 1)
                        sp.wait_ge(q_lo_done, x - 1)
                    for r in range(2):
                        sp.dma_start(q_in[r * HD:(r + 1) * HD, x % 2, :, :],
                                     qT[:, t * P:(t + 1) * P].rearrange("(h d) n -> d h n", d=HD))\
                            .then_inc(q_loaded[x % 2], 16)

                def load_stream(s):
                    last = start_of[SAMPLE] + (s - SR + 1) * PAIRS - 1
                    if s >= SR:
                        sp.wait_ge(turned, key_bank[last] + 1)
                    sp.dma_start(ck[:, s % SR, :, :], cache_k[s].rearrange("(k p) c -> p k c", p=P)).then_inc(ck_in[s % SR], 16)
                    if s >= SR:
                        sp.wait_ge(pv_done, last + 1)
                    sp.dma_start(cv[:, s % SR, :, :], cache_v[s].rearrange("(k p) c -> p k c", p=P)).then_inc(cv_in[s % SR], 16)

                sp.dma_start(kin[:, :, :, :].rearrange("p t v d -> p t (v d)"), k_out.rearrange("(t p) c -> p t c", p=P))\
                    .then_inc(k_loaded, 16)
                sp.dma_start(nk[:, :], k_new).then_inc(new_in, 16)
                sp.dma_start(nv[:, :, :], v_new.rearrange("(b t) c -> t b c", t=DEC_T)).then_inc(new_in, 16)
                load_stream(0)
                sp.wait_ge(qs_zero, 1)
                for v in range(KVH):
                    for g in range(GH4):
                        r0, c0 = (v * GH4 + g) * HD, (v % 2) * HD + g * DEC_T
                        sp.dma_start(q_s[(v % 2) * HD:(v % 2 + 1) * HD, v // 2, :, c0:c0 + DEC_T],
                                     qT[r0:r0 + HD, SEQ:TOK].rearrange("d (b t) -> d b t", t=DEC_T)).then_inc(qs_in, 16)
                load_stream(1)
                load_q(0)
                load_stream(2)
                sp.dma_start(vin[:, :, :], v_out.rearrange("(t p) c -> p t c", p=P)).then_inc(v_loaded, 16)
                load_q(1)
                for s in range(SR, DEC_B):
                    load_stream(s)
                for i, t in enumerate(ORDER):
                    if t != SAMPLE and prompt_no[t] + 2 < NT_P:
                        load_q(prompt_no[t] + 2)
                    sp.wait_ge(o_done, outs(KVH * (i + 1)))
                    if t != SAMPLE:
                        sp.dma_start(o[t * P:(t + 1) * P, :], ot[:, i % 2, :]).then_inc(o_stored[i % 2], 16)
                        continue
                    rows = o[SEQ:TOK, :].rearrange("(s t) (a c) -> a t s c", t=DEC_T, a=PAIRS)
                    for r in range(2):
                        for g in range(GH4):
                            p0, c0 = r * HD + g * DEC_T, (r * GH4 + g) * HD
                            tile = ot[p0:p0 + DEC_T, i % 2, :].rearrange("p (s a d) -> p s a d", a=PAIRS, d=HD)
                            for a in range(PAIRS):
                                sp.dma_start(rows[a][:, :, c0:c0 + HD], tile[:, :, a, :]).then_inc(o_stored[i % 2], 16)
                for i in range(2):
                    sp.wait_ge(o_stored[i], 16 * sum(STORES(ORDER[j]) for j in range(i, NT, 2)))

            @block.gpsimd
            def _(pool):
                pool.memset(q_s[:, :, :, :], 0.0).then_inc(qs_zero, 1)
                pool.memset(open_[:, :, :], 0.0).then_inc(opened, 1)
                pool.wait_ge(opened, 1)
                for t in range(T0):
                    pool.memset(open_[0:CHUNK, t, (t + 1) * P - CHUNK:(t + 1) * P], NEG).then_inc(opened, 1)
                pool.wait_ge(opened, 1 + T0)
                for x in range(NT_P):
                    pool.wait_ge(q_hi_done, x + 1)
                    pool.tensor_tensor(q_split[HD:P, x % 2, :, :], q_in[HD:P, x % 2, :, :],
                                       q_split[HD:P, x % 2, :, :].bitcast(F32), ALU.subtract).then_inc(q_lo_done, 1)

            @block.tensor
            def _(pe):
                for r in range(NT_P):
                    pe.wait_ge(k_doubled, r + 1)
                    if r >= 2:
                        pe.wait_ge(k_lo_done, r - 1)
                    for v in range(KVH):
                        mm = pe.transpose(psT[:, r % 2, v * P:(v + 1) * P],
                                          twice[:, r % 2, v, :, :].rearrange("p r d -> p (r d)"), ident[:, :])
                    mm.then_inc(k_turned, 1)
                pe.wait_ge(new_in, 32)
                pe.wait_ge(k_lo_done, NT_P)
                for pair in range(PAIRS):
                    mm = pe.transpose(psT[:, 0, pair * P:(pair + 1) * P], nk[:, pair * P:(pair + 1) * P], ident[:, :])
                mm.then_inc(k_turned, 1)
                pe.wait_ge(k_hi_done, NT_P + 1)
                pe.wait_ge(qs_in, 16 * HEADS)

                def turn_keys(n):
                    (s, pair), i = stream(n), key_bank[n]
                    if i >= 2:
                        pe.wait_ge(turned_out, i - 1)
                    pe.wait_ge(ck_in[s % SR], 16 * (s // SR + 1))
                    for k in range(PB):
                        mm = pe.transpose(psT[:, i % 2, k * P:(k + 1) * P], ck[:, s % SR, k, pair * P:(pair + 1) * P],
                                          ident[:, :])
                    mm.then_inc(turned, 1)

                def logits(n):
                    t, L, hd = tile_at(n), length(n), n % HEADS
                    if n >= 2:
                        pe.wait_ge(masked, n - 1)
                    if t == SAMPLE:
                        s, pair = stream(n)
                        pe.wait_ge(turned_out, key_bank[n] + 1)
                        H = L // 2
                        for j, c0, rhs in ((0, 0, ckT[:, n % 2, 0:H]), (1, 0, ckT[:, n % 2, H:PAST]),
                                           (1, PAST - H, nkT[:, pair, s * DEC_T:(s + 1) * DEC_T])):
                            mm = pe.matmul(slot[:, n % 2, j, c0:c0 + rhs.shape[1]], q_s[:, pair, s, :], rhs,
                                           start=True, stop=True)
                    else:
                        x, k = prompt_no[t], 1 if L <= 512 else 2
                        if hd == 0:
                            pe.wait_ge(q_lo_done, x + 1)
                        for j in range(k):
                            cols = slice(j * L // k, (j + 1) * L // k)
                            for y, keys in enumerate((k_hi, k_lo)):
                                mm = pe.matmul(slot[:, n % 2, j, 0:L // k], q_split[:, x % 2, hd, :],
                                               keys[:, hd // GH4, cols], start=(y == 0), stop=(y == 1))
                    mm.then_inc(qk_done, 1)

                def turn(n):
                    pe.wait_ge(exp_done, n + 1)
                    for x, i in enumerate(bank_of[n]):
                        if i >= 2:
                            pe.wait_ge(turned_out, i - 1)
                        for j, c0 in enumerate(range(4 * x * P, min(4 * (x + 1) * P, length(n)), P)):
                            w = min(P, length(n) - c0)
                            mm = pe.transpose(psT[0:w, i % 2, j * P:(j + 1) * P], lg[:, n % LR, c0:c0 + w], ident[:, :])
                        mm.then_inc(turned, 1)

                def values(n):
                    t, dst = tile_at(n), pv[:, n // GH4 % 2, n % GH4, :]
                    pe.wait_ge(turned_out, bank_of[n][-1] + 1)
                    if n >= 2 * GH4 and n % GH4 == 0:
                        pe.wait_ge(o_done, outs(n // GH4 - 1))
                    if t == SAMPLE:
                        s, pair = stream(n)
                        pe.wait_ge(cv_in[s % SR], 16 * (s // SR + 1))
                        for k in range(PB):
                            pe.matmul(dst, probs_T[:, n % 2, k * P:(k + 1) * P],
                                      cv[:, s % SR, k, pair * P:(pair + 1) * P], start=(k == 0), stop=False)
                        mm = pe.matmul(dst, probs_T[0:DEC_T, n % 2, PAST:PAST + P], nv[:, s, pair * P:(pair + 1) * P],
                                       start=False, stop=True)
                    else:
                        pair = n % HEADS // (2 * GH4)
                        if n == start_of[PROMPT[0]]:
                            pe.wait_ge(v_loaded, 16)
                        for j in range(t + 1):
                            mm = pe.matmul(dst, probs_T[:, n % 2, j * P:(j + 1) * P],
                                           vin[:, j, pair * P:(pair + 1) * P], start=(j == 0), stop=(j == t))
                    mm.then_inc(pv_done, 1)

                for n in range(-1, N + 3):
                    if n + 1 in key_bank:
                        turn_keys(n + 1)
                    if 0 <= n < N:
                        logits(n)
                    if 2 <= n < N + 2:
                        turn(n - 2)
                    if n >= 3:
                        values(n - 3)

            @block.scalar
            def _(act):
                def q_hi(x):
                    act.wait_ge(q_loaded[x % 2], 32 * (x // 2 + 1))
                    if x >= 2:
                        act.wait_ge(qk_done, start_of[PROMPT[x - 2]] + HEADS)
                    act.activation(q_split[:, x % 2, :, :], q_in[:, x % 2, :, :], ACT.Copy).then_inc(q_hi_done, 1)

                for r in range(NT_P):
                    act.wait_ge(k_turned, r + 1)
                    act.activation(k_hi[:, :, r * P:(r + 1) * P], psT[:, r % 2, :].rearrange("p (v n) -> p v n", v=KVH),
                                   ACT.Copy).then_inc(k_hi_done, 1)
                act.wait_ge(k_turned, NT_P + 1)
                act.activation(nkT[:, :, :], psT[:, 0, 0:PAIRS * P].rearrange("p (a n) -> p a n", n=P), ACT.Copy)\
                    .then_inc(k_hi_done, 1)

                def keys_out(n):
                    i = key_bank[n]
                    act.wait_ge(turned, i + 1)
                    if n >= 2:
                        act.wait_ge(qk_done, n - 1)
                    act.activation(ckT[:, n % 2, :], psT[:, i % 2, :], ACT.Copy).then_inc(turned_out, 1)

                def turn_out(n):
                    for x, i in enumerate(bank_of[n]):
                        act.wait_ge(turned, i + 1)
                        if n >= 2:
                            act.wait_ge(pv_done, n - 1)
                        c0, c1 = 4 * x * P, min(4 * (x + 1) * P, length(n))
                        rows = P if (c1 - c0) % P == 0 else c1 - c0
                        cols = max(c1 - c0, P)
                        act.activation(probs_T[0:rows, n % 2, c0:c0 + cols], psT[0:rows, i % 2, 0:cols], ACT.Copy)\
                            .then_inc(turned_out, 1)

                for n in range(-1, N + 2):
                    if n + 1 in key_bank:
                        keys_out(n + 1)
                    if n == 1:
                        q_hi(0)
                        q_hi(1)
                    if n >= 2:
                        turn_out(n - 2)
                    if 0 <= n < N:
                        t, L = tile_at(n), length(n)
                        act.wait_ge(masked, n + 1)
                        if n >= 4 * GH4:
                            act.wait_ge(rden_done, n // GH4 - 3)
                        x = lg[:, n % LR, 0:L]
                        act.activation(x, x, ACT.Exp, bias=nm[:, n % 4:n % 4 + 1], scale=-1.0,
                                       accum_out=den[:, n // GH4 % 4, n % GH4:n % GH4 + 1]).then_inc(exp_done, 1)
                        if n % HEADS == HEADS - 1 and t != SAMPLE and prompt_no[t] + 2 < NT_P:
                            q_hi(prompt_no[t] + 2)

            @block.vector
            def _(dve):
                def double(r):
                    if r >= 2:
                        dve.wait_ge(k_turned, r - 1)
                    dve.tensor_copy(twice[:, r % 2, :, :, :], kin[:, r, :, :].unsqueeze(2).broadcast_to([P, KVH, 2, HD]))\
                        .then_inc(k_doubled, 1)

                dve.wait_ge(k_loaded, 16)
                double(0)
                for r in range(NT_P):
                    if r + 1 < NT_P:
                        double(r + 1)
                    dve.wait_ge(k_hi_done, r + 1)
                    cols = slice(r * P, (r + 1) * P)
                    dve.tensor_tensor(k_lo[:, :, cols], psT[:, r % 2, :].rearrange("p (v n) -> p v n", v=KVH),
                                      k_hi[:, :, cols].bitcast(F32), ALU.subtract).then_inc(k_lo_done, 1)

                def finish(g):
                    i, x = g // KVH, g % KVH
                    dve.wait_ge(exp_done, GH4 * (g + 1))
                    dve.reciprocal(rden[:, g % 2, :], den[:, g % 4, :]).then_inc(rden_done, 1)
                    dve.wait_ge(rden_done, g + 1)
                    dve.wait_ge(pv_done, GH4 * (g + 1))
                    if x == 0 and stored_before(i):
                        dve.wait_ge(o_stored[i % 2], stored_before(i))
                    dst = ot[:, i % 2, x * GH4 * HD:(x + 1) * GH4 * HD].rearrange("p (h d) -> p h d", d=HD)
                    by = rden[:, g % 2, :].unsqueeze(2).broadcast_to([P, GH4, HD])
                    if ORDER[i] == SAMPLE:
                        for r in range(2):
                            half = slice(r * HD, (r + 1) * HD)
                            dve.tensor_tensor(dst[half], pv[half, g % 2, :, half], by[half], ALU.mult).then_inc(o_done, 1)
                    else:
                        dve.tensor_tensor(dst, pv[:, g % 2, :, (x % 2) * HD:(x % 2 + 1) * HD], by, ALU.mult)\
                            .then_inc(o_done, 1)

                for n in range(N + 4):
                    if n < N:
                        t, L = tile_at(n), length(n)
                        dve.wait_ge(qk_done, n + 1)
                        if n == start_of[t] and t < T0:
                            dve.wait_ge(opened, 1 + T0)
                        if n == start_of[t] and t in late:
                            dve.wait_ge(ch.bias_done, late.index(t) + 1)
                        if n >= LR:
                            dve.wait_ge(turned, bank_of[n - LR][-1] + 1)
                            dve.wait_ge(exp_done, n - LR + 1)
                        bias = s_bias[:, stream(n)[0], :] if t == SAMPLE else open_[:, t, 0:L] if t < T0 else ch.scores(t)
                        dve.tensor_tensor_reduce(pieces(lg[:, n % LR, 0:L], L), pieces(slot[:, n % 2, :, :], L),
                                                 pieces(bias, L), -1.0, -FILL, ALU.add, ALU.min,
                                                 nm[:, n % 4:n % 4 + 1]).then_inc(masked, 1)
                        for tt in rounds_at[n]:
                            ch.dve_round(dve, tt)
                    if n >= GH4 and n % GH4 == GH4 - 1:
                        finish(n // GH4 - 1)


def sample_choice_phase(nc, name, ident, qiT, wt, cache_ki, ki_new, same_frame, bias):
    L = PAST + DEC_T
    PB = PAST // P
    with Block(nc, name) as b:
        frame_of, rows_of = b.sb("frame_of", [P, DEC_B, P]), b.sb("rows_of", [P, DEC_B, P])
        qi = b.sb("qi", [ID, DEC_B, IH, DEC_T])
        w_raw, w = b.sb("w_raw", [P, DEC_B]), b.sb("w", [P, DEC_B])
        cki = b.sb("cki", [P, DEC_B, PB, ID])
        nki, nkiT, ckiT = b.sb("nki", [P, ID]), b.sb("nkiT", [ID, P]), b.sb("ckiT", [ID, 2, PAST])
        rl, sel = b.sb("relu", [P, 2, L]), b.sb("sel", [P, 2, P])
        PAD = (-TOPK_S) % 8
        score = b.sb("score", [P, L + PAD])
        top8 = b.sb("top8", [P, 8])
        slot = b.ps("slot", [P, 2, 2, 512])
        psT, psN = b.ps("psT", [P, 2, 512]), b.ps("psN", [P, 512])
        ki_in, idx_in, w_in, rows_in, w_done = b.sem("ki_in"), b.sem("idx_in"), b.sem("w_in"), b.sem("rows_in"), b.sem("w_done")
        turned, turned_out = b.sem("turned"), b.sem("turned_out")
        qi_done, relu_done, sel_done, summed = b.sem("qi_done"), b.sem("relu_done"), b.sem("sel_done"), b.sem("summed")
        score_out, pad_done = b.sem("score_out"), b.sem("pad_done")
        top8_done, replaced, bias_done = b.sem("top8_done"), b.sem("replaced"), b.sem("bias_done")
        spread, spread_out = b.sem("spread"), b.sem("spread_out")

        def both(x):
            return x[:, :, 0:L // 2]

        with nc.Block() as block:
            @block.sync
            def _(sp):
                sp.dma_start(nki[:, :], ki_new).then_inc(ki_in, 16)
                for s in range(DEC_B):
                    sp.dma_start(cki[:, s, :, :], cache_ki[s].rearrange("(k p) d -> p k d", p=P)).then_inc(ki_in, 16)
                for hh in range(IH):
                    sp.dma_start(qi[:, :, hh, :],
                                 qiT[hh * ID:(hh + 1) * ID, SEQ:TOK].rearrange("d (b t) -> d b t", t=DEC_T)).then_inc(idx_in, 16)
                for hh in range(IH):
                    sp.dma_start(w_raw[hh * DEC_T:(hh + 1) * DEC_T, :],
                                 wt[SEQ:TOK, hh:hh + 1].rearrange("(b t) a -> t (b a)", t=DEC_T),
                                 allow_slow_non_contiguous=True).then_inc(w_in, 16)
                sp.dma_start(frame_of[:, :, :], same_frame[0]).then_inc(w_in, 16)
                sp.dma_start(rows_of[:, :, :], same_frame[1]).then_inc(rows_in, 16)

            @block.gpsimd
            def _(pool):
                pool.memset(score[:, L:L + PAD], -FILL).then_inc(pad_done, 1)


            @block.tensor
            def _(pe):
                pe.wait_ge(ki_in, 16 * (1 + DEC_B))
                pe.transpose(psN[0:ID, 0:P], nki[:, :], ident[:, :]).then_inc(turned, 1)

                def turn_ki(s):
                    if s >= 2:
                        pe.wait_ge(turned_out, s)
                    for k in range(PB):
                        mm = pe.transpose(psT[0:ID, s % 2, k * P:(k + 1) * P], cki[:, s, k, :], ident[:, :])
                    mm.then_inc(turned, 1)

                def add_scores(s):
                    pe.wait_ge(sel_done, s + 1)
                    pe.wait_ge(relu_done, s + 1)
                    pe.matmul(slot[:, 1, 0, 0:PAST], sel[:, s % 2, :], rl[:, s % 2, 0:PAST],
                              start=(s == 0), stop=(s == DEC_B - 1))
                    pe.matmul(slot[:, 1, 1, 0:DEC_T], sel[:, s % 2, :], rl[:, s % 2, PAST:L],
                              start=(s == 0), stop=(s == DEC_B - 1)).then_inc(summed, 1)

                turn_ki(0)
                for s in range(DEC_B):
                    if s + 1 < DEC_B:
                        turn_ki(s + 1)
                    if s == 0:
                        pe.wait_ge(idx_in, 16 * IH)
                    pe.wait_ge(turned_out, s + 2)
                    if s >= 1:
                        pe.wait_ge(relu_done, s)
                    lhs = qi[:, s, :, :].rearrange("d h t -> d (h t)")
                    pe.matmul(slot[:, 0, 0, 0:PAST], lhs, ckiT[:, s % 2, :], start=True, stop=True)
                    pe.matmul(slot[:, 0, 1, 0:DEC_T], lhs, nkiT[:, s * DEC_T:(s + 1) * DEC_T], start=True, stop=True)\
                        .then_inc(qi_done, 1)
                    if s >= 1:
                        add_scores(s - 1)
                add_scores(DEC_B - 1)

                pe.wait_ge(rows_in, 16)
                pe.wait_ge(bias_done, 1)
                for s in range(DEC_B):
                    if s >= 2:
                        pe.wait_ge(spread_out, s - 1)
                    for j in range(2):
                        mm = pe.matmul(slot[:, s % 2, j, 0:L // 2], rows_of[:, s, :],
                                       score[:, j * L // 2:(j + 1) * L // 2], start=True, stop=True)
                    mm.then_inc(spread, 1)

            @block.scalar
            def _(act):
                act.wait_ge(turned, 1)
                act.activation(nkiT[:, :], psN[0:ID, 0:P], ACT.Copy).then_inc(turned_out, 1)

                def ki_out(s):
                    act.wait_ge(turned, s + 2)
                    if s >= 2:
                        act.wait_ge(qi_done, s - 1)
                    act.activation(ckiT[:, s % 2, :], psT[0:ID, s % 2, :], ACT.Copy).then_inc(turned_out, 1)

                ki_out(0)
                for s in range(DEC_B):
                    if s + 1 < DEC_B:
                        ki_out(s + 1)
                    act.wait_ge(qi_done, s + 1)
                    if s >= 2:
                        act.wait_ge(summed, s - 1)
                    act.activation(rl[:, s % 2, :], slot[:, 0, :, :].rearrange("p j n -> p (j n)")[:, 0:L], ACT.Relu, scale=ID ** -0.5).then_inc(relu_done, 1)
                for s in range(DEC_B):
                    act.wait_ge(spread, s + 1)
                    act.activation(bias[:, s, :].rearrange("p (j n) -> p j n", j=2), both(slot[:, s % 2, :, :]),
                                   ACT.Copy).then_inc(spread_out, 1)

            @block.vector
            def _(dve):
                dve.wait_ge(w_in, 16 * (IH + 1))
                dve.tensor_scalar(w[:, :], w_raw[:, :], IH ** -0.5, None, ALU.mult).then_inc(w_done, 1)
                dve.wait_ge(w_done, 1)
                for s in range(DEC_B):
                    if s >= 2:
                        dve.wait_ge(summed, s - 1)
                    dve.tensor_scalar(sel[:, s % 2, :], frame_of[:, s, :], w[:, s:s + 1], None, ALU.mult)\
                        .then_inc(sel_done, 1)
                dve.wait_ge(summed, DEC_B)
                dve.tensor_copy(score[:, 0:L], slot[:, 1, :, :].rearrange("p j n -> p (j n)")[:, 0:L]).then_inc(score_out, 1)
                dve.wait_ge(score_out, 1)
                dve.wait_ge(pad_done, 1)
                for r in range((TOPK_S + PAD) // 8):
                    if r >= 1:
                        dve.wait_ge(replaced, r)
                    dve.max(top8[:, :], score[:, :]).then_inc(top8_done, 1)
                    dve.wait_ge(top8_done, r + 1)
                    dve.match_replace(score[:, :], top8[:, :], score[:, :], MARK).then_inc(replaced, 1)
                dve.wait_ge(replaced, (TOPK_S + PAD) // 8)
                dve.tensor_scalar(score[:, 0:L], score[:, 0:L], CUT, NEG, ALU.is_gt, ALU.mult).then_inc(bias_done, 1)


def same_frame_table():
    m = np.zeros((2, P, DEC_B, P), np.float32)
    for s in range(DEC_B):
        for x in range(P // DEC_T):
            for f in range(DEC_T):
                m[0, x * DEC_T + f, s, s * DEC_T + f] = 1.0
                m[1, s * DEC_T + f, s, x * DEC_T + f] = 1.0
    return m


def project_and_level_phase(nc, name, sh, chunks, slot0, qT, kT, aT, w_a2, b_a, masks, starts, ends, A_d, qe_d, kdT_d):
    HW = GH * P
    NL = len(LEVELS)
    XR = 3
    with Block(nc, name) as b:
        gm = Gemm(b, sh, chunks, True, slot0)
        mask, start = b.sb("mask", [P, NL + 1, P]), b.sb("start", [P, 2, HW])
        wa, a = b.sb("wa", [RANK + 1, HW]), b.sb("a", [RANK + 1, 2, P])
        q, k = b.sb("q", [P, 2, GH, P]), b.sb("k", [P, 2, GH, P])
        az, ez, lz = b.sb("az", [P, HW]), b.sb("ez", [P, HW]), b.sb("lz", [P, HW])
        la, bcum = b.sb("la", [P, HW]), b.sb("b", [P, 2, HW])
        dist, dec = b.sb("dist", [P, 2, HW]), b.sb("dec", [P, 2, HW])
        X, A = b.sb("X", [P, XR, HW]), b.sb("A", [P, 2, HW])
        e_b, d_end, e_end = b.sb("e_b", [P, HW]), b.sb("d_end", [P, HW]), b.sb("e_end", [P, HW])
        qe, kd, kdT = b.sb("qe", [P, 2, HW]), b.sb("kd", [P, HW]), b.sb("kdT", [P, 2, HW])
        G = b.ps("G", [P, 2, 512])
        zp, tp = b.ps("z", [P, 512]), b.ps("tp", [P, 512])
        const_in, wa_in, ones_done = b.sem("const_in"), b.sem("wa_in"), b.sem("ones_done")
        in_a, in_qk = [b.sem("in_a0"), b.sem("in_a1")], [b.sem("in_qk0"), b.sem("in_qk1")]
        z_done, abs_done, ez_done, lz_done = b.sem("z_done"), b.sem("abs_done"), b.sem("ez_done"), b.sem("lz_done")
        la_done, b_done, eb_done = b.sem("la_done"), b.sem("b_done"), b.sem("eb_done")
        dist_done, dec_done, x_done = b.sem("dist_done"), b.sem("dec_done"), b.sem("x_done")
        g_done, g_out = b.sem("g_done"), b.sem("g_out")
        dend_done, eend_done = b.sem("dend_done"), b.sem("eend_done")
        qe_done, kd_done = b.sem("qe_done"), b.sem("kd_done")
        kd_turned, kdT_done, ends_done = b.sem("kd_turned"), b.sem("kdT_done"), b.sem("ends_done")
        A_stored, qe_stored = [b.sem("A_stored0"), b.sem("A_stored1")], [b.sem("qe_stored0"), b.sem("qe_stored1")]
        kdT_stored = [b.sem("kdT_stored0"), b.sem("kdT_stored1")]

        def levels_of(t):
            return [i for i, w in enumerate(LEVELS) if t < NT_P or 2 * w <= DEC_T]

        level_list = [(t, i) for t in range(NT) for i in levels_of(t)]
        product_list = [(t, i) for t in range(NT) for i in [NL] + levels_of(t)]
        lev_no = {x: n for n, x in enumerate(level_list)}
        g_no = {x: m for m, x in enumerate(product_list)}
        last_lev = {t: lev_no[t, levels_of(t)[-1]] for t in range(NT)}
        last_g = {t: g_no[t, levels_of(t)[-1]] for t in range(NT)}

        units, plan = list(gm.units), []

        def step(*what):
            plan.append(what)

        def unit():
            if units:
                step("unit", units.pop(0))

        def prepare(n, upto):
            if n < len(level_list):
                for what in ("dist", "decay", "operands")[:upto]:
                    step(what, n)

        unit(), step("z", 0), unit(), step("log", 0), step("sums", 0)
        prepare(0, 3), unit(), prepare(1, 3), prepare(2, 2), unit()
        for t in range(NT):
            for x, i in enumerate([NL] + levels_of(t)):
                if x >= 1:
                    prepare(lev_no[t, i] + 3, 2)
                    if lev_no[t, i] + 2 < len(level_list):
                        step("operands", lev_no[t, i] + 2)
                if x == 1:
                    step("from_start", t), step("to_end", t)
                if x == 3:
                    step("decayed", t)
                if x == 4:
                    step("turn", t)
                if t + 1 < NT and x in (2, 3, 4):
                    step({2: "z", 3: "log", 4: "sums"}[x], t + 1)
                step("product", t, i)
                unit()
            step("turned", t), step("store", t)
        while units:
            unit()

        def halves(x, w):
            return x.rearrange("p (n two w) -> p n two w", two=2, w=w)

        with nc.Block() as block:
            @block.sync
            def _(sp):
                def load(t):
                    i, cols = t % 2, slice(t * P, (t + 1) * P)
                    if t >= 2:
                        sp.wait_ge(z_done, t - 1)
                    sp.dma_start(a[0:RANK, i, :], aT[:, cols]).then_inc(in_a[i], 16)
                    if t >= 2:
                        sp.wait_ge(x_done, 2 * (last_lev[t - 2] + 1))
                        sp.wait_ge(kd_done, t - 1)
                        sp.wait_ge(qe_done, t - 1)
                        sp.wait_ge(g_done, g_no[t - 2, NL] + 1)
                    sp.dma_start(q[:, i, :, :], qT[:, cols].rearrange("(h p) n -> p h n", p=P)).then_inc(in_qk[i], 16)
                    sp.dma_start(k[:, i, :, :], kT[:, cols].rearrange("(h p) n -> p h n", p=P)).then_inc(in_qk[i], 16)

                sp.dma_start(wa[0:RANK, :], w_a2).then_inc(wa_in, 16)
                sp.dma_start(wa[RANK:RANK + 1, :], b_a.rearrange("(a n) -> a n", a=1)).then_inc(wa_in, 16)
                sp.wait_ge(ones_done, 1)
                load(0)
                gm.sp_load_w(sp, 1)
                sp.dma_start(start[:, :, :], starts.rearrange("(a r) n -> a r n", a=1).broadcast_to([P, 2, HW])).then_inc(const_in, 16)
                sp.dma_start(mask[:, :, :], masks.rearrange("l s t -> s l t")).then_inc(const_in, 16)
                load(1)
                for kind, x, *_ in plan:
                    if kind == "unit":
                        if x is gm.of[x["c"]][0]:
                            gm.sp_load_w(sp, x["c"] + 2)
                        gm.sp_store(sp, x)
                    elif kind == "store":
                        i, rows = x % 2, slice(x * P, (x + 1) * P)
                        sp.wait_ge(g_out, last_g[x] + 1)
                        sp.dma_start(A_d[rows, :], A[:, i, :]).then_inc(A_stored[i], 16)
                        sp.wait_ge(qe_done, x + 1)
                        sp.dma_start(qe_d[rows, :], qe[:, i, :]).then_inc(qe_stored[i], 16)
                        sp.wait_ge(kdT_done, x + 1)
                        sp.dma_start(kdT_d[rows, :], kdT[:, i, :]).then_inc(kdT_stored[i], 16)
                        if x + 2 < NT:
                            load(x + 2)
                for stored in (A_stored, qe_stored, kdT_stored):
                    sp.wait_ge(stored[0], 16 * ((NT + 1) // 2))
                    sp.wait_ge(stored[1], 16 * (NT // 2))
                gm.sp_end(sp)

            @block.gpsimd
            def _(pool):
                pool.memset(a[:, :, :], 1.0).then_inc(ones_done, 1)
                pool.wait_ge(ones_done, 1)
                gm.pool_w_lo(pool, 1)
                for kind, x, *_ in plan:
                    if kind == "operands":
                        n, (t, i) = x, level_list[x]
                        if i == levels_of(t)[0]:
                            pool.wait_ge(in_qk[t % 2], 32 * (t // 2 + 1))
                        pool.wait_ge(dec_done, n + 1)
                        if n >= XR:
                            pool.wait_ge(g_done, g_no[level_list[n - XR]] + 1)
                        w = LEVELS[i]
                        xs, ds = halves(X[:, n % XR, :], w), halves(dec[:, n % 2, :], w)
                        ks = halves(k[:, t % 2, :, :].rearrange("p h n -> p (h n)"), w)
                        qs = halves(q[:, t % 2, :, :].rearrange("p h n -> p (h n)"), w)
                        pool.tensor_tensor(xs[:, :, 0, :], ks[:, :, 0, :], ds[:, :, 0, :], ALU.mult).then_inc(x_done, 1)
                        pool.tensor_tensor(xs[:, :, 1, :], qs[:, :, 1, :], ds[:, :, 1, :], ALU.mult).then_inc(x_done, 1)
                    elif kind == "decayed":
                        t, i = x, x % 2
                        pool.wait_ge(eb_done, t + 1)
                        if t >= 2:
                            pool.wait_ge(qe_stored[i], 16 * (t // 2))
                        pool.tensor_tensor(qe[:, i, :], q[:, i, :, :].rearrange("p h n -> p (h n)"), e_b[:, :], ALU.mult)\
                            .then_inc(qe_done, 1)
                        pool.wait_ge(eend_done, t + 1)
                        if t >= 1:
                            pool.wait_ge(kd_turned, t)
                        pool.tensor_tensor(kd[:, :], k[:, i, :, :].rearrange("p h n -> p (h n)"), e_end[:, :], ALU.mult)\
                            .then_inc(kd_done, 1)
                    elif kind == "unit" and x is gm.of[x["c"]][-1]:
                        gm.pool_w_lo(pool, x["c"] + 2)

            @block.tensor
            def _(pe):
                for kind, t, *more in plan:
                    if kind == "unit":
                        gm.pe_unit(pe, t)
                    elif kind == "z":
                        if t == 0:
                            pe.wait_ge(wa_in, 32)
                            pe.wait_ge(ones_done, 1)
                        pe.wait_ge(in_a[t % 2], 16 * (t // 2 + 1))
                        if t >= 1:
                            pe.wait_ge(la_done, t)
                        for hd in range(GH):
                            mm = pe.matmul(zp[:, hd * P:(hd + 1) * P], wa[:, hd * P:(hd + 1) * P], a[:, t % 2, :],
                                           start=True, stop=True)
                        mm.then_inc(z_done, 1)
                    elif kind == "product":
                        i, m = more[0], g_no[t, more[0]]
                        if m >= 2:
                            pe.wait_ge(g_out, m - 1)
                        if i == NL:
                            pe.wait_ge(in_qk[t % 2], 32 * (t // 2 + 1))
                        else:
                            pe.wait_ge(x_done, 2 * (lev_no[t, i] + 1))
                        for hd in range(GH):
                            cols = slice(hd * P, (hd + 1) * P)
                            if i == NL:
                                lhs, rhs = k[:, t % 2, hd, :], q[:, t % 2, hd, :]
                            else:
                                lhs = rhs = X[:, lev_no[t, i] % XR, cols]
                            mm = pe.matmul(G[:, m % 2, cols], lhs, rhs, start=True, stop=True)
                        mm.then_inc(g_done, 1)
                    elif kind == "turn":
                        pe.wait_ge(kd_done, t + 1)
                        if t >= 1:
                            pe.wait_ge(kdT_done, t)
                        for hd in range(GH):
                            cols = slice(hd * P, (hd + 1) * P)
                            mm = pe.transpose(tp[:, cols], kd[:, cols], sh.ident[:, :])
                        mm.then_inc(kd_turned, 1)

            @block.scalar
            def _(act):
                gm.act_w_hi(act, 1)
                for kind, t, *_ in plan:
                    if kind == "unit":
                        gm.act_evacuate(act, t)
                        if t is gm.of[t["c"]][-1]:
                            gm.act_w_hi(act, t["c"] + 2)
                    elif kind == "log":
                        act.wait_ge(z_done, t + 1)
                        if t >= 1:
                            act.wait_ge(ez_done, t)
                        act.activation(az[:, :], zp[:, :], ACT.Abs).then_inc(abs_done, 1)
                        act.wait_ge(abs_done, t + 1)
                        if t >= 1:
                            act.wait_ge(lz_done, t)
                        act.activation(ez[:, :], az[:, :], ACT.Exp, scale=-1.0).then_inc(ez_done, 1)
                        act.wait_ge(ez_done, t + 1)
                        if t >= 1:
                            act.wait_ge(la_done, t)
                        act.activation(lz[:, :], ez[:, :], ACT.Ln, bias=1.0).then_inc(lz_done, 1)
                    elif kind == "decay":
                        n = t
                        act.wait_ge(dist_done, 2 * (n + 1))
                        if n >= 2:
                            act.wait_ge(x_done, 2 * (n - 1))
                        act.activation(dec[:, n % 2, :], dist[:, n % 2, :], ACT.Exp, scale=1.0 / TAU).then_inc(dec_done, 1)
                    elif kind == "from_start":
                        act.wait_ge(b_done, t + 1)
                        if t >= 1:
                            act.wait_ge(qe_done, t)
                        act.activation(e_b[:, :], bcum[:, t % 2, :], ACT.Exp, scale=1.0 / TAU).then_inc(eb_done, 1)
                        w = P if t < NT_P else DEC_T
                        act.activation(ends[:, GH * t:GH * t + HW // w], bcum[:, t % 2, w - 1::w], ACT.Exp,
                                       scale=1.0 / TAU).then_inc(ends_done, 1)
                    elif kind == "to_end":
                        act.wait_ge(dend_done, t + 1)
                        if t >= 1:
                            act.wait_ge(kd_done, t)
                        act.activation(e_end[:, :], d_end[:, :], ACT.Exp, scale=1.0 / TAU).then_inc(eend_done, 1)
                    elif kind == "turned":
                        act.wait_ge(kd_turned, t + 1)
                        if t >= 2:
                            act.wait_ge(kdT_stored[t % 2], 16 * (t // 2))
                        act.activation(kdT[:, t % 2, :], tp[:, :], ACT.Copy).then_inc(kdT_done, 1)

            @block.vector
            def _(dve):
                dve.wait_ge(const_in, 16 * 2)
                for kind, t, *more in plan:
                    if kind == "sums":
                        dve.wait_ge(lz_done, t + 1)
                        if t >= 1:
                            dve.wait_ge(b_done, t)
                        dve.scalar_tensor_tensor(la[:, :], zp[:, :], 0.0, lz[:, :], ALU.min, ALU.subtract).then_inc(la_done, 1)
                        dve.wait_ge(la_done, t + 1)
                        if t >= 2:
                            dve.wait_ge(eb_done, t - 1)
                            dve.wait_ge(ends_done, t - 1)
                        dve.tensor_tensor_scan(bcum[:, t % 2, :], start[:, int(t == NT_P), :], la[:, :], 0.0, ALU.mult, ALU.add)\
                            .then_inc(b_done, 1)
                    elif kind == "dist":
                        n, (tt, i) = t, level_list[t]
                        w = LEVELS[i]
                        if i == levels_of(tt)[0]:
                            dve.wait_ge(b_done, tt + 1)
                        if n >= 2:
                            dve.wait_ge(dec_done, n - 1)
                        bs, ds = halves(bcum[:, tt % 2, :], w), halves(dist[:, n % 2, :], w)
                        ref = bs[:, :, 0, w - 1:w].broadcast_to([P, HW // (2 * w), w])
                        dve.tensor_tensor(ds[:, :, 0, :], ref, bs[:, :, 0, :], ALU.subtract).then_inc(dist_done, 1)
                        dve.tensor_tensor(ds[:, :, 1, :], bs[:, :, 1, :], ref, ALU.subtract).then_inc(dist_done, 1)
                    elif kind == "product":
                        i, m = more[0], g_no[t, more[0]]
                        dve.wait_ge(g_done, m + 1)
                        mk = mask[:, i, :].unsqueeze(1).broadcast_to([P, GH, P])
                        g, dst = (z.rearrange("p (h n) -> p h n", h=GH) for z in (G[:, m % 2, :], A[:, t % 2, :]))
                        if i == NL:
                            if t >= 2:
                                dve.wait_ge(A_stored[t % 2], 16 * (t // 2))
                            dve.tensor_tensor(dst, g, mk, ALU.mult).then_inc(g_out, 1)
                        else:
                            dve.wait_ge(g_out, m)
                            dve.copy_predicated(dst, mk.bitcast(U32), g).then_inc(g_out, 1)
                    elif kind == "to_end":
                        if t >= 1:
                            dve.wait_ge(eend_done, t)
                        w = P if t < NT_P else DEC_T
                        bs = bcum[:, t % 2, :].rearrange("p (n w) -> p n w", w=w)
                        ref = bs[:, :, w - 1:w].broadcast_to([P, HW // w, w])
                        dve.tensor_tensor(d_end[:, :].rearrange("p (n w) -> p n w", w=w), ref, bs, ALU.subtract)\
                            .then_inc(dend_done, 1)


def state_phase(nc, name, sh, A_d, qe_d, kdT_d, v, g, ends, b_norm, state, stream_of, prompt_state, sample_state):
    HW = GH * P
    R = 3
    with Block(nc, name) as b:
        rows, bn, mhalf = b.sb("rows", [P, DEC_B]), b.sb("bn", [P, DV]), b.sb("mhalf", [P, GH])
        A, qe, kdT = b.sb("A", [P, R, HW]), b.sb("qe", [P, R, HW]), b.sb("kdT", [P, R, HW])
        vt, gt, gate = b.sb("v", [P, R, D]), b.sb("g", [P, R, D]), b.sb("gate", [P, 2, D])
        S, S_in = b.sb("S", [P, 2, GH, DV]), b.sb("S_in", [P, DEC_B, GH, DV])
        qe_s, kd_s = b.sb("qe_s", [P, DEC_B, GH, P]), b.sb("kd_s", [P, 2, HW])
        junk, ss, ms, rstd = b.sb("junk", [P, DV]), b.sb("ss", [P, 2, GH]), b.sb("ms", [P, 2, GH]), b.sb("rstd", [P, 2, GH])
        og = b.sb("og", [P, 2, D])
        op, dS = b.ps("o", [P, 2, GH, DV]), b.ps("dS", [P, GH, DV])
        const_in, sin_in = b.sem("const_in"), b.sem("sin_in")
        att_in, v_in, g_in = ([b.sem(f"{what}_in{i}") for i in range(R)] for what in ("att", "v", "g"))
        mhalf_done, qs_zero = b.sem("mhalf_done"), b.sem("qs_zero")
        sig_done, silu_done, gate_done = b.sem("sig_done"), b.sem("silu_done"), b.sem("gate_done")
        dS_done, S_done, o_done = b.sem("dS_done"), b.sem("S_done"), b.sem("o_done")
        ss_done, ms_done, rstd_done, og_done = b.sem("ss_done"), b.sem("ms_done"), b.sem("rstd_done"), b.sem("og_done")
        qs_done, kds_done = b.sem("qs_done"), b.sem("kds_done")
        s_stored = b.sem("s_stored")
        nxt = TokenStage(b, sh, tag="next_", src_sb=lambda t: og[:, t % 2, :], ready=lambda e, t: e.wait_ge(og_done, GH * (t + 1)))

        def gain(n):
            return op[:, (NT_P + 1) % 2, :, :] if n > NT_P and (n - NT_P) % 2 else dS[:, :, :]

        with nc.Block() as block:
            @block.sync
            def _(sp):
                def load(t):
                    i, rw = t % R, slice(t * P, (t + 1) * P)
                    if t >= R:
                        sp.wait_ge(dS_done, t - R + 1)
                        sp.wait_ge(o_done, t - R + 1)
                    for dst, src in ((kdT, kdT_d), (A, A_d), (qe, qe_d)):
                        sp.dma_start(dst[:, i, :], src[rw, :]).then_inc(att_in[i], 16)
                    sp.dma_start(vt[:, i, :], v[rw, :]).then_inc(v_in[i], 16)
                    if t >= R:
                        sp.wait_ge(silu_done, t - R + 1)
                    sp.dma_start(gt[:, i, :], g[rw, :]).then_inc(g_in[i], 16)

                load(0)
                sp.dma_start(rows[:, :], stream_of).then_inc(const_in, 16)
                sp.dma_start(bn[:, :], bc(b_norm, DV)).then_inc(const_in, 16)
                for t in range(1, R):
                    load(t)
                for t in range(NT):
                    if t + R < NT:
                        load(t + R)
                        for s in range(DEC_B * t // (NT - R), DEC_B * (t + 1) // (NT - R)):
                            sp.dma_start(S_in[:, s, :, :], state[s].rearrange("h p n -> p h n")).then_inc(sin_in, 16)
                    if t == NT_P - 1:
                        sp.wait_ge(S_done, GH * NT_P)
                        sp.dma_start(prompt_state.rearrange("h p n -> p h n"), S[:, (NT_P - 1) % 2, :, :]).then_inc(s_stored, 16)
                for s in range(DEC_B):
                    sp.wait_ge(S_done, GH * (NT_P + s + 1))
                    sp.dma_start(sample_state[s].rearrange("h p n -> p h n"), S_in[:, s, :, :]).then_inc(s_stored, 16)
                sp.wait_ge(s_stored, 16 * (DEC_B + 1))

            @block.gpsimd
            def _(pool):
                pool.memset(mhalf[:, :], -0.5).then_inc(mhalf_done, 1)
                pool.wait_ge(mhalf_done, 1)

                def gates(t):
                    x = gate[:, t % 2, :]
                    pool.wait_ge(sig_done, t + 1)
                    pool.tensor_tensor(x, x, gt[:, t % R, :], ALU.mult).then_inc(silu_done, 1)
                    if t == 0:
                        pool.wait_ge(const_in, 32)
                    pool.wait_ge(silu_done, t + 1)
                    x = x.rearrange("p (h n) -> p h n", h=GH)
                    pool.tensor_tensor(x, x, bn[:, :].unsqueeze(1).broadcast_to([P, GH, DV]), ALU.mult)\
                        .then_inc(gate_done, 1)

                gates(0)
                for t in range(NT):
                    if t + 1 < NT:
                        gates(t + 1)
                    pool.wait_ge(ss_done, GH * (t + 1))
                    if t >= 2:
                        pool.wait_ge(og_done, GH * (t - 1))
                    pool.tensor_scalar(ms[:, t % 2, :], ss[:, t % 2, :], 1.0 / DV, EPS, ALU.mult, ALU.add).then_inc(ms_done, 1)
                    pool.wait_ge(ms_done, t + 1)
                    pool.tensor_tensor(rstd[:, t % 2, :], ms[:, t % 2, :], mhalf[:, :], ALU.pow).then_inc(rstd_done, 1)
                    if t == 1:
                        pool.memset(qe_s[:, :, :, :], 0.0).then_inc(qs_zero, 1)
                    if t == NT_P - 2:
                        pool.wait_ge(qs_zero, 1)
                        pool.wait_ge(att_in[NT_P % R], 48 * (NT_P // R + 1))
                        for s in range(DEC_B):
                            cols = slice(s * DEC_T, (s + 1) * DEC_T)
                            src = qe[:, NT_P % R, :].rearrange("p (h n) -> p h n", h=GH)
                            pool.tensor_copy(qe_s[:, s, :, cols], src[:, :, cols]).then_inc(qs_done, 1)

            @block.tensor
            def _(pe):
                def gains(n, t, keys):
                    if n == NT_P + 1:
                        pe.wait_ge(og_done, GH * NT_P)
                        pe.wait_ge(ss_done, GH * NT_P)
                    elif n >= 1:
                        pe.wait_ge(S_done, GH * (n if n <= NT_P else n - 1))
                    for hd in range(GH):
                        mm = pe.matmul(gain(n)[:, hd, :], keys[:, hd * P:(hd + 1) * P],
                                       vt[:, t % R, hd * DV:(hd + 1) * DV], start=True, stop=True)
                    mm.then_inc(dS_done, 1)

                for t in range(NT):
                    pe.wait_ge(att_in[t % R], 48 * (t // R + 1))
                    pe.wait_ge(v_in[t % R], 16 * (t // R + 1))
                    if t < NT_P:
                        gains(t, t, kdT[:, t % R, :])
                    else:
                        pe.wait_ge(qs_done, DEC_B)
                        pe.wait_ge(sin_in, 16 * DEC_B)
                    if t >= 2:
                        pe.wait_ge(og_done, GH * (t - 1))
                        pe.wait_ge(ss_done, GH * (t - 1))
                    for hd in range(GH):
                        cols, vs = slice(hd * P, (hd + 1) * P), vt[:, t % R, hd * DV:(hd + 1) * DV]
                        mm = pe.matmul(op[:, t % 2, hd, :], A[:, t % R, cols], vs, start=True, stop=(t == 0))
                        if 1 <= t < NT_P:
                            if hd == 0:
                                pe.wait_ge(S_done, GH * t)
                            mm = pe.matmul(op[:, t % 2, hd, :], qe[:, t % R, cols], S[:, (t - 1) % 2, hd, :],
                                           start=False, stop=True)
                        if t == NT_P:
                            for s in range(DEC_B):
                                mm = pe.matmul(op[:, t % 2, hd, :], qe_s[:, s, hd, :], S_in[:, s, hd, :],
                                               start=False, stop=(s == DEC_B - 1))
                    mm.then_inc(o_done, 1)
                    if t >= 1:
                        nxt.pe_transpose(pe, t - 1)
                for s in range(DEC_B):
                    pe.wait_ge(kds_done, s + 1)
                    gains(NT_P + s, NT_P, kd_s[:, s % 2, :])
                    if s == 1:
                        nxt.pe_transpose(pe, NT - 1)

            @block.scalar
            def _(act):
                def sigmoid(t):
                    act.wait_ge(g_in[t % R], 16 * (t // R + 1))
                    if t >= 2:
                        act.wait_ge(og_done, GH * (t - 1))
                    act.activation(gate[:, t % 2, :], gt[:, t % R, :], ACT.Sigmoid).then_inc(sig_done, 1)

                sigmoid(0)
                for t in range(NT):
                    if t + 1 < NT:
                        sigmoid(t + 1)
                    act.wait_ge(o_done, t + 1)
                    if t >= 2:
                        act.wait_ge(ms_done, t - 1)
                    for hd in range(GH):
                        n = GH * t + hd
                        if n >= 1:
                            act.wait_ge(ss_done, n)
                        act.activation(junk[:, :], op[:, t % 2, hd, :], ACT.Square, accum_out=ss[:, t % 2, hd:hd + 1])\
                            .then_inc(ss_done, 1)
                    if t >= 1:
                        nxt.act_hi(act, t - 1)
                nxt.act_hi(act, NT - 1)

            @block.vector
            def _(dve):
                def states(t):
                    dve.wait_ge(dS_done, t + 1)
                    if t >= 2:
                        dve.wait_ge(o_done, t)
                    for hd in range(GH):
                        if t == 0:
                            dve.tensor_copy(S[:, 0, hd, :], dS[:, hd, :]).then_inc(S_done, 1)
                        else:
                            if hd == 0:
                                dve.wait_ge(S_done, GH * t)
                            dve.scalar_tensor_tensor(S[:, t % 2, hd, :], S[:, (t - 1) % 2, hd, :],
                                                     ends[:, GH * t + hd:GH * t + hd + 1], dS[:, hd, :],
                                                     ALU.mult, ALU.add).then_inc(S_done, 1)

                def post(t):
                    dve.wait_ge(rstd_done, t + 1)
                    dve.wait_ge(gate_done, t + 1)
                    if t >= 2:
                        dve.wait_ge(nxt.t_done, 2 * (t - 1))
                    for hd in range(GH):
                        cols = slice(hd * DV, (hd + 1) * DV)
                        dve.scalar_tensor_tensor(og[:, t % 2, cols], op[:, t % 2, hd, :], rstd[:, t % 2, hd:hd + 1],
                                                 gate[:, t % 2, cols], ALU.mult, ALU.mult).then_inc(og_done, 1)

                def keys_of(s):
                    if s >= 2:
                        dve.wait_ge(dS_done, NT_P + s - 1)
                    dve.tensor_scalar(kd_s[:, s % 2, :], kdT[:, NT_P % R, :], rows[:, s:s + 1], None, ALU.mult)\
                        .then_inc(kds_done, 1)

                for t in range(NT_P):
                    states(t)
                    if t >= 1:
                        post(t - 1)
                    if t >= 2:
                        nxt.dve_lo(dve, t - 2)
                post(NT_P - 1)
                nxt.dve_lo(dve, NT_P - 2)
                dve.wait_ge(const_in, 32)
                dve.wait_ge(att_in[NT_P % R], 48 * (NT_P // R + 1))
                keys_of(0)
                keys_of(1)
                post(NT_P)
                nxt.dve_lo(dve, NT_P - 1)
                for s in range(DEC_B):
                    dve.wait_ge(dS_done, NT_P + s + 1)
                    dve.wait_ge(o_done, NT)
                    got = gain(NT_P + s)
                    for hd in range(GH):
                        c = GH * NT_P + hd * DEC_B + s
                        dve.scalar_tensor_tensor(S_in[:, s, hd, :], S_in[:, s, hd, :], ends[:, c:c + 1],
                                                 got[:, hd, :], ALU.mult, ALU.add).then_inc(S_done, 1)
                    if s + 2 < DEC_B:
                        keys_of(s + 2)
                    if s == 3:
                        nxt.dve_lo(dve, NT - 1)


def level_masks():
    s, t = np.arange(P)[:, None], np.arange(P)[None, :]
    ms = [(s // (2 * w) == t // (2 * w)) & (s % (2 * w) < w) & (t % (2 * w) >= w) for w in LEVELS]
    return np.stack(ms + [s == t]).astype(np.float32)


def scan_starts():
    c = np.arange(GH * P)
    return np.stack([c % P != 0, c % DEC_T != 0]).astype(np.float32)


def stream_rows():
    return (np.arange(P)[:, None] // DEC_T == np.arange(DEC_B)[None, :]).astype(np.float32)


def encoder(nc, x_prompt, x_sample, cache_k, cache_v, cache_kidx, state_gla, norm_mix, norm_ffn, norm_final,
            a_w_in, a_w_o, b_w_in, b_w_a2, b_b_a, b_norm, b_w_o, ffn_w_up, ffn_w_down,
            ident_table, same_frame, masks, starts, stream_of,
            y_prompt, y_sample, k_prompt, v_prompt, kidx_prompt, gla_prompt,
            k_sample, v_sample, kidx_sample, gla_sample):
    xp, xs = x_prompt[0], x_sample.rearrange("b t d -> (b t) d")
    yp, ys = y_prompt[0], y_sample.rearrange("b t d -> (b t) d")

    def flat(ap, pattern):
        return ap.rearrange(pattern)

    k_p, v_p = (flat(z[0, 0], "s h d -> s (h d)") for z in (k_prompt, v_prompt))
    k_s, v_s = (flat(z[0], "b t h d -> (b t) (h d)") for z in (k_sample, v_sample))
    ki_p, ki_s = kidx_prompt[0, 0], flat(kidx_sample[0], "b t d -> (b t) d")
    c_k, c_v = (flat(z[0], "b s h d -> b s (h d)") for z in (cache_k, cache_v))
    def dram(name, rows, cols):
        return nc.dram_tensor(name, (rows, cols), F32, kind="Internal").ap()

    qT, qiT, wt, o = dram("qT", D, TOK), dram("qiT", IH * ID, TOK), dram("wt", TOK, IH), dram("o", TOK, D)
    gq, gk, ga = dram("gq", GH * DK, TOK), dram("gk", GH * DK, TOK), dram("ga", RANK, TOK)
    gv, gg, hd = dram("gv", TOK, D), dram("gg", TOK, D), dram("hd", TOK, D)
    A_d, qe_d, kdT_d = dram("A", TOK, GH * P), dram("qe", TOK, GH * P), dram("kdT", TOK, GH * P)

    def either(p, s):
        return lambda t: p[t * P:(t + 1) * P, :] if t < NT_P else s[:, :]

    def to_T(dst, r0, cols=CW):
        return lambda u: [(dst[r0 + u["j"]:r0 + u["j"] + u["m"], u["g"] * GW:(u["g"] + 1) * GW],
                           lambda s, m=u["m"]: s[0:m, :])]

    def to_N(tile, c0=0, n=CW, s0=0):
        return lambda u: [(tile(u["t"])[:, c0:c0 + n], lambda s: s[:, s0:s0 + n])]

    def both(f, g):
        return lambda u: f(u) + g(u)

    def chunk(w, c0, n, form, op, out):
        return dict(w=w[:, c0:c0 + n], form=form, op=op, out=out)

    with ExitStack() as ctx:
        ident = ctx.enter_context(nc.sbuf_tensor("ident", [P, P], F32))
        ident_in = ctx.enter_context(nc.semaphore("ident_in"))
        with nc.Block() as block:
            @block.sync
            def _(sp):
                sp.dma_start(ident[:, :], ident_table).then_inc(ident_in, 16)
                sp.wait_ge(ident_in, 16)

        tile_of = lambda d: (lambda t: d[t * P:(t + 1) * P, :])

        QW, KW, IW = HEADS * HD, KVH * HD, IH * ID
        w0 = a_w_in[0]
        tail = A_IN - CW
        first = [chunk(w0, tail, CW, "N", "copy",
                       both(to_N(either(ki_p, ki_s), 0, ID, CW - IH - ID), to_N(tile_of(wt), 0, IH, CW - IH)))]
        first += [chunk(w0, QW + 2 * KW + c, CW, "T", "copy", to_T(qiT, c)) for c in range(0, IW, CW)]
        rest = [chunk(w0, QW, CW, "N", "copy", to_N(either(k_p, k_s))),
                chunk(w0, QW + KW, CW, "N", "copy", to_N(either(v_p, v_s)))]
        rest += [chunk(w0, c, CW, "T", HD ** -0.5, to_T(qT, c)) for c in range(0, QW, CW)]
        with ExitStack() as scope:
            score = scope.enter_context(nc.sbuf_tensor("score", [P, SCORE_AT[NT_P]], F32))
            s_bias = scope.enter_context(nc.sbuf_tensor("s_bias", [P, DEC_B, PAST + DEC_T], F32))
            with ExitStack() as inner:
                sh = Shared(nc, inner, "proj0", ident)
                gemm_phase(nc, "proj0a", sh, first, src_dram=either(xp, xs), gamma=norm_mix[0], next_w=rest[0]["w"])
                sample_choice_phase(nc, "schoice", ident, qiT, wt, cache_kidx[0], ki_s, same_frame, s_bias)
                begun = project_and_score_phase(nc, "proj0b", sh, rest, True, len(first) % 2, qiT, wt, ki_p, score)
            attention_phase(nc, "att", ident, qT, k_p, v_p, score, c_k, c_v, k_s, v_s, s_bias, o, begun)

        w1 = b_w_in[0]
        HK = GH * DK
        first = [chunk(w1, c, CW, "T", DK ** -0.5, to_T(gq, c)) for c in range(0, HK, CW)]
        first += [chunk(w1, HK + c, CW, "T", "copy", to_T(gk, c)) for c in range(0, HK, CW)]
        first += [chunk(w1, 2 * HK + 2 * D, RANK, "T", "copy", to_T(ga, 0))]
        rest = [chunk(w1, 2 * HK + c, CW, "N", "copy", to_N(tile_of(gv), c)) for c in range(0, D, CW)]
        rest += [chunk(w1, 2 * HK + D + c, CW, "N", "copy", to_N(tile_of(gg), c)) for c in range(0, D, CW)]
        ends = ctx.enter_context(nc.sbuf_tensor("ends", [P, GH * (NT_P + DEC_B)], F32))
        with ExitStack() as scope:
            sh = Shared(nc, scope, "mid", ident)
            with ExitStack() as inner:
                h = inner.enter_context(nc.sbuf_tensor("h0", [P, NT, D], F32))
                gemm_phase(nc, "out0", sh, [chunk(a_w_o[0], c, CW, "N", "resid", None) for c in range(0, D, CW)],
                           src_dram=tile_of(o), residual=either(xp, xs), h=h, next_w=ffn_w_up[0][:, 0:CW],
                           next_gamma=norm_ffn[0])
                mlp_phase(nc, "mlp0", sh, h, ffn_w_up[0], ffn_w_down[0], norm_mix[1], next_w=first[0]["w"])
                gemm_phase(nc, "proj1a", sh, first, preset=True, next_w=rest[0]["w"],
                           spill=[(tile_of(hd)(t), h[:, t, :]) for t in range(NT)])
            project_and_level_phase(nc, "proj1b", sh, rest, len(first) % 2, gq, gk, ga, b_w_a2[0], b_b_a[0],
                                    masks, starts, ends, A_d, qe_d, kdT_d)
        sh = Shared(nc, ctx, "end", ident, weights=False)
        state_phase(nc, "state", sh, A_d, qe_d, kdT_d, gv, gg, ends, b_norm[0], state_gla[0], stream_of,
                    gla_prompt[0, 0], gla_sample[0])
        sh.add_weights()
        h = ctx.enter_context(nc.sbuf_tensor("h1", [P, NT, D], F32))
        gemm_phase(nc, "out1", sh, [chunk(b_w_o[0], c, CW, "N", "resid", None) for c in range(0, D, CW)],
                   residual=tile_of(hd), h=h, next_w=ffn_w_up[1][:, 0:CW], next_gamma=norm_ffn[1])
        mlp_phase(nc, "mlp1", sh, h, ffn_w_up[1], ffn_w_down[1], norm_final, y=either(yp, ys))


INPUTS = ["x_prompt", "x_sample", "cache_k", "cache_v", "cache_kidx", "state_gla", "norm_mix", "norm_ffn",
          "norm_final", "a_w_in", "a_w_o", "b_w_in", "b_w_a2", "b_b_a", "b_norm", "b_w_o", "ffn_w_up", "ffn_w_down"]
OUTPUTS = [(1, SEQ, D), (DEC_B, DEC_T, D), (1, 1, SEQ, KVH, HD), (1, 1, SEQ, KVH, HD), (1, 1, SEQ, ID),
           (1, 1, GH, DK, DV), (1, DEC_B, DEC_T, KVH, HD), (1, DEC_B, DEC_T, KVH, HD), (1, DEC_B, DEC_T, ID),
           (1, DEC_B, GH, DK, DV)]


def kernel(**inputs):
    import concourse.bacc as bacc
    from concourse.bass_utils import run_bass_kernel_spmd

    nc = bacc.Bacc("TRN2", target_bir_lowering=False, num_devices=1)
    arrays = {name: np.ascontiguousarray(inputs[name]) for name in INPUTS}
    arrays |= {"ident": np.eye(P, dtype=np.float32), "same_frame": same_frame_table(), "level_masks": level_masks(),
               "scan_starts": scan_starts(), "stream_rows": stream_rows()}
    feed = {f"in_{name}": a for name, a in arrays.items()}
    args = [nc.dram_tensor(name, a.shape, mybir.dt.from_np(a.dtype), kind="ExternalInput").ap()
            for name, a in feed.items()]
    args += [nc.dram_tensor(f"out_{i}", shape, F32, kind="ExternalOutput").ap() for i, shape in enumerate(OUTPUTS)]
    encoder(nc, *args)
    r = run_bass_kernel_spmd(nc, [feed], core_ids=[0])
    return tuple(r.results[0][f"out_{i}"] for i in range(len(OUTPUTS)))
```
